# Optimizing a Trainium2 kernel written in Bass

```python
import math
import jax, jax.numpy as jnp
from jax import lax
import numpy as np

D_MODEL = 1024
BATCH = 1
SEQ = 256
DEPTH = 2

N_EVEN = (DEPTH + 1) // 2
N_ODD = DEPTH // 2
RMS_EPS = 1e-6
DA_HEADS = 4
DA_HEAD_DIM = 64
DA_V_DIM = 2 * DA_HEAD_DIM
DA_QK_WIDTH = 2 * DA_HEADS * DA_HEAD_DIM
DA_V_WIDTH = DA_HEADS * DA_V_DIM
Q_BLOCK = 128
ROPE_THETA = 500000.0
ROT_DIM = DA_HEAD_DIM // 4
SUBLN_EPS = 1e-5
SC_WIDTH = 512
SC_GROUPS = 8
SC_KERNEL = 3
EVEN_IN_WIDTH = 2 * DA_QK_WIDTH + DA_V_WIDTH + 3 * SC_WIDTH
EVEN_MIX_WIDTH = DA_V_WIDTH + SC_WIDTH
DN_HEADS = 8
DN_HEAD_DIM = 128
DN_WIDTH = DN_HEADS * DN_HEAD_DIM
DN_CONV = 4
DN_CHUNK = 64
ODD_IN_WIDTH = 4 * DN_WIDTH + 2 * DN_HEADS
D_FF = 3584
N_EXPERTS = 8
TOP_K = 2
EXPERT_D_FF = 3584
MOE_BLOCK = 256
PLE_DIM = 256

kernel_name = "hybrid_diffattn_shortconv_gdn_moe_trunk"

def rmsnorm(x, g, eps=RMS_EPS):
    xf = x.astype(jnp.float32)
    y = xf * lax.rsqrt(jnp.mean(xf * xf, axis=-1, keepdims=True) + eps)
    return (y * g.astype(jnp.float32)).astype(x.dtype)

def split_cols(t, widths):
    idx = np.cumsum(widths)[:-1].tolist()
    return jnp.split(t, idx, axis=-1)

def causal_dwconv(u, w):
    K = w.shape[0]
    S = u.shape[1]
    up = jnp.pad(u, ((0, 0), (K - 1, 0), (0, 0)))
    out = up[:, 0:S] * w[0]
    for j in range(1, K):
        out = out + up[:, j:j + S] * w[j]
    return out

def partial_rotary(x, positions):
    inv_freq = ROPE_THETA ** (-jnp.arange(0, ROT_DIM, 2, dtype=jnp.float32) / ROT_DIM)
    ang = positions.astype(jnp.float32)[..., None] * inv_freq
    cos = jnp.cos(ang)[:, :, None, :]
    sin = jnp.sin(ang)[:, :, None, :]
    xr = x[..., :ROT_DIM].astype(jnp.float32)
    x1, x2 = xr[..., :ROT_DIM // 2], xr[..., ROT_DIM // 2:]
    rot = jnp.concatenate([x1 * cos - x2 * sin, x2 * cos + x1 * sin], axis=-1).astype(x.dtype)
    return jnp.concatenate([rot, x[..., ROT_DIM:]], axis=-1)

def lambda_init(layer_idx):
    return 0.8 - 0.6 * math.exp(-0.3 * layer_idx)

def diff_attention(q, k, v, lam, positions):
    Bsz, H2, S, dh = q.shape
    H = H2 // 2
    nqb = S // Q_BLOCK
    qf = (q.astype(jnp.float32) * (dh ** -0.5)).reshape(Bsz, H2, nqb, Q_BLOCK, dh).transpose(2, 0, 1, 3, 4)
    qpos = positions.reshape(Bsz, nqb, Q_BLOCK).transpose(1, 0, 2)
    kf = k.astype(jnp.float32)
    vf = v.astype(jnp.float32)

    def block(args):
        qb, pq = args
        s = jnp.einsum('bhqd,bhkd->bhqk', qb, kf)
        mask = positions[:, None, None, :] <= pq[:, None, :, None]
        s = jnp.where(mask, s, -jnp.inf)
        pm = jax.nn.softmax(s, axis=-1).reshape(Bsz, H, 2, Q_BLOCK, S)
        a = pm[:, :, 0] - lam * pm[:, :, 1]
        return jnp.einsum('bhqk,bhkv->bhqv', a, vf)

    out = lax.map(block, (qf, qpos))
    return out.transpose(1, 2, 0, 3, 4).reshape(Bsz, H, S, 2 * dh)

def even_mixer(hn, positions, w_in, w_out, lam_q1, lam_k1, lam_q2, lam_k2, subln_g, conv_w, layer_idx):
    Bsz, S, _ = hn.shape
    proj = hn @ w_in
    q, k, v, b_gate, c_gate, xb = split_cols(
        proj, [DA_QK_WIDTH, DA_QK_WIDTH, DA_V_WIDTH, SC_WIDTH, SC_WIDTH, SC_WIDTH])
    q = partial_rotary(q.reshape(Bsz, S, 2 * DA_HEADS, DA_HEAD_DIM), positions)
    k = partial_rotary(k.reshape(Bsz, S, 2 * DA_HEADS, DA_HEAD_DIM), positions)
    v = v.reshape(Bsz, S, DA_HEADS, DA_V_DIM)
    lam_0 = lambda_init(layer_idx)
    f32 = jnp.float32
    lam = (jnp.exp(jnp.sum(lam_q1.astype(f32) * lam_k1.astype(f32)))
           - jnp.exp(jnp.sum(lam_q2.astype(f32) * lam_k2.astype(f32))) + lam_0)
    o = diff_attention(q.transpose(0, 2, 1, 3), k.transpose(0, 2, 1, 3), v.transpose(0, 2, 1, 3), lam, positions)
    o = rmsnorm(o, subln_g, SUBLN_EPS) * (1.0 - lam_0)
    o = o.transpose(0, 2, 1, 3).reshape(Bsz, S, DA_V_WIDTH).astype(hn.dtype)
    sc = b_gate * causal_dwconv(c_gate * xb, conv_w)
    return jnp.concatenate([o, sc], axis=-1) @ w_out

def l2norm(x, eps=1e-6):
    return x * lax.rsqrt(jnp.sum(x * x, axis=-1, keepdims=True) + eps)

def chunk_gated_delta_rule(q, k, v, g, beta):
    Bsz, S, H, dk = q.shape
    dv = v.shape[-1]
    C = DN_CHUNK
    N = S // C

    def chunks(t):
        t = jnp.moveaxis(t, 2, 1)
        return t.reshape(t.shape[:2] + (N, C) + t.shape[3:])

    q = chunks(q * (dk ** -0.5))
    k = chunks(k)
    v = chunks(v)
    g = jnp.cumsum(chunks(g), axis=-1)
    beta = chunks(beta)
    k_beta = k * beta[..., None]
    v_beta = v * beta[..., None]
    incl = jnp.tril(jnp.ones((C, C), dtype=bool))
    strict = jnp.tril(jnp.ones((C, C), dtype=bool), -1)
    gdiff = g[..., :, None] - g[..., None, :]
    decay = jnp.where(incl, jnp.exp(jnp.where(incl, gdiff, 0.0)), 0.0)
    L = jnp.where(strict, jnp.einsum('bhnid,bhnjd->bhnij', k_beta, k) * decay, 0.0)
    T = L + jnp.eye(C, dtype=jnp.float32)
    u = lax.linalg.triangular_solve(T, v_beta, left_side=True, lower=True, unit_diagonal=True)
    w = lax.linalg.triangular_solve(T, k_beta * jnp.exp(g)[..., None], left_side=True, lower=True,
                                    unit_diagonal=True)
    a_intra = jnp.einsum('bhnid,bhnjd->bhnij', q, k) * decay

    def step(state, xs):
        qi, ki, ui, wi, gi, ai = xs
        v_new = ui - jnp.einsum('bhcd,bhdv->bhcv', wi, state)
        o = (jnp.einsum('bhcd,bhdv->bhcv', qi * jnp.exp(gi)[..., None], state)
             + jnp.einsum('bhij,bhjv->bhiv', ai, v_new))
        g_last = gi[..., -1:]
        state = (state * jnp.exp(g_last)[..., None]
                 + jnp.einsum('bhcd,bhcv->bhdv', ki * jnp.exp(g_last - gi)[..., None], v_new))
        return state, o

    xs = tuple(jnp.moveaxis(t, 2, 0) for t in (q, k, u, w, g, a_intra))
    state0 = jnp.zeros((Bsz, H, dk, dv), jnp.float32)
    _, o = lax.scan(step, state0, xs)
    o = jnp.moveaxis(o, 0, 2).reshape(Bsz, H, S, dv)
    return jnp.moveaxis(o, 1, 2)

def odd_mixer(hn, w_in, conv_w, a_log, dt_bias, onorm_g, w_out):
    Bsz, S, _ = hn.shape
    f32 = jnp.float32
    proj = hn @ w_in
    qkv, z, b, a = split_cols(proj, [3 * DN_WIDTH, DN_WIDTH, DN_HEADS, DN_HEADS])
    qkv = jax.nn.silu(causal_dwconv(qkv, conv_w))
    q, k, v = jnp.split(qkv.astype(f32), 3, axis=-1)
    q = l2norm(q.reshape(Bsz, S, DN_HEADS, DN_HEAD_DIM))
    k = l2norm(k.reshape(Bsz, S, DN_HEADS, DN_HEAD_DIM))
    v = v.reshape(Bsz, S, DN_HEADS, DN_HEAD_DIM)
    beta = jax.nn.sigmoid(b.astype(f32))
    g = -jnp.exp(a_log.astype(f32)) * jax.nn.softplus(a.astype(f32) + dt_bias.astype(f32))
    o = chunk_gated_delta_rule(q, k, v, g, beta)
    o = rmsnorm(o, onorm_g) * jax.nn.silu(z.astype(f32).reshape(Bsz, S, DN_HEADS, DN_HEAD_DIM))
    return o.reshape(Bsz, S, DN_WIDTH).astype(hn.dtype) @ w_out

def swiglu(xn, w1, w3, w2):
    return (jax.nn.silu(xn @ w1) * (xn @ w3)) @ w2

def moe_swiglu(xn, w_router, w1, w3, w2):
    Bsz, S, D = xn.shape
    T = Bsz * S
    xt = xn.reshape(T, D)
    logits = (xt @ w_router).astype(jnp.float32)
    top_logit, top_idx = lax.top_k(logits, TOP_K)
    gates = jax.nn.softmax(top_logit, axis=-1).astype(xn.dtype)
    n_assign = T * TOP_K
    e_flat = top_idx.reshape(-1).astype(jnp.int32)
    tok_flat = jnp.repeat(jnp.arange(T, dtype=jnp.int32), TOP_K)
    g_flat = gates.reshape(-1)
    order = jnp.argsort(e_flat)
    e_sorted = e_flat[order]
    counts = jnp.zeros((N_EXPERTS,), jnp.int32).at[e_flat].add(1)
    starts = jnp.cumsum(counts) - counts
    padded = ((counts + MOE_BLOCK - 1) // MOE_BLOCK) * MOE_BLOCK
    pends = jnp.cumsum(padded)
    pstarts = pends - padded
    dest = pstarts[e_sorted] + (jnp.arange(n_assign, dtype=jnp.int32) - starts[e_sorted])
    P = ((n_assign + MOE_BLOCK - 1) // MOE_BLOCK) * MOE_BLOCK + N_EXPERTS * MOE_BLOCK
    NB = P // MOE_BLOCK
    buf_tok = jnp.full((P,), T, jnp.int32).at[dest].set(tok_flat[order])
    buf_gate = jnp.zeros((P,), xn.dtype).at[dest].set(g_flat[order])
    blk_e = jnp.minimum(
        jnp.searchsorted(pends, jnp.arange(NB, dtype=jnp.int32) * MOE_BLOCK, side='right'), N_EXPERTS - 1)
    x_pad = jnp.concatenate([xt, jnp.zeros((1, D), xt.dtype)], axis=0)

    def run_block(args):
        tok, gate, e = args
        xb = x_pad[tok]
        hb = jax.nn.silu(xb @ w1[e]) * (xb @ w3[e])
        return (hb @ w2[e]) * gate[:, None]

    y = lax.map(run_block, (buf_tok.reshape(NB, MOE_BLOCK), buf_gate.reshape(NB, MOE_BLOCK), blk_e))
    out = jnp.zeros((T + 1, D), xn.dtype).at[buf_tok].add(y.reshape(P, D))
    return out[:T].reshape(Bsz, S, D)

def setup_inputs(seed: int = 0) -> dict:
    key = jax.random.key(seed)
    ks = jax.random.split(key, 32)
    f32 = jnp.float32

    def nrm(k, shape, fan_in):
        return jax.random.normal(k, shape, f32) * (fan_in ** -0.5)

    def gain(k, shape):
        return 1.0 + 0.05 * jax.random.normal(k, shape, f32)

    x = jax.random.normal(ks[0], (BATCH, SEQ, D_MODEL), f32)
    p = jax.random.normal(ks[1], (DEPTH, BATCH, SEQ, PLE_DIM), f32)
    positions = jnp.tile(jnp.arange(SEQ, dtype=jnp.int32)[None, :], (BATCH, 1))
    ln_mix = gain(ks[2], (DEPTH, D_MODEL))
    ln_ffn = gain(ks[3], (DEPTH, D_MODEL))
    ln_ple = gain(ks[4], (DEPTH, D_MODEL))
    ln_final = gain(ks[5], (D_MODEL,))
    w_in_even = nrm(ks[6], (N_EVEN, D_MODEL, EVEN_IN_WIDTH), D_MODEL)
    w_out_even = nrm(ks[7], (N_EVEN, EVEN_MIX_WIDTH, D_MODEL), EVEN_MIX_WIDTH)
    lam_q1 = 0.1 * jax.random.normal(ks[8], (N_EVEN, DA_HEAD_DIM), f32)
    lam_k1 = 0.1 * jax.random.normal(ks[9], (N_EVEN, DA_HEAD_DIM), f32)
    lam_q2 = 0.1 * jax.random.normal(ks[10], (N_EVEN, DA_HEAD_DIM), f32)
    lam_k2 = 0.1 * jax.random.normal(ks[11], (N_EVEN, DA_HEAD_DIM), f32)
    subln_gain = gain(ks[12], (N_EVEN, DA_V_DIM))
    conv_w_short = nrm(ks[13], (N_EVEN, SC_KERNEL, SC_WIDTH), SC_KERNEL)
    w_in_odd = nrm(ks[14], (N_ODD, D_MODEL, ODD_IN_WIDTH), D_MODEL)
    conv_w_qkv = nrm(ks[15], (N_ODD, DN_CONV, 3 * DN_WIDTH), DN_CONV)
    a_log = jnp.log(jax.random.uniform(ks[16], (N_ODD, DN_HEADS), f32, 1.0, 16.0))
    dt = jnp.exp(jax.random.uniform(ks[17], (N_ODD, DN_HEADS), f32, math.log(1e-3), math.log(1e-1)))
    dt_bias = dt + jnp.log(-jnp.expm1(-dt))
    onorm_gain = gain(ks[18], (N_ODD, DN_HEAD_DIM))
    w_out_odd = nrm(ks[19], (N_ODD, DN_WIDTH, D_MODEL), DN_WIDTH)
    w1_dense = nrm(ks[20], (N_EVEN, D_MODEL, D_FF), D_MODEL)
    w3_dense = nrm(ks[21], (N_EVEN, D_MODEL, D_FF), D_MODEL)
    w2_dense = nrm(ks[22], (N_EVEN, D_FF, D_MODEL), D_FF)
    w_router = nrm(ks[23], (N_ODD, D_MODEL, N_EXPERTS), D_MODEL)
    w1_moe = nrm(ks[24], (N_ODD, N_EXPERTS, D_MODEL, EXPERT_D_FF), D_MODEL)
    w3_moe = nrm(ks[25], (N_ODD, N_EXPERTS, D_MODEL, EXPERT_D_FF), D_MODEL)
    w2_moe = nrm(ks[26], (N_ODD, N_EXPERTS, EXPERT_D_FF, D_MODEL), EXPERT_D_FF)
    w_ple_gate = nrm(ks[27], (DEPTH, D_MODEL, D_MODEL), D_MODEL)
    w_ple_proj = nrm(ks[28], (DEPTH, PLE_DIM, D_MODEL), PLE_DIM)
    return {"x": x, "p": p, "positions": positions, "ln_mix": ln_mix, "ln_ffn": ln_ffn,
            "ln_ple": ln_ple, "ln_final": ln_final, "w_in_even": w_in_even, "w_out_even": w_out_even,
            "lam_q1": lam_q1, "lam_k1": lam_k1, "lam_q2": lam_q2, "lam_k2": lam_k2,
            "subln_gain": subln_gain, "conv_w_short": conv_w_short, "w_in_odd": w_in_odd,
            "conv_w_qkv": conv_w_qkv, "a_log": a_log, "dt_bias": dt_bias, "onorm_gain": onorm_gain,
            "w_out_odd": w_out_odd, "w1_dense": w1_dense, "w3_dense": w3_dense, "w2_dense": w2_dense,
            "w_router": w_router, "w1_moe": w1_moe, "w3_moe": w3_moe, "w2_moe": w2_moe,
            "w_ple_gate": w_ple_gate, "w_ple_proj": w_ple_proj}

def reference(x, p, positions, ln_mix, ln_ffn, ln_ple, ln_final, w_in_even, w_out_even,
              lam_q1, lam_k1, lam_q2, lam_k2, subln_gain, conv_w_short, w_in_odd, conv_w_qkv,
              a_log, dt_bias, onorm_gain, w_out_odd, w1_dense, w3_dense, w2_dense,
              w_router, w1_moe, w3_moe, w2_moe, w_ple_gate, w_ple_proj):
    h = x
    for i in range(DEPTH):
        j = i // 2
        hn = rmsnorm(h, ln_mix[i])
        if i % 2 == 0:
            h = h + even_mixer(hn, positions, w_in_even[j], w_out_even[j], lam_q1[j], lam_k1[j],
                               lam_q2[j], lam_k2[j], subln_gain[j], conv_w_short[j], i)
            hn = rmsnorm(h, ln_ffn[i])
            h = h + swiglu(hn, w1_dense[j], w3_dense[j], w2_dense[j])
        else:
            h = h + odd_mixer(hn, w_in_odd[j], conv_w_qkv[j], a_log[j], dt_bias[j], onorm_gain[j],
                              w_out_odd[j])
            hn = rmsnorm(h, ln_ffn[i])
            h = h + moe_swiglu(hn, w_router[j], w1_moe[j], w3_moe[j], w2_moe[j])
        gate = jax.nn.sigmoid(rmsnorm(h, ln_ple[i]) @ w_ple_gate[i])
        h = h + gate * (p[i] @ w_ple_proj[i])
    return rmsnorm(h, ln_final)


_drawn_inputs = setup_inputs


def setup_inputs(seed=0):
    import zlib

    import numpy as np

    out = dict(_drawn_inputs(seed))
    spreads = {}
    factors = {'ln_ple': 3.069, 'lam_k1': 5.814, 'lam_q2': 5.902}
    for name, (base, spread) in spreads.items():
        noise = np.random.default_rng([zlib.crc32(name.encode()), seed]).standard_normal(out[name].shape)
        drawn = base * np.exp(spread * noise) if base else spread * noise
        out[name] = __import__('jax').numpy.asarray(drawn.astype(out[name].dtype))
    for name, factor in factors.items():
        out[name] = (out[name] * factor).astype(out[name].dtype)
    return out
```

```python
import math
from contextlib import ExitStack

import numpy as np

import concourse.bass as bass
from concourse import mybir

F32 = mybir.dt.float32
I32 = mybir.dt.int32
ALU = mybir.AluOpType
ACT = mybir.ActivationFunctionType
AX = mybir.AxisListType.X

P = 128
SEQ = 256
D = 1024
NT = SEQ // P
KC = D // P
RMS_EPS = 1e-6
SUBLN_EPS = 1e-5
L2_EPS = 1e-6
HEADS_A = 4
DH = 64
ROT = 16
HALF_ROT = ROT // 2
ROPE_THETA = 500000.0
LAM0 = 0.8 - 0.6 * math.exp(0.0)
SC_TAPS = 3
DN_TAPS = 4
HEADS_D = 8
QKV_CHUNKS = 3 * HEADS_D
FF = 3584
FJ = FF // 512
NE = 8
MAX_OVER = 3
RING = 7
SLAB = 4096
PER_BLOCK = 3 * FJ
PLE = 256
NEG = -1.0e30
TWO_PI = (6.28125, 0.0019350051879882812, 2 * math.pi - 6.28125 - 0.0019350051879882812)
N_SETUP = 16 * 17
LEVELS = 7

C_ID, C_UP, C_ONE, C_IOTA, C_LEV = 0, 128, 256, 384, 512
C_FREQ = C_LEV + LEVELS * 128
C_EID = C_FREQ + HALF_ROT
C_LOW = C_EID + NE
C_W = C_LOW + NE * NE

S_QKV_E, S_CONV_E, S_OUT_E, S_MLP = 0, 3, 6, 8
S_GATE_E = S_MLP + PER_BLOCK
S_PROJ_E = S_GATE_E + 2
S_QKV_O = S_PROJ_E + 1
S_Z = S_QKV_O + 6
S_OUT_O = S_Z + 2
S_MOE = S_OUT_O + 2
assert S_MOE % RING == 0 and PER_BLOCK % RING == 0


def shape_constants():
    c = np.zeros((P, C_W), np.float32)
    i = np.arange(P)
    c[:, C_ID:C_ID + P] = np.eye(P)
    c[:, C_UP:C_UP + P] = i[:, None] <= i[None, :]
    c[:, C_ONE:C_ONE + P] = 1.0
    c[:, C_IOTA:C_IOTA + P] = i[None, :]
    for level in range(LEVELS):
        s = 1 << level
        rows, cols = i[:, None] // s, i[None, :] // s
        c[:, C_LEV + level * P:C_LEV + (level + 1) * P] = (cols % 2 == 1) & (rows == cols - 1)
    c[:, C_FREQ:C_FREQ + HALF_ROT] = np.float32(ROPE_THETA) ** (
        -np.arange(0, ROT, 2, dtype=np.float32) / np.float32(ROT))
    e = np.arange(NE)
    c[:, C_EID:C_EID + NE] = e
    c[:, C_LOW:C_LOW + NE * NE] = (e[None, :] < e[:, None]).reshape(-1)
    return c


def moe_order():
    order = [(0, 0), (1, 0)]
    for j in range(1, FJ):
        order += [(0, j), (1, j), (2, j - 1)]
    return order + [(2, FJ - 1)]


MOE_ORDER = moe_order()
MOE_AT = {key: i for i, key in enumerate(MOE_ORDER)}


def gemm_order():
    g = [(("qkv", n, t), S_QKV_E + n) for n in range(3) for t in range(NT)]
    g += [(("conv", n, m), S_CONV_E + n) for n in range(3) for m in range(2)]
    g += [(("out_e", j, t), S_OUT_E + j) for j in range(2) for t in range(NT)]

    def h1(j, t):
        return [(("h1", j, t), S_MLP + 3 * j)] if j < FJ else []

    def h3(j, t):
        return [(("h3", j, t), S_MLP + 3 * j + 1)] if j < FJ else []

    def y(j, t):
        return [(("y", j, t), S_MLP + 3 * j + 2)]

    g += h1(0, 0) + h1(0, 1) + h3(0, 0) + h3(0, 1)
    for j in range(FJ):
        g += y(j, 0) + h1(j + 1, 0) + y(j, 1) + h1(j + 1, 1) + h3(j + 1, 0) + h3(j + 1, 1)
    g += [(("gate", j, t), S_GATE_E + j) for j in range(2) for t in range(NT)]
    g += [(("proj", j, t), S_PROJ_E) for j in range(2) for t in range(NT)]
    g += [(("cin", n, m), S_QKV_O + n) for n in range(6) for m in range(2)]
    g += [(("z", j, t), S_Z + j) for j in range(2) for t in range(NT)]
    g += [(("out_o", j, t), S_OUT_O + j) for j in range(2) for t in range(NT)]
    return g


GEMMS = gemm_order()
DONE_AT = {what: i + 1 for i, (what, _) in enumerate(GEMMS)}
USED_AT = {n: i + 1 for i, (_, n) in enumerate(GEMMS)}
G_MOE = len(GEMMS)
TAIL = {("gate", j, t): 1 + 2 * j + t for j in range(2) for t in range(NT)}
TAIL.update({("proj", j, t): 5 + 2 * j + t for j in range(2) for t in range(NT)})
ARENA = 15600


def trunk(nc, a, out):
    ctx = ExitStack()
    with ctx:
        def sb(name, shape, dt=F32):
            return ctx.enter_context(nc.sbuf_tensor(name, shape, dt))

        def sem(name):
            return ctx.enter_context(nc.semaphore(name))

        ring = sb("ring", [P, RING, SLAB])
        h = sb("h", [P, NT, D])
        hn = sb("hn", [P, NT, D])
        xTs = sb("xTs", [P, KC * SEQ])
        xT = xTs[:, :].rearrange("p (k s) -> p k s", k=KC)
        con = sb("con", [P, C_W])
        wba = sb("wba", [P, KC, 2 * HEADS_D])
        wrt = sb("wrt", [P, KC, NE])
        gT = sb("gT", [P, 62])
        cwT = sb("cwT", [P, DN_TAPS * QKV_CHUNKS])
        alog = sb("alog", [P, HEADS_D])
        dtb = sb("dtb", [P, HEADS_D])
        ssq = sb("ssq", [P, 7, NT])
        std = sb("std", [P, 7, NT])
        rstd = sb("rstd", [P, 7, NT])
        eps6 = sb("eps6", [P, 1])
        eps5 = sb("eps5", [P, 1])
        posi = sb("posi", [P, NT + SEQ], I32)
        posc = sb("posc", [P, NT])
        cs = sb("cs", [P, 2, NT, HALF_ROT])
        lamd = sb("lamd", [P, 2])
        lame = sb("lame", [P, 2])
        nlam = sb("nlam", [P, 1])
        mx = sb("mx", [P, 2, 4])
        nb = sb("nb", [P, 2, 4])
        esum = sb("esum", [P, 2, 4])
        erc = sb("erc", [P, 2, 4])
        oss = sb("oss", [P, NT * HEADS_D])
        osd = sb("osd", [P, NT * HEADS_D])
        ors = sb("ors", [P, NT * HEADS_D])
        ba = sb("ba", [P, NT, 2 * HEADS_D])
        yneg = sb("yneg", [P, NT, 2 * HEADS_D])
        yexp = sb("yexp", [P, NT, 2 * HEADS_D])
        yln = sb("yln", [P, NT, HEADS_D])
        beta = sb("beta", [P, NT, HEADS_D])
        gdec = sb("gdec", [P, NT, HEADS_D])
        cum = sb("cum", [P, NT, 2, HEADS_D])
        dcy = sb("dcy", [P, NT, 2, HEADS_D])
        bec = sb("bec", [P, NT, HEADS_D])
        ealog = sb("ealog", [P, HEADS_D])
        NBC = NE + MAX_OVER + 1
        posb = sb("posb", [P, NT, NBC])
        gateb = sb("gateb", [P, NT, NBC])
        blk_i = sb("blk_i", [P, 16], I32)
        ps = ctx.enter_context(nc.psum_tensor("ps", [P, 8, 512], F32))
        arena = sb("arena", [P, ARENA])

        ident = con[:, C_ID:C_ID + P]
        upper = con[:, C_UP:C_UP + P]
        ones = con[:, C_ONE:C_ONE + P]
        iota = con[:, C_IOTA:C_IOTA + P]

        def over(ap, n):
            return ap.unsqueeze(1).broadcast_to([P, n, ap.shape[-1]])

        def along(ap, n):
            return ap.unsqueeze(2).broadcast_to([P, ap.shape[-1], n])

        def level_mask(l):
            return con[:, C_LEV + l * P:C_LEV + (l + 1) * P]

        class Area:

            def __init__(self, at=0):
                self.at = at

            def take(self, *dims):
                n = int(np.prod(dims))
                v = arena[:, self.at:self.at + n]
                self.at += n
                assert self.at <= ARENA, self.at
                if len(dims) == 1:
                    return v
                names = "abcd"[:len(dims)]
                return v.rearrange(f"p ({' '.join(names)}) -> p {' '.join(names)}",
                                   **dict(zip(names[1:], dims[1:])))

        G_MIX, G_FFN, G_PLE, G_SUB, G_ON, G_CW = 0, 16, 32, 48, 49, 50
        GAIN_AT = [G_MIX, G_FFN, G_PLE, G_MIX + KC, G_FFN + KC, G_PLE + KC]

        ar = Area()
        qk = ar.take(NT, 1024)
        vt = ar.take(NT, 512)
        qkT = ar.take(KC, SEQ)
        mixT = ar.take(KC, SEQ)
        cT = ar.take(4, SEQ)
        PADS = SC_TAPS - 1 + SEQ
        upad = ar.take(4, PADS)
        rt = ar.take(4, 16, HALF_ROT)
        sm = ar.take(2, 4, SEQ)
        adf = ar.take(2, NT, SEQ)
        maskb = ar.take(NT, SEQ)
        rows1 = ar.take(P)
        rows2 = ar.take(P)
        posrow = ar.take(SEQ)
        lamv = ar.take(4, DH)
        lamp = ar.take(2, DH)
        ang = ar.take(NT, HALF_ROT)
        turns = ar.take(NT, HALF_ROT)
        oat = qk[:, 0, :].rearrange("p (t h v) -> p t h v", t=NT, h=HEADS_A)
        osq = qk[:, 1, :].rearrange("p (t h v) -> p t h v", t=NT, h=HEADS_A)
        aTt = cT.rearrange("p (u k) s -> p u k s", u=2)

        ar = Area()
        sil = ar.take(2, 512)
        gated = ar.take(2, 512)
        gTt = ar.take(2, 4, P)
        sgm = ar.take(NT, D)
        ptmp = ar.take(2, 512)
        p_tok = ar.take(NT, PLE)
        pTl = ar.take(2, SEQ)
        gfin = ar.take(D)
        xg = ar.take(KC, P)
        ysb = ar.take(D)
        sel = ar.take(NT, P)
        selg = ar.take(NT, P)
        selgT = ar.take(SEQ)
        r_l = ar.take(NT, NE)
        r_gt = ar.take(NT, NE * NE)
        r_eq = ar.take(NT, NE * NE)
        r_rank = ar.take(NT, NE)
        r_m = ar.take(NT, NE)
        r_mx = ar.take(NT)
        r_nmx = ar.take(NT)
        r_e = ar.take(NT, NE)
        r_s = ar.take(NT)
        r_rs = ar.take(NT)
        r_im = ar.take(NT, NE)
        r_cnt = ar.take(NE)
        r_ov = ar.take(NE)
        r_w = ar.take(NE * NE)
        r_ord = ar.take(NE)
        r_sl = ar.take(MAX_OVER, NE)
        r_t = ar.take(NT, MAX_OVER, NE)
        blk_f = ar.take(16)

        ar = Area()
        qkvT = ar.take(QKV_CHUNKS, SEQ)
        PADW = DN_TAPS - 1 + SEQ
        upo_at = ar.at
        upo = ar.take(2, 4, PADW)
        LT = ar.take(HEADS_D, P)
        X = ar.take(HEADS_D, P)
        XT = ar.take(NT, HEADS_D, P)
        bt = ar.take(2, 4, P)
        pm = ar.take(2, 4, P)
        S1 = ar.take(HEADS_D, P)
        qT, kT = qkvT[:, 0:8, :], qkvT[:, 8:16, :]
        by_tok = dict(t=NT, h=HEADS_D)
        ktok = arena[:, upo_at:upo_at + 2048].rearrange("p (t h d) -> p t h d", **by_tok)
        vb = xTs[:, :].rearrange("p (t h d) -> p t h d", **by_tok)
        AT = arena[:, 4096:6144].rearrange("p (t h d) -> p t h d", **by_tok)
        odq = arena[:, 0:2048].rearrange("p (t h d) -> p t h d", **by_tok)
        odT = qkvT[:, 8:16, :]
        un = bt.rearrange("p a b c -> p (a b) c")
        qgT = pm.rearrange("p a b c -> p (a b) c")
        nwT, kbe, zs = LT, X, hn

        slab_in = [sem(f"slab_in{i}") for i in range(RING)]
        gemm_done = sem("gemm_done")
        x_in, con_in, setup_in, out_done = sem("x_in"), sem("con_in"), sem("setup_in"), sem("out_done")
        p_in, gfin_in = sem("p_in"), sem("gfin_in")
        dve_link, act_link, pool_link = sem("dve_link"), sem("act_link"), sem("pool_link")
        h_ready = sem("h_ready")
        n_std, n_hn, n_ps, n_xa, n_xd = (sem(x) for x in ("n_std", "n_hn", "n_ps", "n_xa", "n_xd"))
        eps_set, st_ps, st_sb = sem("eps_set"), sem("st_ps"), sem("st_sb")
        ang_rdy, cs_rdy, lam_dot, lam_exp = sem("ang_rdy"), sem("cs_rdy"), sem("lam_dot"), sem("lam_exp")
        qkv_sb, v_sb, c_sb, xb_used, rope_done, mix_conv = (sem(x) for x in (
            "qkv_sb", "v_sb", "c_sb", "xb_used", "rope_done", "mix_conv"))
        qkT_ps, qkT_sb = sem("qkT_ps"), sem("qkT_sb")
        sc_ps, sm_read, sm_rdy, ex_done, a_done = (sem(x) for x in (
            "sc_ps", "sm_read", "sm_rdy", "ex_done", "a_done"))
        aT_ps, aT_sb, av_ps, o_sb, o_ss, o_sd, o_nrm, oT_ps, oT_sb = (sem(x) for x in (
            "aT_ps", "aT_sb", "av_ps", "o_sb", "o_ss", "o_sd", "o_nrm", "oT_ps", "oT_sb"))
        silu_sb, gated_sb, gT_ps, gT_sb = sem("silu_sb"), sem("gated_sb"), sem("gT_ps"), sem("gT_sb")
        pT_ps, pT_sb, sgm_sb = sem("pT_ps"), sem("pT_sb"), sem("sgm_sb")
        ba_ps, ba_neg, ba_exp, ba_ln, g_rdy, cum_ps, cum_sb, dcy_rdy = (sem(x) for x in (
            "ba_ps", "ba_neg", "ba_exp", "ba_ln", "g_rdy", "cum_ps", "cum_sb", "dcy_rdy"))
        q_pad, cv_done, cv_silu, z_sb, pad_zero = (sem(x) for x in (
            "q_pad", "cv_done", "cv_silu", "z_sb", "pad_zero"))
        l2_sq, l2_ps, l2_sd, l2_done = sem("l2_sq"), sem("l2_ps"), sem("l2_sd"), sem("l2_done")
        kv_ps, k_sb, vb_sb = sem("kv_ps"), sem("k_sb"), sem("vb_sb")
        rc_ps, dd_rdy, dec_exp, dec_rdy, br_ps, kb_rdy, lt_ps, lt_sb, at_ps, at_sb = (sem(x) for x in (
            "rc_ps", "dd_rdy", "dec_exp", "dec_rdy", "br_ps", "kb_rdy", "lt_ps", "lt_sb", "at_ps", "at_sb"))
        bt_rdy, x1_rdy, x1_ps, x1_sb, p_ps, p_sb, x_ps, x_sb = (sem(x) for x in (
            "bt_rdy", "x1_rdy", "x1_ps", "x1_sb", "p_ps", "p_sb", "x_ps", "x_sb"))
        ksc_rdy, w_ps, w_sb, u_ps, u_sb, od_ps, od_sb, s_ps, s_sb, qg_ps, qg_exp, qg_rdy = (
            sem(x) for x in ("ksc_rdy", "w_ps", "w_sb", "u_ps", "u_sb", "od_ps", "od_sb", "s_ps",
                             "s_sb", "qg_ps", "qg_exp", "qg_rdy"))
        od_ss, od_sd, od_nrm, odT_ps, odT_sb = (sem(x) for x in (
            "od_ss", "od_sd", "od_nrm", "odT_ps", "odT_sb"))
        lg_ps, lg_max, lg_exp, mk_rdy, rk_ps, tab_rdy = (sem(x) for x in (
            "lg_ps", "lg_max", "lg_exp", "mk_rdy", "rk_ps", "tab_rdy"))
        m_sel, m_xg_ps, m_xg, m_sT_ps, m_sT = (sem(x) for x in (
            "m_sel", "m_xg_ps", "m_xg", "m_sT_ps", "m_sT"))
        m_silu, m_gated, m_gTps, m_gT, m_ysb, m_sc, m_add = (sem(x) for x in (
            "m_silu", "m_gated", "m_gTps", "m_gT", "m_ysb", "m_sc", "m_add"))
        f_out = sem("f_out")

        H_AT = {1: 4, 2: 8, 3: 12, 4: 16, 6: 20}

        def cols(w, j):
            return w.rearrange("(k p) n -> p k n", p=P)[:, :, j * 512:(j + 1) * 512]

        def rows(w, j):
            return w.rearrange("(k p) n -> p k n", p=P)[:, 4 * j:4 * j + 4, :]

        def cols_of(n):
            return ring[:, n % RING, :].rearrange("p (k n) -> p k n", n=512)

        def rows_of(n):
            return ring[:, n % RING, :].rearrange("p (k n) -> p k n", n=1024)

        wie, woe, wio, woo = a["w_in_even"][0], a["w_out_even"][0], a["w_in_odd"][0], a["w_out_odd"][0]
        static = [(cols(wie, j), 512) for j in (0, 1, 2, 4, 5, 3)]
        static += [(cols(woe, j), 512) for j in range(2)]
        for j in range(FJ):
            static += [(cols(a["w1_dense"][0], j), 512), (cols(a["w3_dense"][0], j), 512),
                       (rows(a["w2_dense"][0], j), 1024)]
        proj_src = [a["w_ple_proj"][i].rearrange("(k p) n -> p k n", p=P) for i in range(2)]
        static += [(cols(a["w_ple_gate"][0], j), 512) for j in range(2)] + [(proj_src[0], 1024)]
        static += [(cols(wio, j), 512) for j in range(8)] + [(cols(woo, j), 512) for j in range(2)]
        assert len(static) == S_MOE

        block = ctx.enter_context(nc.Block())

        @block.sync
        def _(sp):
            def put(n, src, width):
                dst = ring[:, n % RING, 0:src.shape[1] * width].rearrange("p (k n) -> p k n", n=width)
                sp.dma_start(dst, src).then_inc(slab_in[n % RING], 16)

            for n, (src, width) in enumerate(static):
                if n >= RING:
                    sp.wait_ge(gemm_done, USED_AT[n - RING])
                put(n, src, width)

            def expert_slab(e, i):
                m, j = MOE_ORDER[i]
                w = a[("w1_moe", "w3_moe", "w2_moe")[m]].rearrange("o e (k p) n -> p (o e) k n", p=P)
                w = w[:, bass.ds(e, 1)]
                if m < 2:
                    return w[:, :, :, j * 512:(j + 1) * 512].rearrange("p o k n -> p (o k) n"), 512
                return w[:, :, 4 * j:4 * j + 4, :].rearrange("p o k n -> p (o k) n"), 1024

            for i in range(PER_BLOCK):
                before = S_MOE + i - RING
                sp.wait_ge(gemm_done, USED_AT[before] if before < S_MOE else G_MOE + i - RING + 1)
                put(i, *expert_slab(0, i))
            sp.wait_ge(tab_rdy, 1)
            nblk = sp.value_load(blk_i[0:1, 15:16], min_val=NE, max_val=NE + MAX_OVER)
            with sp.Fori(1, nblk) as b:
                e = sp.value_load(blk_i[0:1, bass.ds(b, 1)], min_val=0, max_val=NE - 1)
                for i in range(PER_BLOCK):
                    sp.wait_ge(gemm_done, b * PER_BLOCK + (G_MOE + i - RING + 1))
                    put(i, *expert_slab(e, i))
            for i, (src, width) in enumerate([(cols(a["w_ple_gate"][1], 0), 512),
                                              (cols(a["w_ple_gate"][1], 1), 512), (proj_src[1], 1024)]):
                sp.wait_ge(gemm_done, nblk * PER_BLOCK + (G_MOE + i - RING + 1))
                put(i, src, width)
            out_v = out.rearrange("o (t p) d -> p (o t) d", p=P)
            for t in range(NT):
                sp.wait_ge(f_out, t + 1)
                sp.dma_start(out_v[:, t, :], hn[:, t, :]).then_inc(out_done, 16)
            sp.wait_ge(out_done, 16 * NT)

        @block.tensor
        def _(pe):
            def slab_wait(n):
                pe.wait_ge(slab_in[n % RING], 16 * (n // RING + 1))

            def tokens_out(bank, x, n, t):
                for k in range(KC):
                    last = pe.matmul(ps[:, bank, :], x[:, k, t * P:(t + 1) * P], cols_of(n)[:, k, :],
                                     start=(k == 0), stop=(k == KC - 1))
                last.then_inc(gemm_done, 1)

            def channels_out(bank, n, m):
                for c in range(2):
                    for k in range(KC):
                        last = pe.matmul(ps[:, bank, c * SEQ:(c + 1) * SEQ],
                                         cols_of(n)[:, k, (2 * m + c) * P:(2 * m + c + 1) * P], xT[:, k, :],
                                         start=(k == 0), stop=(k == KC - 1))
                last.then_inc(gemm_done, 1)

            def down(banks, g, n, first, final):
                for half in range(2):
                    for c in range(4):
                        last = pe.matmul(ps[:, banks + half, :], g[:, c, :],
                                         rows_of(n)[:, c, half * 512:(half + 1) * 512],
                                         start=(first and c == 0), stop=(final and c == 3))
                last.then_inc(gemm_done, 1)

            def turn(bank, src, done):
                for c in range(4):
                    last = pe.transpose(ps[:, bank, c * P:(c + 1) * P], src[:, c * P:(c + 1) * P], ident)
                last.then_inc(done, 1)

            def norm_x(n):
                pe.wait_ge(n_hn, NT * (n + 1))
                for b in range(4):
                    for k in (2 * b, 2 * b + 1):
                        for t in range(NT):
                            at = (k % 2) * SEQ + t * P
                            last = pe.transpose(ps[:, b, at:at + P], hn[:, t, k * P:(k + 1) * P], ident)
                    last.then_inc(n_ps, 1)
                pe.wait_ge(n_xa, 4 * (n + 1))
                pe.wait_ge(n_xd, 4 * (n + 1))

            pe.wait_ge(con_in, 16)
            pe.wait_ge(setup_in, N_SETUP)
            pe.transpose(ps[:, 4, 0:62], rows1[0:62, :], ident[0:62, 0:62])
            pe.transpose(ps[:, 4, 128:224], rows2[0:96, :], ident[0:96, 0:96]).then_inc(st_ps, 1)

            norm_x(0)
            pe.wait_ge(st_sb, 2)
            for n in range(3):
                slab_wait(S_QKV_E + n)
                for t in range(NT):
                    tokens_out(2 * n + t, xT, S_QKV_E + n, t)
            for n in range(3):
                slab_wait(S_CONV_E + n)
                if n == 1:
                    pe.wait_ge(qkv_sb, 2)
                if n == 2:
                    pe.wait_ge(qkv_sb, 4)
                for m in range(2):
                    channels_out((6, 0, 2)[n] + m, S_CONV_E + n, m)
            pe.wait_ge(rope_done, NT)
            pe.wait_ge(v_sb, 2)
            pe.wait_ge(c_sb, 2)
            for b in range(4):
                for c in (2 * b, 2 * b + 1):
                    for t in range(NT):
                        at = (c % 2) * SEQ + t * P
                        last = pe.transpose(ps[:, 4 + b, at:at + P], qk[:, t, c * P:(c + 1) * P], ident)
                last.then_inc(qkT_ps, 1)

            def scores(hd):
                for m in range(2):
                    for t in range(NT):
                        last = pe.matmul(ps[:, 2 * (hd % 2) + m, t * SEQ:(t + 1) * SEQ],
                                         qkT[DH * m:DH * (m + 1), hd, t * P:(t + 1) * P],
                                         qkT[DH * m:DH * (m + 1), 4 + hd, :], start=True, stop=True)
                last.then_inc(sc_ps, 1)

            pe.wait_ge(qkT_sb, 4)
            pe.wait_ge(xb_used, 2)
            scores(0)
            pe.wait_ge(mix_conv, 4)
            scores(1)
            for hd in range(HEADS_A):
                pe.wait_ge(a_done, hd + 1)
                if hd >= 2:
                    pe.wait_ge(aT_sb, hd - 1)
                for kt in range(NT):
                    for t in range(NT):
                        at = kt * SEQ + t * P
                        last = pe.transpose(ps[:, 4 + hd % 2, at:at + P],
                                            adf[:, hd % 2, t, kt * P:(kt + 1) * P], ident)
                last.then_inc(aT_ps, 1)
                if hd + 2 < HEADS_A:
                    pe.wait_ge(sm_read, 2 * (hd + 1))
                    scores(hd + 2)
                pe.wait_ge(aT_sb, hd + 1)
                if hd >= 2:
                    pe.wait_ge(o_sb, hd - 1)
                for t in range(NT):
                    for kt in range(NT):
                        last = pe.matmul(ps[:, 6 + hd % 2, t * P:(t + 1) * P],
                                         aTt[:, hd % 2, kt, t * P:(t + 1) * P],
                                         vt[:, kt, hd * P:(hd + 1) * P], start=(kt == 0), stop=(kt == NT - 1))
                last.then_inc(av_ps, 1)
            pe.wait_ge(o_nrm, 1)
            for b in range(2):
                for hd in (2 * b, 2 * b + 1):
                    for t in range(NT):
                        at = (hd % 2) * SEQ + t * P
                        last = pe.transpose(ps[:, 4 + b, at:at + P], oat[:, t, hd, :], ident)
                last.then_inc(oT_ps, 1)
            pe.wait_ge(oT_sb, 2)
            for j in range(2):
                slab_wait(S_OUT_E + j)
                for t in range(NT):
                    tokens_out(2 * j + t, mixT, S_OUT_E + j, t)

            norm_x(1)

            def hidden(j, m, t):
                if j < FJ:
                    n = S_MLP + 3 * j + m
                    if t == 0:
                        slab_wait(n)
                    tokens_out(2 * t + m, xT, n, t)

            for m in range(2):
                for t in range(NT):
                    hidden(0, m, t)
            for j in range(FJ):
                pe.wait_ge(gated_sb, 2 * j + 1)
                turn(0, gated[:, 0, :], gT_ps)
                slab_wait(S_MLP + 3 * j + 2)
                pe.wait_ge(gT_sb, 2 * j + 1)
                down(4, gTt[:, 0], S_MLP + 3 * j + 2, j == 0, j == FJ - 1)
                pe.wait_ge(gated_sb, 2 * j + 2)
                turn(2, gated[:, 1, :], gT_ps)
                hidden(j + 1, 0, 0)
                pe.wait_ge(gT_sb, 2 * j + 2)
                down(6, gTt[:, 1], S_MLP + 3 * j + 2, j == 0, j == FJ - 1)
                hidden(j + 1, 0, 1)
                hidden(j + 1, 1, 0)
                hidden(j + 1, 1, 1)

            def embed(i, wait_slab):
                norm_x(2 + 3 * i)
                pe.wait_ge(p_in, 16 * (i + 1))
                for c in range(2):
                    for t in range(NT):
                        last = pe.transpose(ps[:, 4, c * SEQ + t * P:c * SEQ + (t + 1) * P],
                                            p_tok[:, t, c * P:(c + 1) * P], ident)
                last.then_inc(pT_ps, 1)
                base = S_GATE_E if i == 0 else 0
                for j in range(2):
                    wait_slab(j)
                    for t in range(NT):
                        tokens_out(2 * j + t, xT, base + j, t)
                pe.wait_ge(pT_sb, i + 1)
                wait_slab(2)
                for j in range(2):
                    for t in range(NT):
                        for c in range(2):
                            last = pe.matmul(ps[:, 4 + 2 * j + t, :], pTl[:, c, t * P:(t + 1) * P],
                                             rows_of(base + 2)[:, c, j * 512:(j + 1) * 512],
                                             start=(c == 0), stop=(c == 1))
                        last.then_inc(gemm_done, 1)

            embed(0, lambda j: slab_wait(S_GATE_E + j))

            norm_x(3)
            for t in range(NT):
                for k in range(KC):
                    last = pe.matmul(ps[:, 7, t * 16:(t + 1) * 16], xT[:, k, t * P:(t + 1) * P], wba[:, k, :],
                                     start=(k == 0), stop=(k == KC - 1))
            last.then_inc(ba_ps, 1)
            for n in range(6):
                slab_wait(S_QKV_O + n)
                if n >= 2:
                    pe.wait_ge(q_pad, 2 * (n - 1))
                for m in range(2):
                    channels_out(2 * (n % 2) + m, S_QKV_O + n, m)
            pe.wait_ge(g_rdy, 1)
            for t in range(NT):
                pe.matmul(ps[:, 6, t * 16:t * 16 + 8], upper, gdec[:, t, :], start=True, stop=True)
                last = pe.matmul(ps[:, 6, t * 16 + 8:t * 16 + 16], ones, gdec[:, t, :], start=True, stop=True)
            last.then_inc(cum_ps, 1)
            pe.wait_ge(cum_sb, 1)
            for j in range(2):
                slab_wait(S_Z + j)
                for t in range(NT):
                    tokens_out(4 + 2 * j + t, xT, S_Z + j, t)

            pe.wait_ge(q_pad, 12)
            for g in range(8):
                pe.wait_ge(l2_sq, g + 1)
                if g >= 4:
                    pe.wait_ge(l2_sd, g - 3)
                pe.matmul(ps[:, g % 4, :], ones, bt[:, g % 2].rearrange("p a b -> p (a b)"),
                          start=True, stop=True).then_inc(l2_ps, 1)
            pe.wait_ge(l2_done, 8)
            pe.wait_ge(z_sb, 4)
            for t in range(NT):
                for b in range(4):
                    for c in range(4):
                        hd = 4 * b + c
                        last = pe.transpose(ps[:, 4 * t + b, c * P:(c + 1) * P],
                                            qkvT[:, 8 + hd, t * P:(t + 1) * P], ident)
                    last.then_inc(kv_ps, 1)

            def head_cols(bank, c):
                return ps[:, bank, c * P:(c + 1) * P]

            for t in range(NT):
                tok = slice(t * P, (t + 1) * P)
                u = 2 * t
                if t == 0:
                    pe.wait_ge(k_sb, 4)
                    pe.wait_ge(vb_sb, 4)
                else:
                    pe.wait_ge(od_sb, 2)
                    pe.wait_ge(s_sb, 2)
                for g in range(2):
                    for c in range(4):
                        last = pe.matmul(head_cols(g, c), gdec[:, t, 4 * g + c:4 * g + c + 1].broadcast_to([P, P]),
                                         upper, start=True, stop=True)
                    last.then_inc(rc_ps, 1)
                    for c in range(4):
                        last = pe.matmul(head_cols(2 + g, c), beta[:, t, 4 * g + c:4 * g + c + 1].broadcast_to([P, P]),
                                         ident, start=True, stop=True)
                    last.then_inc(br_ps, 1)
                for g in range(2):
                    for c in range(4):
                        last = pe.matmul(head_cols(6 + g, c), kT[:, 4 * g + c, tok], qT[:, 4 * g + c, tok],
                                         start=True, stop=True)
                    last.then_inc(at_ps, 1)
                for g in range(2):
                    pe.wait_ge(kb_rdy, u + g + 1)
                    for c in range(4):
                        last = pe.matmul(head_cols(4 + g, c), kT[:, 4 * g + c, tok], pm[:, g, c, :],
                                         start=True, stop=True)
                    last.then_inc(lt_ps, 1)
                for g in range(2):
                    pe.wait_ge(x1_rdy, u + g + 1)
                    for c in range(4):
                        last = pe.transpose(head_cols(g, c), XT[:, t, 4 * g + c, :], ident)
                    last.then_inc(x1_ps, 1)
                for l in range(1, LEVELS):
                    v = (LEVELS - 1) * u + 2 * (l - 1)
                    for g in range(2):
                        pe.wait_ge(bt_rdy, LEVELS * u + 2 * l + g + 1)
                        if l == 1:
                            pe.wait_ge(x1_sb, u + g + 1)
                        else:
                            pe.wait_ge(x_sb, v - 1 + g)
                        for c in range(4):
                            last = pe.matmul(head_cols(2 + g, c), bt[:, g, c, :], X[:, 4 * g + c, :],
                                             start=True, stop=True)
                        last.then_inc(p_ps, 1)
                    for g in range(2):
                        if l == 1:
                            pe.wait_ge(at_sb, u + g + 1)
                            pe.wait_ge(lt_sb, u + g + 1)
                        pe.wait_ge(p_sb, v + g + 1)
                        for c in range(4):
                            last = pe.matmul(head_cols(6 + g, c), pm[:, g, c, :], XT[:, t, 4 * g + c, :],
                                             start=True, stop=True)
                        if l < LEVELS - 1:
                            for c in range(4):
                                last = pe.matmul(head_cols(4 + g, c), XT[:, t, 4 * g + c, :], pm[:, g, c, :],
                                                 start=True, stop=True)
                        last.then_inc(x_ps, 1)
                pe.wait_ge(x_sb, (LEVELS - 1) * (u + 2))
                pe.wait_ge(ksc_rdy, t + 1)
                if t == 0:
                    for g in range(2):
                        for c in range(4):
                            last = pe.matmul(head_cols(g, c), XT[:, 0, 4 * g + c, :], vb[:, 0, 4 * g + c, :],
                                             start=True, stop=True)
                        last.then_inc(u_ps, 1)
                    for g in range(2):
                        pe.wait_ge(u_sb, g + 1)
                        for c in range(4):
                            last = pe.matmul(head_cols(4 + g, c), kbe[:, 4 * g + c, :], un[:, 4 * g + c, :],
                                             start=True, stop=True)
                        last.then_inc(s_ps, 1)
                        for c in range(4):
                            last = pe.matmul(head_cols(2 + g, c), AT[:, 0, 4 * g + c, :], un[:, 4 * g + c, :],
                                             start=True, stop=True)
                        last.then_inc(od_ps, 1)
                else:
                    for g in range(2):
                        for c in range(4):
                            last = pe.matmul(head_cols(g, c), kbe[:, 4 * g + c, :], XT[:, 1, 4 * g + c, :],
                                             start=True, stop=True)
                        last.then_inc(w_ps, 1)
                    for g in range(2):
                        for c in range(4):
                            last = pe.matmul(head_cols(6 + g, c), gdec[:, 1, 4 * g + c:4 * g + c + 1].broadcast_to([P, P]),
                                             upper, start=True, stop=True)
                        last.then_inc(qg_ps, 1)
                    for g in range(2):
                        pe.wait_ge(w_sb, g + 1)
                        for c in range(4):
                            hd = 4 * g + c
                            pe.matmul(head_cols(2 + g, c), XT[:, 1, hd, :], vb[:, 1, hd, :], start=True, stop=False)
                            last = pe.matmul(head_cols(2 + g, c), nwT[:, hd, :], S1[:, hd, :], start=False, stop=True)
                        last.then_inc(u_ps, 1)
                    for g in range(2):
                        pe.wait_ge(u_sb, 2 + g + 1)
                        pe.wait_ge(qg_rdy, g + 1)
                        for c in range(4):
                            hd = 4 * g + c
                            pe.matmul(head_cols(4 + g, c), qgT[:, hd, :], S1[:, hd, :], start=True, stop=False)
                            last = pe.matmul(head_cols(4 + g, c), AT[:, 1, hd, :], un[:, hd, :], start=False, stop=True)
                        last.then_inc(od_ps, 1)
            for b in range(4):
                pe.wait_ge(od_nrm, NT)
                for hd in (2 * b, 2 * b + 1):
                    for t in range(NT):
                        at = (hd % 2) * SEQ + t * P
                        last = pe.transpose(ps[:, b, at:at + P], AT[:, t, hd, :], ident)
                last.then_inc(odT_ps, 1)
            pe.wait_ge(odT_sb, 4)
            for j in range(2):
                slab_wait(S_OUT_O + j)
                for t in range(NT):
                    tokens_out(4 + 2 * j + t, odT, S_OUT_O + j, t)

            norm_x(4)
            for t in range(NT):
                for k in range(KC):
                    last = pe.matmul(ps[:, 4, t * NE:(t + 1) * NE], xT[:, k, t * P:(t + 1) * P], wrt[:, k, :],
                                     start=(k == 0), stop=(k == KC - 1))
            last.then_inc(lg_ps, 1)
            pe.wait_ge(mk_rdy, 1)
            pe.matmul(ps[:, 5, 0:NE], upper, r_m[:, 0, :], start=True, stop=True)
            pe.matmul(ps[:, 5, NE:2 * NE], ones, r_m[:, 0, :], start=True, stop=False)
            pe.matmul(ps[:, 5, NE:2 * NE], upper, r_m[:, 1, :], start=False, stop=True)
            pe.matmul(ps[:, 5, 2 * NE:3 * NE], ones, r_m[:, 0, :], start=True, stop=False)
            pe.matmul(ps[:, 5, 2 * NE:3 * NE], ones, r_m[:, 1, :], start=False, stop=True).then_inc(rk_ps, 1)
            pe.wait_ge(tab_rdy, 1)
            nblk = pe.value_load(blk_i[0:1, 15:16], min_val=NE, max_val=NE + MAX_OVER)

            def gather():
                for q in range(2):
                    for c in range(4):
                        for t in range(NT):
                            last = pe.matmul(ps[:, 6 + q, c * P:(c + 1) * P],
                                             hn[:, t, (4 * q + c) * P:(4 * q + c + 1) * P], sel[:, t, :],
                                             start=(t == 0), stop=(t == NT - 1))
                    last.then_inc(m_xg_ps, 1)

            pe.wait_ge(m_sel, 1)
            gather()
            with pe.Fori(0, nblk) as b:
                def arrived(m, j):
                    i = MOE_AT[m, j]
                    pe.wait_ge(slab_in[i % RING], b * (16 * PER_BLOCK // RING) + 16 * ((S_MOE + i) // RING + 1))

                def up(m, j):
                    arrived(m, j)
                    tokens_out(2 * (j % 2) + m, xg, MOE_AT[m, j], 0)

                pe.wait_ge(m_xg, b * 2 + 2)
                up(0, 0)
                up(1, 0)
                pe.wait_ge(m_add, b * 4 + 1)
                for t in range(NT):
                    last = pe.transpose(ps[:, 6, t * P:(t + 1) * P], selg[:, t, :], ident)
                last.then_inc(m_sT_ps, 1)
                for j in range(FJ):
                    if j + 1 < FJ:
                        up(0, j + 1)
                    else:
                        pe.wait_ge(m_sel, b + 2)
                        pe.wait_ge(m_sT, b + 1)
                        gather()
                    pe.wait_ge(m_gated, b * FJ + (j + 1))
                    turn(2 * (j % 2), gated[:, j % 2, :], m_gTps)
                    if j + 1 < FJ:
                        up(1, j + 1)
                    arrived(2, j)
                    pe.wait_ge(m_gT, b * FJ + (j + 1))
                    down(4, gTt[:, j % 2], MOE_AT[2, j], j == 0, j == FJ - 1)
                pe.wait_ge(m_ysb, b * 2 + 2)
                for t in range(NT):
                    if t == 1:
                        pe.wait_ge(m_xg, b * 2 + 4)
                    for half in range(2):
                        pe.matmul(ps[:, 2 + 4 * t + half, :], selgT[:, t * P:(t + 1) * P],
                                  ysb[:, half * 512:(half + 1) * 512], start=True, stop=True).then_inc(m_sc, 1)

            turns_of_ring = PER_BLOCK // RING

            def tail_wait(j):
                pe.wait_ge(slab_in[j], nblk * (16 * turns_of_ring) + 16 * (S_MOE // RING + 1))

            embed(1, tail_wait)

        @block.scalar
        def _(act):
            count = [0]

            def link(ins):
                count[0] += 1
                ins.then_inc(act_link, 1)
                act.wait_ge(act_link, count[0])

            act.dma_start(h[:, :, :], a["x"][0].rearrange("(t p) d -> p t d", p=P)).then_inc(x_in, 16)
            act.dma_start(con[:, :], a["con"]).then_inc(con_in, 16)
            small = [
                (rows1[0:16, :], a["ln_mix"].rearrange("i (k p) -> (i k) p", p=P)),
                (rows1[16:32, :], a["ln_ffn"].rearrange("i (k p) -> (i k) p", p=P)),
                (rows1[32:48, :], a["ln_ple"].rearrange("i (k p) -> (i k) p", p=P)),
                (rows1[48:49, :], a["subln_gain"]),
                (rows1[49:50, :], a["onorm_gain"]),
                (rows1[50:62, :], a["conv_w_short"].rearrange("o j (m p) -> (o j m) p", p=P)),
                (rows2[0:96, :], a["conv_w_qkv"].rearrange("o j (m p) -> (o j m) p", p=P)),
                (posi[:, 0:NT], a["positions"].rearrange("o (t p) -> p (o t)", p=P)),
                (posi[:, NT:NT + SEQ], a["positions"].broadcast_to([P, SEQ])),
            ]
            small += [(lamv[:, i, :], a[w].broadcast_to([P, DH])) for i, w in enumerate(("lam_q1", "lam_k1", "lam_q2", "lam_k2"))]
            small += [
                (alog[:, :], a["a_log"].broadcast_to([P, HEADS_D])),
                (dtb[:, :], a["dt_bias"].broadcast_to([P, HEADS_D])),
                (wba[:, :, :], wio[:, 4 * 1024:4 * 1024 + 2 * HEADS_D].rearrange("(k p) n -> p k n", p=P)),
                (wrt[:, :, :], a["w_router"][0].rearrange("(k p) n -> p k n", p=P)),
            ]
            assert 16 * len(small) == N_SETUP
            for dst, src in small:
                act.dma_start(dst, src, allow_slow_non_contiguous=True).then_inc(setup_in, 16)

            def norm_std(n):
                for t in range(NT):
                    last = act.activation(hn[:, t, :], h[:, t, :], ACT.Square, accum_out=ssq[:, n, t:t + 1])
                link(last)
                act.activation(std[:, n, :], ssq[:, n, :], ACT.Sqrt, scale=1.0 / D, bias=eps6[:, 0:1]).then_inc(n_std, 1)

            def norm_xT(n):
                for b in range(2):
                    act.wait_ge(n_ps, 4 * n + b + 1)
                    for k in (2 * b, 2 * b + 1):
                        act.activation(xT[:, k, :], ps[:, b, (k % 2) * SEQ:(k % 2 + 1) * SEQ], ACT.Copy,
                                       scale=gT[:, GAIN_AT[n] + k:GAIN_AT[n] + k + 1]).then_inc(n_xa, 1)

            act.wait_ge(eps_set, 1)
            act.wait_ge(x_in, 16)
            norm_std(0)
            act.wait_ge(lam_dot, 1)
            act.activation(lame[:, :], lamd[:, :], ACT.Exp).then_inc(lam_exp, 1)
            act.wait_ge(st_sb, 2)
            norm_xT(0)
            act.wait_ge(ang_rdy, 1)
            act.activation(cs[:, :, :, :], cs[:, :, :, :], ACT.Sin).then_inc(cs_rdy, 1)

            for n in range(2):
                for t in range(NT):
                    act.wait_ge(gemm_done, DONE_AT["qkv", n, t])
                    act.activation(qk[:, t, n * 512:(n + 1) * 512], ps[:, 2 * n + t, :], ACT.Copy).then_inc(qkv_sb, 1)
            for t in range(NT):
                act.wait_ge(gemm_done, DONE_AT["qkv", 2, t])
                act.activation(vt[:, t, :], ps[:, 4 + t, :], ACT.Copy).then_inc(v_sb, 1)
            for m in range(2):
                act.wait_ge(gemm_done, DONE_AT["conv", 0, m])
                act.activation(cT[:, 2 * m:2 * m + 2, :], ps[:, 6 + m, :].rearrange("p (c s) -> p c s", c=2),
                               ACT.Copy).then_inc(c_sb, 1)
            for b in range(2):
                act.wait_ge(qkT_ps, b + 1)
                act.activation(qkT[:, 2 * b:2 * b + 2, :], ps[:, 4 + b, :].rearrange("p (c s) -> p c s", c=2),
                               ACT.Copy).then_inc(qkT_sb, 1)

            def exps(hd):
                act.wait_ge(sm_rdy, hd + 1)
                for i in range(4):
                    last = act.activation(sm[:, hd % 2, i, :], sm[:, hd % 2, i, :], ACT.Exp, scale=DH ** -0.5,
                                          bias=nb[:, hd % 2, i:i + 1], accum_out=esum[:, hd % 2, i:i + 1])
                last.then_inc(ex_done, 1)

            exps(0)
            for hd in range(HEADS_A):
                if hd + 1 < HEADS_A:
                    exps(hd + 1)
                act.wait_ge(aT_ps, hd + 1)
                if hd >= 2:
                    act.wait_ge(av_ps, hd - 1)
                act.activation(aTt[:, hd % 2, :, :], ps[:, 4 + hd % 2, :].rearrange("p (k s) -> p k s", k=NT),
                               ACT.Copy).then_inc(aT_sb, 1)
            act.wait_ge(o_ss, 1)
            act.activation(osd[:, 0:8], oss[:, 0:8], ACT.Sqrt, scale=1.0 / P, bias=eps5[:, 0:1]).then_inc(o_sd, 1)
            for b in range(2):
                act.wait_ge(oT_ps, b + 1)
                act.activation(mixT[:, 2 * b:2 * b + 2, :], ps[:, 4 + b, :].rearrange("p (c s) -> p c s", c=2),
                               ACT.Copy, scale=gT[:, G_SUB:G_SUB + 1]).then_inc(oT_sb, 1)

            act.wait_ge(h_ready, H_AT[1])
            act.dma_start(p_tok[:, :, :], a["p"][0, 0].rearrange("(t p) d -> p t d", p=P)).then_inc(p_in, 16)
            norm_std(1)
            norm_xT(1)

            def silus(j):
                for t in range(NT):
                    act.wait_ge(gemm_done, DONE_AT["h1", j, t])
                    act.activation(sil[:, t, :], ps[:, 2 * t, :], ACT.Silu).then_inc(silu_sb, 1)

            silus(0)
            for j in range(FJ):
                for t in range(NT):
                    act.wait_ge(gT_ps, 2 * j + t + 1)
                    act.activation(gTt[:, t], ps[:, 2 * t, :].rearrange("p (c s) -> p c s", c=4), ACT.Copy).then_inc(gT_sb, 1)
                if j + 1 < FJ:
                    silus(j + 1)

            def embed(i, product_wait):
                norm_xT(2 + 3 * i)
                act.wait_ge(pT_ps, i + 1)
                act.activation(pTl[:, :, :], ps[:, 4, :].rearrange("p (c s) -> p c s", c=2), ACT.Copy).then_inc(pT_sb, 1)
                for j in range(2):
                    for t in range(NT):
                        product_wait(("gate", j, t))
                        act.activation(sgm[:, t, j * 512:(j + 1) * 512], ps[:, 2 * j + t, :], ACT.Sigmoid).then_inc(sgm_sb, 1)

            act.wait_ge(h_ready, H_AT[2])
            norm_std(2)
            embed(0, lambda what: act.wait_ge(gemm_done, DONE_AT[what]))

            act.wait_ge(h_ready, H_AT[3])
            norm_std(3)
            norm_xT(3)
            act.wait_ge(ba_neg, 1)
            act.activation(yexp[:, :, :], yneg[:, :, :], ACT.Exp)
            act.activation(ealog[:, :], alog[:, :], ACT.Exp).then_inc(ba_exp, 1)
            act.wait_ge(ba_exp, 1)
            act.activation(yln[:, :, :], yexp[:, :, 8:16], ACT.Ln, bias=1.0).then_inc(ba_ln, 1)
            act.wait_ge(pad_zero, 1)
            for n in range(6):
                for m in range(2):
                    act.wait_ge(gemm_done, DONE_AT["cin", n, m])
                    if n >= 2 and m == 0:
                        act.wait_ge(cv_done, n - 1)
                    act.activation(upo[:, n % 2, 2 * m:2 * m + 2, DN_TAPS - 1:], ps[:, 2 * (n % 2) + m, :].rearrange(
                        "p (c s) -> p c s", c=2), ACT.Copy).then_inc(q_pad, 1)
                if n >= 1:
                    act.wait_ge(cv_done, n)
                    act.activation(qkvT[:, 4 * (n - 1):4 * n, :], qkvT[:, 4 * (n - 1):4 * n, :], ACT.Silu).then_inc(cv_silu, 1)
            act.wait_ge(cv_done, 6)
            act.activation(qkvT[:, 20:24, :], qkvT[:, 20:24, :], ACT.Silu).then_inc(cv_silu, 1)
            for j in range(2):
                for t in range(NT):
                    act.wait_ge(gemm_done, DONE_AT["z", j, t])
                    act.activation(zs[:, t, j * 512:(j + 1) * 512], ps[:, 4 + 2 * j + t, :], ACT.Silu).then_inc(z_sb, 1)
            act.wait_ge(cum_sb, 1)
            act.activation(dcy[:, :, :, :], dcy[:, :, :, :], ACT.Exp).then_inc(dcy_rdy, 1)
            act.wait_ge(cv_silu, 6)
            for g in range(9):
                if g < 8:
                    if g >= 2:
                        act.wait_ge(l2_ps, g - 1)
                    act.activation(bt[:, g % 2].rearrange("p a b -> p (a b)"),
                                   qkvT[:, 2 * g:2 * g + 2, :].rearrange("p a b -> p (a b)"), ACT.Square).then_inc(l2_sq, 1)
                if g >= 1:
                    act.wait_ge(l2_ps, g)
                    if g >= 3:
                        act.wait_ge(l2_done, g - 2)
                    act.activation(pm[:, (g - 1) % 2].rearrange("p a b -> p (a b)"), ps[:, (g - 1) % 4, :], ACT.Sqrt,
                                   bias=eps6[:, 0:1]).then_inc(l2_sd, 1)
            for t in range(NT):
                for b in range(2):
                    act.wait_ge(kv_ps, 4 * t + b + 1)
                    act.activation(ktok[:, t, 4 * b:4 * b + 4, :], ps[:, 4 * t + b, :].rearrange(
                        "p (c s) -> p c s", c=4), ACT.Copy).then_inc(k_sb, 1)
            four = dict(c=4)
            for t in range(NT):
                u = 2 * t
                for g in range(2):
                    act.wait_ge(dd_rdy, u + g + 1)
                    act.activation(AT[:, t, 4 * g:4 * g + 4, :], AT[:, t, 4 * g:4 * g + 4, :], ACT.Exp).then_inc(dec_exp, 1)
                for g in range(2):
                    act.wait_ge(x1_ps, u + g + 1)
                    act.activation(X[:, 4 * g:4 * g + 4, :], ps[:, g, :].rearrange("p (c s) -> p c s", **four),
                                   ACT.Copy).then_inc(x1_sb, 1)
                for l in range(1, LEVELS):
                    for g in range(2):
                        act.wait_ge(p_ps, (LEVELS - 1) * u + 2 * (l - 1) + g + 1)
                        act.activation(pm[:, g], ps[:, 2 + g, :].rearrange("p (c s) -> p c s", **four),
                                       ACT.Copy).then_inc(p_sb, 1)
                if t == 0:
                    for g in range(2):
                        act.wait_ge(u_ps, g + 1)
                        act.activation(un[:, 4 * g:4 * g + 4, :], ps[:, g, :].rearrange("p (c s) -> p c s", **four),
                                       ACT.Copy).then_inc(u_sb, 1)
                    for g in range(2):
                        act.wait_ge(s_ps, g + 1)
                        act.activation(S1[:, 4 * g:4 * g + 4, :], ps[:, 4 + g, :].rearrange("p (c s) -> p c s", **four),
                                       ACT.Copy).then_inc(s_sb, 1)
                else:
                    for g in range(2):
                        act.wait_ge(w_ps, g + 1)
                        act.activation(nwT[:, 4 * g:4 * g + 4, :], ps[:, g, :].rearrange("p (c s) -> p c s", **four),
                                       ACT.Copy, scale=-1.0).then_inc(w_sb, 1)
                    for g in range(2):
                        act.wait_ge(qg_ps, g + 1)
                        act.activation(qgT[:, 4 * g:4 * g + 4, :], ps[:, 6 + g, :].rearrange("p (c s) -> p c s", **four),
                                       ACT.Exp).then_inc(qg_exp, 1)
                    for g in range(2):
                        act.wait_ge(u_ps, 2 + g + 1)
                        act.activation(un[:, 4 * g:4 * g + 4, :], ps[:, 2 + g, :].rearrange("p (c s) -> p c s", **four),
                                       ACT.Copy).then_inc(u_sb, 1)
            act.wait_ge(od_sb, 4)
            for t in range(NT):
                last = act.activation(odq[:, t, :, :], AT[:, t, :, :], ACT.Square)
                last.then_inc(od_ss, 1)
            act.wait_ge(od_sd, 1)
            act.activation(osd[:, :], oss[:, :], ACT.Sqrt, scale=1.0 / P, bias=eps6[:, 0:1]).then_inc(od_sd, 1)
            for b in range(4):
                act.wait_ge(odT_ps, b + 1)
                act.activation(odT[:, 2 * b:2 * b + 2, :], ps[:, b, :].rearrange("p (c s) -> p c s", c=2), ACT.Copy,
                               scale=gT[:, G_ON:G_ON + 1]).then_inc(odT_sb, 1)

            act.wait_ge(h_ready, H_AT[4])
            norm_std(4)
            act.dma_start(p_tok[:, :, :], a["p"][1, 0].rearrange("(t p) d -> p t d", p=P)).then_inc(p_in, 16)
            act.dma_start(gfin[:, :], a["ln_final"].unsqueeze(0).broadcast_to([P, D])).then_inc(gfin_in, 16)
            norm_xT(4)
            act.wait_ge(lg_max, 1)
            for t in range(NT):
                last = act.activation(r_e[:, t, :], r_l[:, t, :], ACT.Exp, bias=r_nmx[:, t:t + 1])
            last.then_inc(lg_exp, 1)
            act.wait_ge(tab_rdy, 1)
            nblk = act.value_load(blk_i[0:1, 15:16], min_val=NE, max_val=NE + MAX_OVER)

            with act.Fori(0, nblk) as b:
                def silu_of(j):
                    act.wait_ge(gemm_done, b * PER_BLOCK + (G_MOE + MOE_AT[0, j] + 1))
                    act.activation(sil[:, j % 2, :], ps[:, 2 * (j % 2), :], ACT.Silu).then_inc(m_silu, 1)

                silu_of(0)
                act.wait_ge(m_sT_ps, b + 1)
                act.activation(selgT[:, :], ps[:, 6, 0:SEQ], ACT.Copy).then_inc(m_sT, 1)
                for j in range(FJ):
                    if j + 1 < FJ:
                        silu_of(j + 1)
                    act.wait_ge(m_gTps, b * FJ + (j + 1))
                    act.activation(gTt[:, j % 2], ps[:, 2 * (j % 2), :].rearrange("p (c s) -> p c s", c=4),
                                   ACT.Copy).then_inc(m_gT, 1)
                act.wait_ge(gemm_done, b * PER_BLOCK + (G_MOE + PER_BLOCK))
                for half in range(2):
                    act.activation(ysb[:, half * 512:(half + 1) * 512], ps[:, 4 + half, :], ACT.Copy).then_inc(m_ysb, 1)

            act.wait_ge(m_add, nblk * 4 + 1)
            norm_std(5)
            embed(1, lambda what: act.wait_ge(gemm_done, nblk * PER_BLOCK + (G_MOE + TAIL[what])))
            act.wait_ge(h_ready, H_AT[6])
            norm_std(6)

        @block.gpsimd
        def _(pool):
            for t in range(NT):
                u = 2 * t
                for l in range(LEVELS):
                    for g in range(2):
                        if l == 0:
                            pool.wait_ge(lt_sb, u + g + 1)
                            if t == 0:
                                pool.wait_ge(l2_ps, 8)
                            else:
                                pool.wait_ge(od_ps, 2)
                        elif l == 1:
                            pool.wait_ge(x1_rdy, u + g + 1)
                        else:
                            pool.wait_ge(p_ps, (LEVELS - 1) * u + 2 * (l - 2) + g + 1)
                        pool.tensor_tensor(bt[:, g], LT[:, 4 * g:4 * g + 4, :], over(level_mask(l), 4),
                                           ALU.mult).then_inc(bt_rdy, 1)

        @block.vector
        def _(dve):
            count = [0]

            def link(ins):
                count[0] += 1
                ins.then_inc(dve_link, 1)
                dve.wait_ge(dve_link, count[0])

            dve.memset(eps5[:, :], SUBLN_EPS)
            dve.memset(upad[:, :, 0:SC_TAPS - 1], 0.0)
            dve.memset(eps6[:, :], RMS_EPS).then_inc(eps_set, 1)
            dve.wait_ge(setup_in, N_SETUP)
            dve.tensor_tensor(lamp[:, :, :], lamv.rearrange("p (a b) d -> p a b d", b=2)[:, :, 0, :],
                              lamv.rearrange("p (a b) d -> p a b d", b=2)[:, :, 1, :], ALU.mult).then_inc(dve_link, 1)
            count[0] += 1
            dve.wait_ge(dve_link, count[0])
            dve.tensor_reduce(lamd[:, :], lamp[:, :, :], AX, ALU.add).then_inc(lam_dot, 1)
            dve.wait_ge(st_ps, 1)
            link(dve.tensor_copy(gT[:, :], ps[:, 4, 0:62]))
            dve.tensor_copy(cwT[:, :], ps[:, 4, 128:224]).then_inc(st_sb, 1)
            dve.tensor_scalar(gT[:, G_SUB:G_SUB + 1], gT[:, G_SUB:G_SUB + 1], 1.0 - LAM0, None, ALU.mult).then_inc(st_sb, 1)

            def norm_hn(n):
                dve.wait_ge(n_std, n + 1)
                link(dve.reciprocal(rstd[:, n, :], std[:, n, :]))
                for t in range(NT):
                    dve.tensor_scalar(hn[:, t, :], h[:, t, :], rstd[:, n, t:t + 1], None, ALU.mult).then_inc(n_hn, 1)

            def norm_xT(n):
                for b in range(2, 4):
                    dve.wait_ge(n_ps, 4 * n + b + 1)
                    for k in (2 * b, 2 * b + 1):
                        dve.tensor_scalar(xT[:, k, :], ps[:, b, (k % 2) * SEQ:(k % 2 + 1) * SEQ],
                                          gT[:, GAIN_AT[n] + k:GAIN_AT[n] + k + 1], None, ALU.mult).then_inc(n_xd, 1)

            norm_hn(0)
            dve.wait_ge(st_sb, 2)
            norm_xT(0)

            dve.tensor_copy(posc[:, :], posi[:, 0:NT])
            link(dve.tensor_copy(posrow, posi[:, NT:NT + SEQ]))
            for t in range(NT):
                dve.tensor_scalar(maskb[:, t, :], posrow, posc[:, t:t + 1], NEG, ALU.is_gt, ALU.mult)
                last = dve.tensor_scalar(ang[:, t, :], con[:, C_FREQ:C_FREQ + HALF_ROT], posc[:, t:t + 1], None, ALU.mult)
            link(last)
            link(dve.tensor_scalar(turns, ang, 1.0 / (2 * math.pi), 12582912.0, ALU.mult, ALU.add))
            link(dve.tensor_scalar(turns, turns, 12582912.0, None, ALU.subtract))
            for part in TWO_PI:
                link(dve.scalar_tensor_tensor(ang, turns, -part, ang, ALU.mult, ALU.add))
            link(dve.tensor_scalar(cs[:, 1], ang, math.pi - 1e-6, -(math.pi - 1e-6), ALU.min, ALU.max))
            link(dve.scalar_tensor_tensor(ang, cs[:, 1], -1.0, cs[:, 1], ALU.mult, ALU.max))
            dve.tensor_scalar(cs[:, 0], ang, -1.0, math.pi / 2, ALU.mult, ALU.add).then_inc(ang_rdy, 1)
            dve.wait_ge(lam_exp, 1)
            link(dve.scalar_tensor_tensor(nlam[:, :], lame[:, 1:2], LAM0, lame[:, 0:1], ALU.subtract, ALU.subtract))

            dve.wait_ge(cs_rdy, 1)
            for t in range(NT):
                dve.wait_ge(qkv_sb, 3 + t)
                heads = qk[:, t, :].rearrange("p (h d) -> p h d", d=DH)
                x1, x2 = heads[:, :, 0:HALF_ROT], heads[:, :, HALF_ROT:ROT]
                cos, sin = over(cs[:, 0, t, :], 16), over(cs[:, 1, t, :], 16)
                dve.tensor_tensor(rt[:, 0], x1, cos, ALU.mult)
                dve.tensor_tensor(rt[:, 1], x2, sin, ALU.mult)
                dve.tensor_tensor(rt[:, 2], x2, cos, ALU.mult)
                link(dve.tensor_tensor(rt[:, 3], x1, sin, ALU.mult))
                dve.tensor_tensor(x1, rt[:, 0], rt[:, 1], ALU.subtract)
                link(dve.tensor_tensor(x2, rt[:, 2], rt[:, 3], ALU.add))
                dve.engine_nop().then_inc(rope_done, 1)
            for m in range(2):
                dve.wait_ge(c_sb, m + 1)
                dve.wait_ge(gemm_done, DONE_AT["conv", 1, m])
                dve.tensor_tensor(upad[:, 2 * m:2 * m + 2, SC_TAPS - 1:], cT[:, 2 * m:2 * m + 2, :],
                                  ps[:, m, :].rearrange("p (c s) -> p c s", c=2), ALU.mult).then_inc(xb_used, 1)
            for b in range(2, 4):
                dve.wait_ge(qkT_ps, b + 1)
                dve.tensor_copy(qkT[:, 2 * b:2 * b + 2, :], ps[:, 4 + b, :].rearrange("p (c s) -> p c s", c=2)).then_inc(qkT_sb, 1)
            dve.wait_ge(xb_used, 2)
            for j in range(SC_TAPS):
                for m in range(4):
                    tap = gT[:, G_CW + 4 * j + m:G_CW + 4 * j + m + 1]
                    src = upad[:, m, j:j + SEQ]
                    if j == 0:
                        last = dve.tensor_scalar(mixT[:, 4 + m, :], src, tap, None, ALU.mult)
                    else:
                        last = dve.scalar_tensor_tensor(mixT[:, 4 + m, :], src, tap, mixT[:, 4 + m, :], ALU.mult, ALU.add)
                link(last)
            dve.wait_ge(gemm_done, DONE_AT["conv", 2, 1])
            for m in range(4):
                dve.tensor_tensor(mixT[:, 4 + m, :], mixT[:, 4 + m, :],
                                  ps[:, 2 + m // 2, (m % 2) * SEQ:(m % 2 + 1) * SEQ], ALU.mult).then_inc(mix_conv, 1)

            def masked(hd):
                dve.wait_ge(sc_ps, hd + 1)
                for m in range(2):
                    dve.tensor_tensor(sm[:, hd % 2, 2 * m:2 * m + 2, :], ps[:, 2 * (hd % 2) + m, :].rearrange(
                        "p (t s) -> p t s", t=NT), maskb, ALU.add).then_inc(sm_read, 1)
                dve.wait_ge(sm_read, 2 * (hd + 1))
                link(dve.tensor_reduce(mx[:, hd % 2, :], sm[:, hd % 2], AX, ALU.max))
                dve.tensor_scalar(nb[:, hd % 2, :], mx[:, hd % 2, :], -(DH ** -0.5), None, ALU.mult).then_inc(sm_rdy, 1)

            masked(0)
            for hd in range(HEADS_A):
                if hd + 1 < HEADS_A:
                    masked(hd + 1)
                u = hd % 2
                dve.wait_ge(ex_done, hd + 1)
                link(dve.reciprocal(erc[:, u, :], esum[:, u, :]))
                link(dve.tensor_scalar(erc[:, u, 2:4], erc[:, u, 2:4], nlam[:, 0:1], None, ALU.mult))
                if hd >= 2:
                    dve.wait_ge(aT_ps, hd - 1)
                for t in range(NT):
                    last = dve.tensor_scalar(adf[:, u, t, :], sm[:, u, t, :], erc[:, u, t:t + 1], None, ALU.mult)
                link(last)
                for t in range(NT):
                    last = dve.scalar_tensor_tensor(adf[:, u, t, :], sm[:, u, 2 + t, :], erc[:, u, 2 + t:3 + t],
                                                    adf[:, u, t, :], ALU.mult, ALU.add)
                last.then_inc(a_done, 1)
                dve.wait_ge(a_done, hd + 1)
                if hd >= 1:
                    dve.wait_ge(av_ps, hd)
                    dve.tensor_copy(oat[:, :, hd - 1, :], ps[:, 6 + (hd - 1) % 2, 0:SEQ].rearrange(
                        "p (t v) -> p t v", t=NT)).then_inc(o_sb, 1)
            dve.wait_ge(av_ps, HEADS_A)
            dve.tensor_copy(oat[:, :, HEADS_A - 1, :], ps[:, 6 + (HEADS_A - 1) % 2, 0:SEQ].rearrange(
                "p (t v) -> p t v", t=NT)).then_inc(o_sb, 1)
            dve.wait_ge(o_sb, HEADS_A)
            o3 = oat.rearrange("p t h v -> p (t h) v")
            q3 = osq.rearrange("p t h v -> p (t h) v")
            link(dve.tensor_tensor(q3, o3, o3, ALU.mult))
            dve.tensor_reduce(oss[:, 0:8], q3, AX, ALU.add).then_inc(o_ss, 1)
            dve.wait_ge(o_sd, 1)
            link(dve.reciprocal(ors[:, 0:8], osd[:, 0:8]))
            dve.tensor_tensor(o3, o3, along(ors[:, 0:8], P), ALU.mult).then_inc(o_nrm, 1)

            def add_h(t, half, src):
                piece = h[:, t, half * 512:(half + 1) * 512]
                return dve.tensor_tensor(piece, piece, src, ALU.add)

            for j in range(2):
                for t in range(NT):
                    dve.wait_ge(gemm_done, DONE_AT["out_e", j, t])
                    add_h(t, j, ps[:, 2 * j + t, :]).then_inc(h_ready, 1)

            dve.wait_ge(h_ready, H_AT[1])
            norm_hn(1)
            norm_xT(1)
            for j in range(FJ):
                for t in range(NT):
                    dve.wait_ge(gemm_done, DONE_AT["h3", j, t])
                    dve.wait_ge(silu_sb, 2 * j + t + 1)
                    dve.tensor_tensor(gated[:, t, :], sil[:, t, :], ps[:, 2 * t + 1, :], ALU.mult).then_inc(gated_sb, 1)
            for t in range(NT):
                dve.wait_ge(gemm_done, DONE_AT["y", FJ - 1, t])
                for half in range(2):
                    add_h(t, half, ps[:, 4 + 2 * t + half, :]).then_inc(h_ready, 1)

            def embed(i, product_wait):
                for j in range(2):
                    for t in range(NT):
                        product_wait(("proj", j, t))
                        dve.wait_ge(sgm_sb, 4 * i + 2 * j + t + 1)
                        link(dve.tensor_tensor(ptmp[:, t, :], sgm[:, t, j * 512:(j + 1) * 512],
                                               ps[:, 4 + 2 * j + t, :], ALU.mult))
                        add_h(t, j, ptmp[:, t, :]).then_inc(h_ready, 1)

            dve.wait_ge(h_ready, H_AT[2])
            norm_hn(2)
            norm_xT(2)
            embed(0, lambda what: dve.wait_ge(gemm_done, DONE_AT[what]))

            dve.wait_ge(h_ready, H_AT[3])
            norm_hn(3)
            norm_xT(3)
            dve.memset(upo[:, :, :, 0:DN_TAPS - 1], 0.0).then_inc(pad_zero, 1)
            dve.wait_ge(ba_ps, 1)
            link(dve.tensor_copy(ba[:, :, :], ps[:, 7, 0:32].rearrange("p (t n) -> p t n", t=NT)))
            link(dve.tensor_tensor(ba[:, :, 8:16], ba[:, :, 8:16], over(dtb[:, :], NT), ALU.add))
            dve.tensor_scalar(yneg[:, :, 0:8], ba[:, :, 0:8], -1.0, None, ALU.mult)
            dve.scalar_tensor_tensor(yneg[:, :, 8:16], ba[:, :, 8:16], -1.0, ba[:, :, 8:16], ALU.mult, ALU.min).then_inc(ba_neg, 1)
            dve.wait_ge(ba_ln, 1)
            link(dve.tensor_scalar(yexp[:, :, 0:8], yexp[:, :, 0:8], 1.0, None, ALU.add))
            dve.reciprocal(beta[:, :, :], yexp[:, :, 0:8])
            link(dve.scalar_tensor_tensor(gdec[:, :, :], ba[:, :, 8:16], 0.0, yln[:, :, :], ALU.max, ALU.add))
            dve.scalar_tensor_tensor(gdec[:, :, :], gdec[:, :, :], -1.0, over(ealog[:, :], NT), ALU.mult, ALU.mult).then_inc(g_rdy, 1)

            def conv(n):
                for m in range(2):
                    dve.wait_ge(q_pad, 2 * n + m + 1)
                for j in range(DN_TAPS):
                    for m in range(4):
                        ch = 4 * n + m
                        tap = cwT[:, j * QKV_CHUNKS + ch:j * QKV_CHUNKS + ch + 1]
                        src = upo[:, n % 2, m, j:j + SEQ]
                        if j == 0:
                            last = dve.tensor_scalar(qkvT[:, ch, :], src, tap, None, ALU.mult)
                        else:
                            last = dve.scalar_tensor_tensor(qkvT[:, ch, :], src, tap, qkvT[:, ch, :], ALU.mult, ALU.add)
                    if j < DN_TAPS - 1:
                        link(last)
                last.then_inc(cv_done, 1)

            for n in range(6):
                conv(n)
            dve.wait_ge(cum_ps, 1)
            link(dve.tensor_copy(cum[:, :, :, :], ps[:, 6, 0:32].rearrange("p (t k n) -> p t k n", t=NT, k=2)))
            dve.tensor_copy(dcy[:, :, 0, :], cum[:, :, 0, :])
            dve.tensor_tensor(dcy[:, :, 1, :], cum[:, :, 1, :], cum[:, :, 0, :], ALU.subtract).then_inc(cum_sb, 1)
            dve.wait_ge(cum_sb, 1)
            dve.wait_ge(dcy_rdy, 1)
            link(dve.tensor_tensor(bec[:, :, :], beta[:, :, :], dcy[:, :, 0, :], ALU.mult))
            for g in range(8):
                dve.wait_ge(l2_sd, g + 1)
                norms = pm[:, g % 2].rearrange("p a b -> p (a b)")
                link(dve.reciprocal(norms, norms))
                pair = qkvT[:, 2 * g:2 * g + 2, :].rearrange("p a b -> p (a b)")
                dve.scalar_tensor_tensor(pair, pair, P ** -0.5 if g < 4 else 1.0, norms, ALU.mult, ALU.mult).then_inc(l2_done, 1)
            for t in range(NT):
                for b in range(2):
                    dve.wait_ge(kv_ps, 4 * t + 2 + b + 1)
                    dve.tensor_tensor(vb[:, t, 4 * b:4 * b + 4, :], ps[:, 4 * t + 2 + b, :].rearrange(
                        "p (c s) -> p c s", c=4), along(beta[:, t, 4 * b:4 * b + 4], P), ALU.mult).then_inc(vb_sb, 1)
            dve.wait_ge(kv_ps, 8)
            for t in range(NT):
                tok = slice(t * P, (t + 1) * P)
                u = 2 * t
                for g in range(2):
                    dve.wait_ge(rc_ps, u + g + 1)
                    for c in range(4):
                        hd = 4 * g + c
                        last = dve.tensor_scalar(AT[:, t, hd, :], ps[:, g, c * P:(c + 1) * P],
                                                 cum[:, t, 0, hd:hd + 1], 0.0, ALU.subtract, ALU.min)
                    last.then_inc(dd_rdy, 1)
                    dve.wait_ge(br_ps, u + g + 1)
                    if t == 0:
                        dve.wait_ge(l2_done, 8)
                    else:
                        dve.wait_ge(x_ps, 12)
                    dve.tensor_tensor(pm[:, g], kT[:, 4 * g:4 * g + 4, tok], ps[:, 2 + g, :].rearrange(
                        "p (c s) -> p c s", c=4), ALU.mult).then_inc(kb_rdy, 1)
                for g in range(2):
                    heads = slice(4 * g, 4 * g + 4)
                    dve.wait_ge(dec_exp, u + g + 1)
                    link(dve.tensor_tensor(AT[:, t, heads, :], AT[:, t, heads, :], over(upper, 4), ALU.mult))
                    dve.wait_ge(lt_ps, u + g + 1)
                    dve.tensor_tensor(LT[:, heads, :], ps[:, 4 + g, :].rearrange("p (c s) -> p c s", c=4),
                                      AT[:, t, heads, :], ALU.mult).then_inc(lt_sb, 1)
                    dve.wait_ge(at_ps, u + g + 1)
                    dve.wait_ge(lt_sb, u + g + 1)
                    dve.tensor_tensor(AT[:, t, heads, :], ps[:, 6 + g, :].rearrange("p (c s) -> p c s", c=4),
                                      AT[:, t, heads, :], ALU.mult).then_inc(at_sb, 1)
                for g in range(2):
                    dve.wait_ge(bt_rdy, LEVELS * u + g + 1)
                    dve.tensor_tensor(XT[:, t, 4 * g:4 * g + 4, :], over(ident, 4), bt[:, g], ALU.subtract).then_inc(x1_rdy, 1)
                for l in range(1, LEVELS):
                    for g in range(2):
                        heads = slice(4 * g, 4 * g + 4)
                        v = (LEVELS - 1) * u + 2 * (l - 1) + g
                        dve.wait_ge(x_ps, v + 1)
                        if l == 1:
                            dve.wait_ge(x1_rdy, u + g + 1)
                        else:
                            dve.wait_ge(x_sb, v - 1)
                        if l < LEVELS - 1:
                            dve.wait_ge(x1_sb, u + g + 1)
                            dve.tensor_tensor(X[:, heads, :], X[:, heads, :], ps[:, 4 + g, :].rearrange(
                                "p (c s) -> p c s", c=4), ALU.subtract)
                        dve.tensor_tensor(XT[:, t, heads, :], XT[:, t, heads, :], ps[:, 6 + g, :].rearrange(
                            "p (c s) -> p c s", c=4), ALU.subtract).then_inc(x_sb, 1)
                dve.wait_ge(p_ps, (LEVELS - 1) * (u + 2))
                scale = dcy[:, 0, 1, :] if t == 0 else bec[:, 1, :]
                dve.wait_ge(k_sb, 4)
                dve.tensor_tensor(kbe, ktok[:, t], along(scale, P), ALU.mult).then_inc(ksc_rdy, 1)
                if t == 1:
                    for g in range(2):
                        dve.wait_ge(qg_exp, g + 1)
                        dve.tensor_tensor(qgT[:, 4 * g:4 * g + 4, :], qgT[:, 4 * g:4 * g + 4, :],
                                          qT[:, 4 * g:4 * g + 4, tok], ALU.mult).then_inc(qg_rdy, 1)
                for g in range(2):
                    dve.wait_ge(od_ps, u + g + 1)
                    dve.tensor_copy(AT[:, t, 4 * g:4 * g + 4, :], ps[:, (2 if t == 0 else 4) + g, :].rearrange(
                        "p (c s) -> p c s", c=4)).then_inc(od_sb, 1)
            for t in range(NT):
                dve.wait_ge(od_ss, t + 1)
                last = dve.tensor_reduce(oss[:, 8 * t:8 * t + 8], odq[:, t], AX, ALU.add)
            last.then_inc(od_sd, 1)
            dve.wait_ge(od_sd, 2)
            link(dve.reciprocal(ors[:, :], osd[:, :]))
            for t in range(NT):
                dve.tensor_tensor(AT[:, t], AT[:, t], along(ors[:, 8 * t:8 * t + 8], P), ALU.mult).then_inc(dve_link, 1)
                count[0] += 1
            dve.wait_ge(dve_link, count[0])
            for t in range(NT):
                dve.tensor_tensor(AT[:, t], AT[:, t], zs[:, t, :].rearrange("p (h d) -> p h d", d=P), ALU.mult).then_inc(od_nrm, 1)
            for j in range(2):
                for t in range(NT):
                    dve.wait_ge(gemm_done, DONE_AT["out_o", j, t])
                    add_h(t, j, ps[:, 4 + 2 * j + t, :]).then_inc(h_ready, 1)

            dve.wait_ge(h_ready, H_AT[4])
            norm_hn(4)
            norm_xT(4)
            dve.wait_ge(lg_ps, 1)
            link(dve.tensor_copy(r_l, ps[:, 4, 0:NT * NE].rearrange("p (t e) -> p t e", t=NT)))
            link(dve.tensor_reduce(r_mx, r_l, AX, ALU.max))
            dve.tensor_scalar(r_nmx, r_mx, -1.0, None, ALU.mult).then_inc(lg_max, 1)
            for t in range(NT):
                other, own = over(r_l[:, t, :], NE), along(r_l[:, t, :], NE)
                dve.tensor_tensor(r_gt[:, t, :].rearrange("p (e f) -> p e f", e=NE), other, own, ALU.is_gt)
                last = dve.tensor_tensor(r_eq[:, t, :].rearrange("p (e f) -> p e f", e=NE), other, own, ALU.is_equal)
            link(last)
            link(dve.tensor_tensor(r_eq, r_eq, over(con[:, C_LOW:C_LOW + NE * NE], NT), ALU.mult))
            link(dve.tensor_tensor(r_gt, r_gt, r_eq, ALU.add))
            link(dve.tensor_reduce(r_rank, r_gt.rearrange("p t (e f) -> p t e f", e=NE), AX, ALU.add))
            dve.tensor_scalar(r_m, r_rank, 1.5, None, ALU.is_lt).then_inc(mk_rdy, 1)
            dve.wait_ge(mk_rdy, 1)
            dve.wait_ge(lg_exp, 1)
            link(dve.tensor_tensor(r_e, r_e, r_m, ALU.mult))
            link(dve.tensor_reduce(r_s, r_e, AX, ALU.add))
            link(dve.reciprocal(r_rs, r_s))
            dve.memset(posb[:, :, :], -1.0)
            dve.memset(gateb[:, :, :], 0.0)
            link(dve.memset(blk_f, 0.0))
            link(dve.tensor_tensor(gateb[:, :, 0:NE], r_e, along(r_rs, NE), ALU.mult))
            dve.wait_ge(rk_ps, 1)
            dve.tensor_scalar(r_ov, ps[:, 5, 2 * NE:3 * NE], float(P) + 0.5, None, ALU.is_gt)
            link(dve.tensor_tensor(r_im, ps[:, 5, 0:NT * NE].rearrange("p (t e) -> p t e", t=NT), r_m, ALU.mult))
            dve.tensor_scalar(posb[:, :, 0:NE], r_im, -1.0, None, ALU.add)
            w3 = r_w.rearrange("p (e f) -> p e f", e=NE)
            link(dve.tensor_tensor(w3, con[:, C_LOW:C_LOW + NE * NE].rearrange("p (e f) -> p e f", e=NE),
                                   over(r_ov, NE), ALU.mult))
            link(dve.tensor_reduce(r_ord, w3, AX, ALU.add))
            for i in range(MAX_OVER):
                last = dve.tensor_scalar(r_sl[:, i, :], r_ord, float(i), None, ALU.is_equal)
            link(last)
            link(dve.tensor_tensor(r_sl, r_sl, over(r_ov, MAX_OVER), ALU.mult))
            for t in range(NT):
                last = dve.tensor_tensor(r_t[:, t], r_sl, over(r_im[:, t, :], MAX_OVER), ALU.mult)
            link(last)
            link(dve.tensor_reduce(posb[:, :, NE:NE + MAX_OVER], r_t, AX, ALU.add))
            link(dve.tensor_scalar(posb[:, :, NE:NE + MAX_OVER], posb[:, :, NE:NE + MAX_OVER], -1.0 - P, None, ALU.add))
            for t in range(NT):
                last = dve.tensor_tensor(r_t[:, t], r_sl, over(gateb[:, t, 0:NE], MAX_OVER), ALU.mult)
            link(last)
            link(dve.tensor_reduce(gateb[:, :, NE:NE + MAX_OVER], r_t, AX, ALU.add))
            link(dve.tensor_tensor(r_sl, r_sl, over(con[:, C_EID:C_EID + NE], MAX_OVER), ALU.mult))
            dve.tensor_reduce(blk_f[:, NE:NE + MAX_OVER], r_sl, AX, ALU.add)
            dve.tensor_copy(blk_f[:, 0:NE], con[:, C_EID:C_EID + NE])
            link(dve.tensor_reduce(blk_f[:, 15:16], r_ov, AX, ALU.add))
            link(dve.tensor_scalar(blk_f[:, 15:16], blk_f[:, 15:16], float(NE), None, ALU.add))
            dve.tensor_copy(blk_i[:, :], blk_f).then_inc(tab_rdy, 1)
            dve.wait_ge(tab_rdy, 1)
            nblk = dve.value_load(blk_i[0:1, 15:16], min_val=NE, max_val=NE + MAX_OVER)

            def select(b):
                for t in range(NT):
                    dve.tensor_scalar(sel[:, t, :], iota, posb[:, t, bass.ds(b, 1)], None, ALU.is_equal)
                    last = dve.tensor_scalar(selg[:, t, :], iota, posb[:, t, bass.ds(b, 1)], gateb[:, t, bass.ds(b, 1)],
                                             ALU.is_equal, ALU.mult)
                last.then_inc(m_sel, 1)

            def gathered(done):
                for q in range(2):
                    dve.wait_ge(m_xg_ps, done + (q + 1))
                    at = GAIN_AT[4] + 4 * q
                    dve.tensor_tensor(xg[:, 4 * q:4 * q + 4, :], ps[:, 6 + q, :].rearrange("p (c s) -> p c s", c=4),
                                      along(gT[:, at:at + 4], P), ALU.mult).then_inc(m_xg, 1)

            select(0)
            gathered(0)
            dve.engine_nop().then_inc(m_add, 1)
            with dve.Fori(0, nblk) as b:
                for j in range(FJ):
                    dve.wait_ge(gemm_done, b * PER_BLOCK + (G_MOE + MOE_AT[1, j] + 1))
                    dve.wait_ge(m_silu, b * FJ + (j + 1))
                    dve.tensor_tensor(gated[:, j % 2, :], sil[:, j % 2, :], ps[:, 2 * (j % 2) + 1, :],
                                      ALU.mult).then_inc(m_gated, 1)
                    if j == 0:
                        dve.wait_ge(m_sT_ps, b + 1)
                        select(b + 1)
                gathered(b * 2 + 2)
                for t in range(NT):
                    for half in range(2):
                        dve.wait_ge(m_sc, b * 4 + (2 * t + half + 1))
                        add_h(t, half, ps[:, 2 + 4 * t + half, :]).then_inc(m_add, 1)

            dve.wait_ge(m_add, nblk * 4 + 1)
            norm_hn(5)
            norm_xT(5)
            embed(1, lambda what: dve.wait_ge(gemm_done, nblk * PER_BLOCK + (G_MOE + TAIL[what])))

            dve.wait_ge(h_ready, H_AT[6])
            dve.wait_ge(n_std, 7)
            link(dve.reciprocal(rstd[:, 6, :], std[:, 6, :]))
            dve.wait_ge(gfin_in, 16)
            for t in range(NT):
                dve.scalar_tensor_tensor(hn[:, t, :], h[:, t, :], rstd[:, 6, t:t + 1], gfin, ALU.mult, ALU.mult).then_inc(f_out, 1)


_INS = ["x", "p", "positions", "ln_mix", "ln_ffn", "ln_ple", "ln_final", "w_in_even", "w_out_even",
        "lam_q1", "lam_k1", "lam_q2", "lam_k2", "subln_gain", "conv_w_short", "w_in_odd", "conv_w_qkv",
        "a_log", "dt_bias", "onorm_gain", "w_out_odd", "w1_dense", "w3_dense", "w2_dense",
        "w_router", "w1_moe", "w3_moe", "w2_moe", "w_ple_gate", "w_ple_proj"]


def kernel(**inputs):
    import concourse.bacc as bacc
    from concourse.bass_utils import run_bass_kernel_spmd

    nc = bacc.Bacc("TRN2", target_bir_lowering=False, num_devices=1)
    arrays, aps = {}, {}
    for name in _INS + ["con"]:
        v = shape_constants() if name == "con" else np.ascontiguousarray(inputs[name])
        arrays[f"in_{name}"] = v
        aps[name] = nc.dram_tensor(f"in_{name}", v.shape, mybir.dt.from_np(v.dtype), kind="ExternalInput").ap()
    out = nc.dram_tensor("out", (1, SEQ, D), F32, kind="ExternalOutput").ap()
    trunk(nc, aps, out)
    r = run_bass_kernel_spmd(nc, [arrays], core_ids=[0])
    return r.results[0]["out"]
```

```python
import math
from contextlib import ExitStack

import numpy as np

import concourse.bass as bass
from concourse import mybir

F32 = mybir.dt.float32
F32R = mybir.dt.float32r
I32 = mybir.dt.int32
ALU = mybir.AluOpType
ACT = mybir.ActivationFunctionType
AX = mybir.AxisListType.X

P = 128
SEQ = 256
D = 1024
NT = SEQ // P
KC = D // P
RMS_EPS = 1e-6
SUBLN_EPS = 1e-5
L2_EPS = 1e-6
HEADS_A = 4
DH = 64
ROT = 16
HALF_ROT = ROT // 2
ROPE_THETA = 500000.0
LAM0 = 0.8 - 0.6 * math.exp(0.0)
SC_TAPS = 3
DN_TAPS = 4
HEADS_D = 8
QKV_CHUNKS = 3 * HEADS_D
FF = 3584
FJ = FF // 512
NE = 8
MAX_OVER = 3
HALF_FJ = 2 * FJ
PIECE = 2048
RAW = 6
SPLIT = 3
PER_BLOCK = 6 * FJ
PLE = 256
NEG = -1.0e30
TWO_PI = (6.28125, 0.0019350051879882812, 2 * math.pi - 6.28125 - 0.0019350051879882812)
N_SETUP = 16 * 17
LEVELS = 7

C_ID, C_UP, C_ONE, C_IOTA, C_LEV = 0, 128, 256, 384, 512
C_FREQ = C_LEV + LEVELS * 128
C_EID = C_FREQ + HALF_ROT
C_LOW = C_EID + NE
C_W = C_LOW + NE * NE

P_QKV_E = 0
P_CONV_E = P_QKV_E + 6
P_OUT_E = P_CONV_E + 6
P_MLP = P_OUT_E + 4
P_GATE_E = P_MLP + 3 * HALF_FJ
P_PROJ_E = P_GATE_E + 4
P_QKV_O = P_PROJ_E + 2
P_Z = P_QKV_O + 12
P_OUT_O = P_Z + 4
P_MOE = P_OUT_O + 4
for ring in (RAW, SPLIT):
    assert P_MOE % ring == 0 and PER_BLOCK % ring == 0


def shape_constants():
    c = np.zeros((P, C_W), np.float32)
    i = np.arange(P)
    c[:, C_ID:C_ID + P] = np.eye(P)
    c[:, C_UP:C_UP + P] = i[:, None] <= i[None, :]
    c[:, C_ONE:C_ONE + P] = 1.0
    c[:, C_IOTA:C_IOTA + P] = i[None, :]
    for level in range(LEVELS):
        s = 1 << level
        rows, cols = i[:, None] // s, i[None, :] // s
        c[:, C_LEV + level * P:C_LEV + (level + 1) * P] = (cols % 2 == 1) & (rows == cols - 1)
    c[:, C_FREQ:C_FREQ + HALF_ROT] = np.float32(ROPE_THETA) ** (
        -np.arange(0, ROT, 2, dtype=np.float32) / np.float32(ROT))
    e = np.arange(NE)
    c[:, C_EID:C_EID + NE] = e
    c[:, C_LOW:C_LOW + NE * NE] = (e[None, :] < e[:, None]).reshape(-1)
    return c


def up_down_order(steps):
    order = [(0, 0), (1, 0)]
    for j in range(1, steps):
        order += [(0, j), (1, j), (2, j - 1)]
    return order + [(2, steps - 1)]


MLP_ORDER = up_down_order(HALF_FJ)
MLP_AT = {key: P_MLP + i for i, key in enumerate(MLP_ORDER)}
MOE_ORDER = [(m, j, part) for m, j in up_down_order(FJ) for part in range(2)]
MOE_AT = {key: i for i, key in enumerate(MOE_ORDER)}


def trunk(nc, a, out):
    ctx = ExitStack()
    with ctx:
        def sb(name, shape, dt=F32):
            return ctx.enter_context(nc.sbuf_tensor(name, shape, dt))

        def sem(name):
            return ctx.enter_context(nc.semaphore(name))

        raw = sb("raw", [P, RAW, PIECE])
        w_hi = sb("w_hi", [P, SPLIT, PIECE], F32R)
        w_lo = sb("w_lo", [P, SPLIT, PIECE], F32R)
        x_hi = sb("x_hi", [P, KC * SEQ], F32R)
        x_lo = sb("x_lo", [P, KC * SEQ], F32R)
        h = sb("h", [P, NT, D])
        hn = sb("hn", [P, NT, D])
        con = sb("con", [P, C_W])
        wba = sb("wba", [P, KC, 2 * HEADS_D])
        wrt = sb("wrt", [P, KC, NE])
        wba_hi = sb("wba_hi", [P, KC, 2 * HEADS_D], F32R)
        wba_lo = sb("wba_lo", [P, KC, 2 * HEADS_D], F32R)
        wrt_hi = sb("wrt_hi", [P, KC, NE], F32R)
        wrt_lo = sb("wrt_lo", [P, KC, NE], F32R)
        gT = sb("gT", [P, 62])
        cwT = sb("cwT", [P, DN_TAPS * QKV_CHUNKS])
        alog = sb("alog", [P, HEADS_D])
        dtb = sb("dtb", [P, HEADS_D])
        ssq = sb("ssq", [P, 7, NT])
        std = sb("std", [P, 7, NT])
        rstd = sb("rstd", [P, 7, NT])
        eps6 = sb("eps6", [P, 1])
        eps5 = sb("eps5", [P, 1])
        posi = sb("posi", [P, NT + SEQ], I32)
        posc = sb("posc", [P, NT])
        cs = sb("cs", [P, 2, NT, HALF_ROT])
        lamd = sb("lamd", [P, 2])
        lame = sb("lame", [P, 2])
        nlam = sb("nlam", [P, 1])
        mx = sb("mx", [P, 2, 4])
        nb = sb("nb", [P, 2, 4])
        esum = sb("esum", [P, 2, 4])
        erc = sb("erc", [P, 2, 4])
        oss = sb("oss", [P, NT * HEADS_D])
        osd = sb("osd", [P, NT * HEADS_D])
        ors = sb("ors", [P, NT * HEADS_D])
        ba = sb("ba", [P, NT, 2 * HEADS_D])
        yneg = sb("yneg", [P, NT, 2 * HEADS_D])
        yexp = sb("yexp", [P, NT, 2 * HEADS_D])
        yln = sb("yln", [P, NT, HEADS_D])
        beta = sb("beta", [P, NT, HEADS_D])
        gdec = sb("gdec", [P, NT, HEADS_D])
        cum = sb("cum", [P, NT, 2, HEADS_D])
        dcy = sb("dcy", [P, NT, 2, HEADS_D])
        bec = sb("bec", [P, NT, HEADS_D])
        ealog = sb("ealog", [P, HEADS_D])
        NBC = NE + MAX_OVER + 1
        posb = sb("posb", [P, NT, NBC])
        gateb = sb("gateb", [P, NT, NBC])
        blk_i = sb("blk_i", [P, 16], I32)
        ps = ctx.enter_context(nc.psum_tensor("ps", [P, 8, 512], F32))

        def by_chunk(x, n=SEQ):
            return x[:, 0:KC * n].rearrange("p (k s) -> p k s", k=KC)

        xs_hi, xs_lo = by_chunk(x_hi), by_chunk(x_lo)
        ident = con[:, C_ID:C_ID + P]
        upper = con[:, C_UP:C_UP + P]
        ones = con[:, C_ONE:C_ONE + P]
        iota = con[:, C_IOTA:C_IOTA + P]

        def over(ap, n):
            return ap.unsqueeze(1).broadcast_to([P, n, ap.shape[-1]])

        def along(ap, n):
            return ap.unsqueeze(2).broadcast_to([P, ap.shape[-1], n])

        def level_mask(l):
            return con[:, C_LEV + l * P:C_LEV + (l + 1) * P]

        class Area:

            def __init__(self, name):
                self.name, self.n, self.held = name, 0, ExitStack()

            def take(self, *dims, dt=F32):
                self.n += 1
                size = int(np.prod(dims))
                v = self.held.enter_context(nc.sbuf_tensor(f"{self.name}{self.n}", [P, size], dt))[:, :]
                if len(dims) == 1:
                    return v
                names = "abcd"[:len(dims)]
                return v.rearrange(f"p ({' '.join(names)}) -> p {' '.join(names)}",
                                   **dict(zip(names[1:], dims[1:])))

            def close(self):
                self.held.close()

        G_MIX, G_FFN, G_PLE, G_SUB, G_ON, G_CW = 0, 16, 32, 48, 49, 50
        GAIN_AT = [G_MIX, G_FFN, G_PLE, G_MIX + KC, G_FFN + KC, G_PLE + KC]

        ar = Area("even")
        qk = ar.take(NT, 1024)
        vt = ar.take(NT, 512)
        qkT = ar.take(KC, SEQ)
        mix_c = ar.take(4, SEQ)
        cT = ar.take(4, SEQ)
        PADS = SC_TAPS - 1 + SEQ
        upad = ar.take(4, PADS)
        rt = ar.take(4, 16, HALF_ROT)
        sm = ar.take(2, 4, SEQ)
        adf = ar.take(2, NT, SEQ)
        maskb = ar.take(NT, SEQ)
        rows1 = ar.take(P)
        rows2 = ar.take(P)
        posrow = ar.take(SEQ)
        lamv = ar.take(4, DH)
        lamp = ar.take(2, DH)
        ang = ar.take(NT, HALF_ROT)
        turns = ar.take(NT, HALF_ROT)
        oat = qk[:, 0, :].rearrange("p (t h v) -> p t h v", t=NT, h=HEADS_A)
        osq = qk[:, 1, :].rearrange("p (t h v) -> p t h v", t=NT, h=HEADS_A)
        aTt = cT.rearrange("p (u k) s -> p u k s", u=2)
        ar.close()

        ar = Area("ff")
        sil = ar.take(2, 512)
        gated = ar.take(2, 512)
        g_hi = ar.take(2, 512, dt=F32R)
        g_lo = ar.take(2, 512, dt=F32R)
        sgm = ar.take(NT, D)
        ptmp = ar.take(2, 512)
        p_tok = ar.take(NT, PLE)
        p_hi = ar.take(2, SEQ, dt=F32R)
        p_lo = ar.take(2, SEQ, dt=F32R)
        gfin = ar.take(D)
        gffn = ar.take(D)
        xg_hi, xg_lo = by_chunk(x_hi, P), by_chunk(x_lo, P)
        ysb = ar.take(D)
        sel = ar.take(NT, P)
        selg = ar.take(NT, P)
        selgT = ar.take(SEQ)
        r_l = ar.take(NT, NE)
        r_gt = ar.take(NT, NE * NE)
        r_eq = ar.take(NT, NE * NE)
        r_rank = ar.take(NT, NE)
        r_m = ar.take(NT, NE)
        r_mx = ar.take(NT)
        r_nmx = ar.take(NT)
        r_e = ar.take(NT, NE)
        r_s = ar.take(NT)
        r_rs = ar.take(NT)
        r_im = ar.take(NT, NE)
        r_cnt = ar.take(NE)
        r_ov = ar.take(NE)
        r_w = ar.take(NE * NE)
        r_ord = ar.take(NE)
        r_sl = ar.take(MAX_OVER, NE)
        r_t = ar.take(NT, MAX_OVER, NE)
        blk_f = ar.take(16)
        ar.close()

        ar = Area("odd")
        qkvT = ar.take(QKV_CHUNKS, SEQ)
        PADW = DN_TAPS - 1 + SEQ
        upo_flat = ar.take(2 * 4 * PADW)
        upo = upo_flat.rearrange("p (a b c) -> p a b c", a=2, b=4)
        LT = ar.take(HEADS_D, P)
        X = ar.take(HEADS_D, P)
        XT = ar.take(NT, HEADS_D, P)
        bt = ar.take(2, 4, P)
        pm = ar.take(2, 4, P)
        S1 = ar.take(HEADS_D, P)
        vb = ar.take(NT, HEADS_D, P)
        ar.close()
        qT, kT = qkvT[:, 0:8, :], qkvT[:, 8:16, :]
        by_tok = dict(t=NT, h=HEADS_D)
        ktok = upo_flat[:, 0:NT * D].rearrange("p (t h d) -> p t h d", **by_tok)
        AT = qkvT[:, 16:24, :].rearrange("p a b -> p (a b)").rearrange("p (t h d) -> p t h d", **by_tok)
        odq = qkvT[:, 0:8, :].rearrange("p a b -> p (a b)").rearrange("p (t h d) -> p t h d", **by_tok)
        un = bt.rearrange("p a b c -> p (a b) c")
        qgT = pm.rearrange("p a b c -> p (a b) c")
        nwT, kbe, zs = LT, X, hn

        raw_in = [sem(f"raw_in{i}") for i in range(RAW)]
        hi_rdy, lo_rdy = sem("hi_rdy"), sem("lo_rdy")
        piece_used = sem("piece_used")
        small_hi, small_lo = sem("small_hi"), sem("small_lo")
        mix_hi, mix_lo = sem("mix_hi"), sem("mix_lo")
        x_in, con_in, setup_in, out_done = sem("x_in"), sem("con_in"), sem("setup_in"), sem("out_done")
        p_in, gfin_in = sem("p_in"), sem("gfin_in")
        dve_link, act_link, pool_link = sem("dve_link"), sem("act_link"), sem("pool_link")
        h_ready = sem("h_ready")
        n_std, n_hn, n_ps, n_hi, n_lo = (sem(x) for x in ("n_std", "n_hn", "n_ps", "n_hi", "n_lo"))
        eps_set, st_ps, st_sb = sem("eps_set"), sem("st_ps"), sem("st_sb")
        ang_rdy, cs_rdy, lam_dot, lam_exp = sem("ang_rdy"), sem("cs_rdy"), sem("lam_dot"), sem("lam_exp")
        qkv_sb, v_sb, c_sb, xb_used, rope_done, mix_conv = (sem(x) for x in (
            "qkv_sb", "v_sb", "c_sb", "xb_used", "rope_done", "mix_conv"))
        qkT_ps, qkT_sb = sem("qkT_ps"), sem("qkT_sb")
        sc_ps, sm_read, sm_rdy, ex_done, a_done = (sem(x) for x in (
            "sc_ps", "sm_read", "sm_rdy", "ex_done", "a_done"))
        aT_ps, aT_sb, av_ps, o_sb, o_ss, o_sd, o_nrm, oT_ps = (sem(x) for x in (
            "aT_ps", "aT_sb", "av_ps", "o_sb", "o_ss", "o_sd", "o_nrm", "oT_ps"))
        silu_sb, gated_sb, gated_hi, gated_lo = sem("silu_sb"), sem("gated_sb"), sem("gated_hi"), sem("gated_lo")
        pT_ps, pT_hi, pT_lo, sgm_sb = sem("pT_ps"), sem("pT_hi"), sem("pT_lo"), sem("sgm_sb")
        ba_ps, ba_neg, ba_exp, ba_ln, g_rdy, cum_ps, cum_sb, dcy_rdy = (sem(x) for x in (
            "ba_ps", "ba_neg", "ba_exp", "ba_ln", "g_rdy", "cum_ps", "cum_sb", "dcy_rdy"))
        q_pad, cv_done, cv_silu, z_sb, pad_zero = (sem(x) for x in (
            "q_pad", "cv_done", "cv_silu", "z_sb", "pad_zero"))
        l2_sq, l2_ps, l2_sd, l2_done = sem("l2_sq"), sem("l2_ps"), sem("l2_sd"), sem("l2_done")
        kv_ps, k_sb, vb_sb = sem("kv_ps"), sem("k_sb"), sem("vb_sb")
        rc_ps, dd_rdy, dec_exp, dec_rdy, br_ps, kb_rdy, lt_ps, lt_sb, at_ps, at_sb = (sem(x) for x in (
            "rc_ps", "dd_rdy", "dec_exp", "dec_rdy", "br_ps", "kb_rdy", "lt_ps", "lt_sb", "at_ps", "at_sb"))
        bt_rdy, x1_rdy, x1_ps, x1_sb, p_ps, p_sb, x_ps, x_sb = (sem(x) for x in (
            "bt_rdy", "x1_rdy", "x1_ps", "x1_sb", "p_ps", "p_sb", "x_ps", "x_sb"))
        ksc_rdy, w_ps, w_sb, u_ps, u_sb, od_ps, od_sb, s_ps, s_sb, qg_ps, qg_exp, qg_rdy = (
            sem(x) for x in ("ksc_rdy", "w_ps", "w_sb", "u_ps", "u_sb", "od_ps", "od_sb", "s_ps",
                             "s_sb", "qg_ps", "qg_exp", "qg_rdy"))
        od_ss, od_sd, od_nrm, odT_ps, odT_hi, odT_lo = (sem(x) for x in (
            "od_ss", "od_sd", "od_nrm", "odT_ps", "odT_hi", "odT_lo"))
        lg_ps, lg_max, lg_exp, mk_rdy, rk_ps, tab_rdy = (sem(x) for x in (
            "lg_ps", "lg_max", "lg_exp", "mk_rdy", "rk_ps", "tab_rdy"))
        m_sel, m_xg_ps, m_xhi, m_xlo, m_sT_ps, m_sT = (sem(x) for x in (
            "m_sel", "m_xg_ps", "m_xhi", "m_xlo", "m_sT_ps", "m_sT"))
        m_silu, m_gated, m_gTps, m_ghi, m_glo, m_ysb, m_sc, m_add = (sem(x) for x in (
            "m_silu", "m_gated", "m_gTps", "m_ghi", "m_glo", "m_ysb", "m_sc", "m_add"))
        gffn_in, m_hn = sem("gffn_in"), sem("m_hn")
        f_out = sem("f_out")

        H_AT = {1: 4, 2: 8, 3: 12, 4: 16, 6: 20}

        def part_k(w, j, half):
            return w.rearrange("(k p) n -> p k n", p=P)[:, 4 * half:4 * half + 4, j * 512:(j + 1) * 512]

        def part_n(w, j):
            return w.rearrange("(k p) n -> p k n", p=P)[:, :, j * SEQ:(j + 1) * SEQ]

        def part_rows(w, j):
            return w.rearrange("(k p) n -> p k n", p=P)[:, 2 * j:2 * j + 2, :]

        def split_of(n, width):
            return tuple(w[:, n % SPLIT, :].rearrange("p (k n) -> p k n", n=width) for w in (w_hi, w_lo))

        wie, woe, wio, woo = a["w_in_even"][0], a["w_out_even"][0], a["w_in_odd"][0], a["w_out_odd"][0]
        gate_w = [[part_k(a["w_ple_gate"][i], j, half) for j in range(2) for half in range(2)] for i in range(2)]
        proj_w = [[a["w_ple_proj"][i].rearrange("(k p) n -> p k n", p=P)[:, c:c + 1, :] for c in range(2)]
                  for i in range(2)]
        static = [part_k(wie, j, half) for j in range(3) for half in range(2)]
        static += [part_n(wie, 2 * j + half) for j in (4, 5, 3) for half in range(2)]
        static += [part_k(woe, j, half) for j in range(2) for half in range(2)]
        for m, j in MLP_ORDER:
            w = a[("w1_dense", "w3_dense", "w2_dense")[m]][0]
            static.append(part_n(w, j) if m < 2 else part_rows(w, j))
        static += gate_w[0] + proj_w[0]
        static += [part_n(wio, j) for j in range(12)]
        static += [part_k(wio, j, half) for j in (6, 7) for half in range(2)]
        static += [part_k(woo, j, half) for j in range(2) for half in range(2)]
        assert len(static) == P_MOE

        block = ctx.enter_context(nc.Block())

        @block.sync
        def _(sp):
            def put(n, src):
                dst = raw[:, n % RAW, 0:src.shape[1] * src.shape[2]].rearrange("p (k n) -> p k n", n=src.shape[2])
                sp.dma_start(dst, src).then_inc(raw_in[n % RAW], 16)

            for n, src in enumerate(static):
                if n >= RAW:
                    sp.wait_ge(lo_rdy, n - RAW + 1)
                put(n, src)

            def expert_piece(e, i):
                m, j, part = MOE_ORDER[i]
                w = a[("w1_moe", "w3_moe", "w2_moe")[m]].rearrange("o e (k p) n -> p (o e) k n", p=P)
                w = w[:, bass.ds(e, 1)]
                if m < 2:
                    w = w[:, :, 4 * part:4 * part + 4, j * 512:(j + 1) * 512]
                else:
                    w = w[:, :, 4 * j + 2 * part:4 * j + 2 * part + 2, :]
                return w.rearrange("p o k n -> p (o k) n")

            for i in range(PER_BLOCK):
                sp.wait_ge(lo_rdy, P_MOE + i - RAW + 1)
                put(i, expert_piece(0, i))
            sp.wait_ge(tab_rdy, 1)
            nblk = sp.value_load(blk_i[0:1, 15:16], min_val=NE, max_val=NE + MAX_OVER)
            with sp.Fori(1, nblk) as b:
                e = sp.value_load(blk_i[0:1, bass.ds(b, 1)], min_val=0, max_val=NE - 1)
                for i in range(PER_BLOCK):
                    sp.wait_ge(lo_rdy, b * PER_BLOCK + (P_MOE + i - RAW + 1))
                    put(i, expert_piece(e, i))
            for i, src in enumerate(gate_w[1] + proj_w[1]):
                sp.wait_ge(lo_rdy, nblk * PER_BLOCK + (P_MOE + i - RAW + 1))
                put(i, src)
            out_v = out.rearrange("o (t p) d -> p (o t) d", p=P)
            for t in range(NT):
                sp.wait_ge(f_out, t + 1)
                sp.dma_start(out_v[:, t, :], hn[:, t, :]).then_inc(out_done, 16)
            sp.wait_ge(out_done, 16 * NT)

        @block.tensor
        def _(pe):
            def split_wait(n):
                pe.wait_ge(lo_rdy, n + 1)

            def product(acc, lhs, rhs, first, final):
                (lh, ll), (rh, rl) = lhs, rhs
                pe.matmul(acc, lh, rh, start=first, stop=False)
                pe.matmul(acc, lh, rl, start=False, stop=False)
                return pe.matmul(acc, ll, rh, start=False, stop=final)

            def tokens_out(banks, x, n, half, tiles=NT):
                wh, wl = split_of(n, 512)
                for t in range(tiles):
                    for k in range(4):
                        xk = tuple(v[:, 4 * half + k, t * P:(t + 1) * P] for v in x)
                        last = product(ps[:, banks[t], :], xk, (wh[:, k, :], wl[:, k, :]),
                                       half == 0 and k == 0, half == 1 and k == 3)
                last.then_inc(piece_used, 1)

            def channels_out(bank, n):
                wh, wl = split_of(n, SEQ)
                for c in range(2):
                    for k in range(KC):
                        last = product(ps[:, bank, c * SEQ:(c + 1) * SEQ],
                                       (wh[:, k, c * P:(c + 1) * P], wl[:, k, c * P:(c + 1) * P]),
                                       (xs_hi[:, k, :], xs_lo[:, k, :]), k == 0, k == KC - 1)
                last.then_inc(piece_used, 1)

            def both_tokens_out(banks, n):
                for half in range(2):
                    split_wait(n + half)
                    tokens_out(banks, (xs_hi, xs_lo), n + half, half)

            def turn(bank, src, done):
                for c in range(4):
                    last = pe.transpose(ps[:, bank, c * P:(c + 1) * P], src[:, c * P:(c + 1) * P], ident)
                last.then_inc(done, 1)

            def norm_x(n):
                pe.wait_ge(n_hn, NT * (n + 1))
                for b in range(4):
                    for k in (2 * b, 2 * b + 1):
                        for t in range(NT):
                            at = (k % 2) * SEQ + t * P
                            last = pe.transpose(ps[:, b, at:at + P], hn[:, t, k * P:(k + 1) * P], ident)
                    last.then_inc(n_ps, 1)
                pe.wait_ge(n_lo, KC * (n + 1))

            pe.wait_ge(con_in, 16)
            pe.wait_ge(setup_in, N_SETUP)
            pe.transpose(ps[:, 4, 0:62], rows1[0:62, :], ident[0:62, 0:62])
            pe.transpose(ps[:, 4, 128:224], rows2[0:96, :], ident[0:96, 0:96]).then_inc(st_ps, 1)

            norm_x(0)
            pe.wait_ge(st_sb, 2)
            for n in range(3):
                both_tokens_out((2 * n, 2 * n + 1), P_QKV_E + 2 * n)
            for n in range(3):
                if n == 1:
                    pe.wait_ge(qkv_sb, 2)
                if n == 2:
                    pe.wait_ge(qkv_sb, 4)
                for m in range(2):
                    split_wait(P_CONV_E + 2 * n + m)
                    channels_out((6, 0, 2)[n] + m, P_CONV_E + 2 * n + m)
            pe.wait_ge(rope_done, NT)
            pe.wait_ge(v_sb, 2)
            pe.wait_ge(c_sb, 2)
            for b in range(4):
                for c in (2 * b, 2 * b + 1):
                    for t in range(NT):
                        at = (c % 2) * SEQ + t * P
                        last = pe.transpose(ps[:, 4 + b, at:at + P], qk[:, t, c * P:(c + 1) * P], ident)
                last.then_inc(qkT_ps, 1)

            def scores(hd):
                for m in range(2):
                    for t in range(NT):
                        last = pe.matmul(ps[:, 2 * (hd % 2) + m, t * SEQ:(t + 1) * SEQ],
                                         qkT[DH * m:DH * (m + 1), hd, t * P:(t + 1) * P],
                                         qkT[DH * m:DH * (m + 1), 4 + hd, :], start=True, stop=True)
                last.then_inc(sc_ps, 1)

            pe.wait_ge(qkT_sb, 4)
            pe.wait_ge(xb_used, 2)
            scores(0)
            pe.wait_ge(mix_conv, 4)
            scores(1)
            for hd in range(HEADS_A):
                pe.wait_ge(a_done, hd + 1)
                if hd >= 2:
                    pe.wait_ge(aT_sb, hd - 1)
                for kt in range(NT):
                    for t in range(NT):
                        at = kt * SEQ + t * P
                        last = pe.transpose(ps[:, 4 + hd % 2, at:at + P],
                                            adf[:, hd % 2, t, kt * P:(kt + 1) * P], ident)
                last.then_inc(aT_ps, 1)
                if hd + 2 < HEADS_A:
                    pe.wait_ge(sm_read, 2 * (hd + 1))
                    scores(hd + 2)
                pe.wait_ge(aT_sb, hd + 1)
                if hd >= 2:
                    pe.wait_ge(o_sb, hd - 1)
                for t in range(NT):
                    for kt in range(NT):
                        last = pe.matmul(ps[:, 6 + hd % 2, t * P:(t + 1) * P],
                                         aTt[:, hd % 2, kt, t * P:(t + 1) * P],
                                         vt[:, kt, hd * P:(hd + 1) * P], start=(kt == 0), stop=(kt == NT - 1))
                last.then_inc(av_ps, 1)
            pe.wait_ge(o_nrm, 1)
            for b in range(2):
                for hd in (2 * b, 2 * b + 1):
                    for t in range(NT):
                        at = (hd % 2) * SEQ + t * P
                        last = pe.transpose(ps[:, 4 + b, at:at + P], oat[:, t, hd, :], ident)
                last.then_inc(oT_ps, 1)
            pe.wait_ge(mix_lo, 3)
            for j in range(2):
                both_tokens_out((2 * j, 2 * j + 1), P_OUT_E + 2 * j)

            norm_x(1)

            def hidden(m, s):
                split_wait(MLP_AT[m, s])
                channels_out(2 * (s % 2) + m, MLP_AT[m, s])

            hidden(0, 0)
            hidden(1, 0)
            for s in range(HALF_FJ):
                if s + 1 < HALF_FJ:
                    hidden(0, s + 1)
                    hidden(1, s + 1)
                n = MLP_AT[2, s]
                split_wait(n)
                pe.wait_ge(gated_lo, s + 1)
                wh, wl = split_of(n, D)
                for c in range(2):
                    for t in range(NT):
                        at = c * SEQ + t * P
                        for half in range(2):
                            cut = slice(half * 512, (half + 1) * 512)
                            last = product(ps[:, 4 + 2 * t + half, :],
                                           (g_hi[:, s % 2, at:at + P], g_lo[:, s % 2, at:at + P]),
                                           (wh[:, c, cut], wl[:, c, cut]),
                                           s == 0 and c == 0, s == HALF_FJ - 1 and c == 1)
                last.then_inc(piece_used, 1)

            def embed(i, base, wait_piece):
                norm_x(2 + 3 * i)
                pe.wait_ge(p_in, 16 * (i + 1))
                for c in range(2):
                    for t in range(NT):
                        last = pe.transpose(ps[:, 4, c * SEQ + t * P:c * SEQ + (t + 1) * P],
                                            p_tok[:, t, c * P:(c + 1) * P], ident)
                last.then_inc(pT_ps, 1)
                for j in range(2):
                    for half in range(2):
                        wait_piece(2 * j + half)
                        tokens_out((2 * j, 2 * j + 1), (xs_hi, xs_lo), base + 2 * j + half, half)
                pe.wait_ge(pT_lo, i + 1)
                for c in range(2):
                    wait_piece(4 + c)
                    wh, wl = (w[:, (base + 4 + c) % SPLIT, 0:D] for w in (w_hi, w_lo))
                    for j in range(2):
                        cut = slice(j * 512, (j + 1) * 512)
                        for t in range(NT):
                            tok = slice(t * P, (t + 1) * P)
                            last = product(ps[:, 4 + 2 * j + t, :], (p_hi[:, c, tok], p_lo[:, c, tok]),
                                           (wh[:, cut], wl[:, cut]), c == 0, c == 1)
                    last.then_inc(piece_used, 1)

            embed(0, P_GATE_E, lambda i: split_wait(P_GATE_E + i))

            norm_x(3)
            pe.wait_ge(small_lo, 2)

            def small_product(bank, width, wh, wl, done):
                for t in range(NT):
                    for k in range(KC):
                        tok = slice(t * P, (t + 1) * P)
                        last = product(ps[:, bank, t * width:(t + 1) * width], (xs_hi[:, k, tok], xs_lo[:, k, tok]),
                                       (wh[:, k, :], wl[:, k, :]), k == 0, k == KC - 1)
                last.then_inc(done, 1)

            small_product(7, 2 * HEADS_D, wba_hi, wba_lo, ba_ps)
            for n in range(12):
                split_wait(P_QKV_O + n)
                if n >= 4:
                    pe.wait_ge(q_pad, n - 3)
                channels_out(n % 4, P_QKV_O + n)
            pe.wait_ge(g_rdy, 1)
            for t in range(NT):
                pe.matmul(ps[:, 6, t * 16:t * 16 + 8], upper, gdec[:, t, :], start=True, stop=True)
                last = pe.matmul(ps[:, 6, t * 16 + 8:t * 16 + 16], ones, gdec[:, t, :], start=True, stop=True)
            last.then_inc(cum_ps, 1)
            pe.wait_ge(cum_sb, 1)
            for j in range(2):
                both_tokens_out((4 + 2 * j, 5 + 2 * j), P_Z + 2 * j)

            pe.wait_ge(q_pad, 12)
            for g in range(8):
                pe.wait_ge(l2_sq, g + 1)
                if g >= 4:
                    pe.wait_ge(l2_sd, g - 3)
                pe.matmul(ps[:, g % 4, :], ones, bt[:, g % 2].rearrange("p a b -> p (a b)"),
                          start=True, stop=True).then_inc(l2_ps, 1)
            pe.wait_ge(l2_done, 8)
            pe.wait_ge(z_sb, 4)
            for t in range(NT):
                for b in range(4):
                    for c in range(4):
                        hd = 4 * b + c
                        last = pe.transpose(ps[:, 4 * t + b, c * P:(c + 1) * P],
                                            qkvT[:, 8 + hd, t * P:(t + 1) * P], ident)
                    last.then_inc(kv_ps, 1)

            def head_cols(bank, c):
                return ps[:, bank, c * P:(c + 1) * P]

            for t in range(NT):
                tok = slice(t * P, (t + 1) * P)
                u = 2 * t
                if t == 0:
                    pe.wait_ge(k_sb, 4)
                    pe.wait_ge(vb_sb, 4)
                else:
                    pe.wait_ge(od_sb, 2)
                    pe.wait_ge(s_sb, 2)
                for g in range(2):
                    for c in range(4):
                        last = pe.matmul(head_cols(g, c), gdec[:, t, 4 * g + c:4 * g + c + 1].broadcast_to([P, P]),
                                         upper, start=True, stop=True)
                    last.then_inc(rc_ps, 1)
                    for c in range(4):
                        last = pe.matmul(head_cols(2 + g, c), beta[:, t, 4 * g + c:4 * g + c + 1].broadcast_to([P, P]),
                                         ident, start=True, stop=True)
                    last.then_inc(br_ps, 1)
                for g in range(2):
                    for c in range(4):
                        last = pe.matmul(head_cols(6 + g, c), kT[:, 4 * g + c, tok], qT[:, 4 * g + c, tok],
                                         start=True, stop=True)
                    last.then_inc(at_ps, 1)
                for g in range(2):
                    pe.wait_ge(kb_rdy, u + g + 1)
                    for c in range(4):
                        last = pe.matmul(head_cols(4 + g, c), kT[:, 4 * g + c, tok], pm[:, g, c, :],
                                         start=True, stop=True)
                    last.then_inc(lt_ps, 1)
                for g in range(2):
                    pe.wait_ge(x1_rdy, u + g + 1)
                    for c in range(4):
                        last = pe.transpose(head_cols(g, c), XT[:, t, 4 * g + c, :], ident)
                    last.then_inc(x1_ps, 1)
                for l in range(1, LEVELS):
                    v = (LEVELS - 1) * u + 2 * (l - 1)
                    for g in range(2):
                        pe.wait_ge(bt_rdy, LEVELS * u + 2 * l + g + 1)
                        if l == 1:
                            pe.wait_ge(x1_sb, u + g + 1)
                        else:
                            pe.wait_ge(x_sb, v - 1 + g)
                        for c in range(4):
                            last = pe.matmul(head_cols(2 + g, c), bt[:, g, c, :], X[:, 4 * g + c, :],
                                             start=True, stop=True)
                        last.then_inc(p_ps, 1)
                    for g in range(2):
                        if l == 1:
                            pe.wait_ge(at_sb, u + g + 1)
                            pe.wait_ge(lt_sb, u + g + 1)
                        pe.wait_ge(p_sb, v + g + 1)
                        for c in range(4):
                            last = pe.matmul(head_cols(6 + g, c), pm[:, g, c, :], XT[:, t, 4 * g + c, :],
                                             start=True, stop=True)
                        if l < LEVELS - 1:
                            for c in range(4):
                                last = pe.matmul(head_cols(4 + g, c), XT[:, t, 4 * g + c, :], pm[:, g, c, :],
                                                 start=True, stop=True)
                        last.then_inc(x_ps, 1)
                pe.wait_ge(x_sb, (LEVELS - 1) * (u + 2))
                pe.wait_ge(ksc_rdy, t + 1)
                if t == 0:
                    for g in range(2):
                        for c in range(4):
                            last = pe.matmul(head_cols(g, c), XT[:, 0, 4 * g + c, :], vb[:, 0, 4 * g + c, :],
                                             start=True, stop=True)
                        last.then_inc(u_ps, 1)
                    for g in range(2):
                        pe.wait_ge(u_sb, g + 1)
                        for c in range(4):
                            last = pe.matmul(head_cols(4 + g, c), kbe[:, 4 * g + c, :], un[:, 4 * g + c, :],
                                             start=True, stop=True)
                        last.then_inc(s_ps, 1)
                        for c in range(4):
                            last = pe.matmul(head_cols(2 + g, c), AT[:, 0, 4 * g + c, :], un[:, 4 * g + c, :],
                                             start=True, stop=True)
                        last.then_inc(od_ps, 1)
                else:
                    for g in range(2):
                        for c in range(4):
                            last = pe.matmul(head_cols(g, c), kbe[:, 4 * g + c, :], XT[:, 1, 4 * g + c, :],
                                             start=True, stop=True)
                        last.then_inc(w_ps, 1)
                    for g in range(2):
                        for c in range(4):
                            last = pe.matmul(head_cols(6 + g, c), gdec[:, 1, 4 * g + c:4 * g + c + 1].broadcast_to([P, P]),
                                             upper, start=True, stop=True)
                        last.then_inc(qg_ps, 1)
                    for g in range(2):
                        pe.wait_ge(w_sb, g + 1)
                        for c in range(4):
                            hd = 4 * g + c
                            pe.matmul(head_cols(2 + g, c), XT[:, 1, hd, :], vb[:, 1, hd, :], start=True, stop=False)
                            last = pe.matmul(head_cols(2 + g, c), nwT[:, hd, :], S1[:, hd, :], start=False, stop=True)
                        last.then_inc(u_ps, 1)
                    for g in range(2):
                        pe.wait_ge(u_sb, 2 + g + 1)
                        pe.wait_ge(qg_rdy, g + 1)
                        for c in range(4):
                            hd = 4 * g + c
                            pe.matmul(head_cols(4 + g, c), qgT[:, hd, :], S1[:, hd, :], start=True, stop=False)
                            last = pe.matmul(head_cols(4 + g, c), AT[:, 1, hd, :], un[:, hd, :], start=False, stop=True)
                        last.then_inc(od_ps, 1)
            for b in range(4):
                pe.wait_ge(od_nrm, NT)
                for hd in (2 * b, 2 * b + 1):
                    for t in range(NT):
                        at = (hd % 2) * SEQ + t * P
                        last = pe.transpose(ps[:, b, at:at + P], AT[:, t, hd, :], ident)
                last.then_inc(odT_ps, 1)
            pe.wait_ge(odT_lo, 4)
            for j in range(2):
                both_tokens_out((4 + 2 * j, 5 + 2 * j), P_OUT_O + 2 * j)

            norm_x(4)
            small_product(4, NE, wrt_hi, wrt_lo, lg_ps)
            pe.wait_ge(mk_rdy, 1)
            pe.matmul(ps[:, 5, 0:NE], upper, r_m[:, 0, :], start=True, stop=True)
            pe.matmul(ps[:, 5, NE:2 * NE], ones, r_m[:, 0, :], start=True, stop=False)
            pe.matmul(ps[:, 5, NE:2 * NE], upper, r_m[:, 1, :], start=False, stop=True)
            pe.matmul(ps[:, 5, 2 * NE:3 * NE], ones, r_m[:, 0, :], start=True, stop=False)
            pe.matmul(ps[:, 5, 2 * NE:3 * NE], ones, r_m[:, 1, :], start=False, stop=True).then_inc(rk_ps, 1)
            pe.wait_ge(tab_rdy, 1)
            nblk = pe.value_load(blk_i[0:1, 15:16], min_val=NE, max_val=NE + MAX_OVER)

            def gather():
                for q in range(2):
                    for c in range(4):
                        for t in range(NT):
                            last = pe.matmul(ps[:, 6 + q, c * P:(c + 1) * P],
                                             hn[:, t, (4 * q + c) * P:(4 * q + c + 1) * P], sel[:, t, :],
                                             start=(t == 0), stop=(t == NT - 1))
                    last.then_inc(m_xg_ps, 1)

            pe.wait_ge(m_hn, NT)
            pe.wait_ge(m_sel, 1)
            gather()
            with pe.Fori(0, nblk) as b:
                def ready(i):
                    pe.wait_ge(lo_rdy, b * PER_BLOCK + (P_MOE + i + 1))

                def up(m, j):
                    for half in range(2):
                        i = MOE_AT[m, j, half]
                        ready(i)
                        tokens_out((2 * (j % 2) + m,), (xg_hi, xg_lo), i, half, 1)

                pe.wait_ge(m_xlo, b * 2 + 2)
                up(0, 0)
                up(1, 0)
                pe.wait_ge(m_add, b * 4 + 1)
                for t in range(NT):
                    last = pe.transpose(ps[:, 6, t * P:(t + 1) * P], selg[:, t, :], ident)
                last.then_inc(m_sT_ps, 1)
                for j in range(FJ):
                    if j + 1 < FJ:
                        up(0, j + 1)
                    else:
                        pe.wait_ge(m_sel, b + 2)
                        pe.wait_ge(m_sT, b + 1)
                        gather()
                    pe.wait_ge(m_gated, b * FJ + (j + 1))
                    turn(2 * (j % 2), gated[:, j % 2, :], m_gTps)
                    if j + 1 < FJ:
                        up(1, j + 1)
                    pe.wait_ge(m_glo, b * FJ + (j + 1))
                    for part in range(2):
                        i = MOE_AT[2, j, part]
                        ready(i)
                        wh, wl = split_of(i, D)
                        for c in range(2):
                            at = (2 * part + c) * P
                            for half in range(2):
                                cut = slice(half * 512, (half + 1) * 512)
                                last = product(ps[:, 4 + half, :],
                                               (g_hi[:, j % 2, at:at + P], g_lo[:, j % 2, at:at + P]),
                                               (wh[:, c, cut], wl[:, c, cut]),
                                               j == 0 and part == 0 and c == 0, j == FJ - 1 and part == 1 and c == 1)
                        last.then_inc(piece_used, 1)
                pe.wait_ge(m_ysb, b * 2 + 2)
                for t in range(NT):
                    if t == 1:
                        pe.wait_ge(m_xlo, b * 2 + 4)
                    for half in range(2):
                        pe.matmul(ps[:, 2 + 4 * t + half, :], selgT[:, t * P:(t + 1) * P],
                                  ysb[:, half * 512:(half + 1) * 512], start=True, stop=True).then_inc(m_sc, 1)

            embed(1, 0, lambda i: pe.wait_ge(lo_rdy, nblk * PER_BLOCK + (P_MOE + i + 1)))

        @block.scalar
        def _(act):
            count = [0]

            def link(ins):
                count[0] += 1
                ins.then_inc(act_link, 1)
                act.wait_ge(act_link, count[0])

            def split(n, used, landed):
                act.wait_ge(raw_in[n % RAW], landed)
                if used is not None:
                    act.wait_ge(piece_used, used)
                act.activation(w_hi[:, n % SPLIT, :], raw[:, n % RAW, :], ACT.Copy).then_inc(hi_rdy, 1)

            ahead = [0]

            def splits(upto):
                while ahead[0] <= upto:
                    n = ahead[0]
                    if n in (P_PROJ_E, P_PROJ_E + 1):
                        act.wait_ge(raw_in[n % RAW], 16 * (n // RAW + 1))
                        act.wait_ge(piece_used, n - SPLIT + 1)
                        act.activation(w_hi[:, n % SPLIT, 0:D], raw[:, n % RAW, 0:D], ACT.Copy).then_inc(hi_rdy, 1)
                    else:
                        split(n, n - SPLIT + 1 if n >= SPLIT else None, 16 * (n // RAW + 1))
                    ahead[0] += 1

            act.dma_start(h[:, :, :], a["x"][0].rearrange("(t p) d -> p t d", p=P)).then_inc(x_in, 16)
            act.dma_start(con[:, :], a["con"]).then_inc(con_in, 16)
            small = [
                (rows1[0:16, :], a["ln_mix"].rearrange("i (k p) -> (i k) p", p=P)),
                (rows1[16:32, :], a["ln_ffn"].rearrange("i (k p) -> (i k) p", p=P)),
                (rows1[32:48, :], a["ln_ple"].rearrange("i (k p) -> (i k) p", p=P)),
                (rows1[48:49, :], a["subln_gain"]),
                (rows1[49:50, :], a["onorm_gain"]),
                (rows1[50:62, :], a["conv_w_short"].rearrange("o j (m p) -> (o j m) p", p=P)),
                (rows2[0:96, :], a["conv_w_qkv"].rearrange("o j (m p) -> (o j m) p", p=P)),
                (posi[:, 0:NT], a["positions"].rearrange("o (t p) -> p (o t)", p=P)),
                (posi[:, NT:NT + SEQ], a["positions"].broadcast_to([P, SEQ])),
            ]
            small += [(lamv[:, i, :], a[w].broadcast_to([P, DH])) for i, w in enumerate(("lam_q1", "lam_k1", "lam_q2", "lam_k2"))]
            small += [
                (alog[:, :], a["a_log"].broadcast_to([P, HEADS_D])),
                (dtb[:, :], a["dt_bias"].broadcast_to([P, HEADS_D])),
                (wba[:, :, :], wio[:, 4 * 1024:4 * 1024 + 2 * HEADS_D].rearrange("(k p) n -> p k n", p=P)),
                (wrt[:, :, :], a["w_router"][0].rearrange("(k p) n -> p k n", p=P)),
            ]
            assert 16 * len(small) == N_SETUP
            for dst, src in small:
                act.dma_start(dst, src, allow_slow_non_contiguous=True).then_inc(setup_in, 16)

            def norm_std(n):
                for t in range(NT):
                    last = act.activation(hn[:, t, :], h[:, t, :], ACT.Square, accum_out=ssq[:, n, t:t + 1])
                link(last)
                act.activation(std[:, n, :], ssq[:, n, :], ACT.Sqrt, scale=1.0 / D, bias=eps6[:, 0:1]).then_inc(n_std, 1)

            def norm_hi(n):
                for k in range(KC):
                    act.wait_ge(n_ps, 4 * n + k // 2 + 1)
                    act.activation(xs_hi[:, k, :], ps[:, k // 2, (k % 2) * SEQ:(k % 2 + 1) * SEQ], ACT.Copy,
                                   scale=gT[:, GAIN_AT[n] + k:GAIN_AT[n] + k + 1]).then_inc(n_hi, 1)

            act.wait_ge(eps_set, 1)
            act.wait_ge(x_in, 16)
            norm_std(0)
            act.wait_ge(lam_dot, 1)
            act.activation(lame[:, :], lamd[:, :], ACT.Exp).then_inc(lam_exp, 1)
            act.activation(wba_hi[:, :, :], wba[:, :, :], ACT.Copy).then_inc(small_hi, 1)
            act.activation(wrt_hi[:, :, :], wrt[:, :, :], ACT.Copy).then_inc(small_hi, 1)
            act.wait_ge(st_sb, 2)
            norm_hi(0)
            splits(2)
            act.wait_ge(ang_rdy, 1)
            act.activation(cs[:, :, :, :], cs[:, :, :, :], ACT.Sin).then_inc(cs_rdy, 1)

            for n in range(2):
                splits(P_QKV_E + 2 * n + 3)
                act.wait_ge(piece_used, P_QKV_E + 2 * n + 2)
                for t in range(NT):
                    act.activation(qk[:, t, n * 512:(n + 1) * 512], ps[:, 2 * n + t, :], ACT.Copy).then_inc(qkv_sb, 1)
            splits(P_QKV_E + 7)
            act.wait_ge(piece_used, P_QKV_E + 6)
            for t in range(NT):
                act.activation(vt[:, t, :], ps[:, 4 + t, :], ACT.Copy).then_inc(v_sb, 1)
            for m in range(2):
                splits(P_CONV_E + m + 2)
                act.wait_ge(piece_used, P_CONV_E + m + 1)
                act.activation(cT[:, 2 * m:2 * m + 2, :], ps[:, 6 + m, :].rearrange("p (c s) -> p c s", c=2),
                               ACT.Copy).then_inc(c_sb, 1)
            splits(P_OUT_E + 1)
            act.wait_ge(mix_conv, 4)
            act.activation(xs_hi[:, 4:8, :], mix_c, ACT.Copy).then_inc(mix_hi, 1)
            splits(P_OUT_E + 2)
            for b in range(2):
                act.wait_ge(qkT_ps, b + 1)
                act.activation(qkT[:, 2 * b:2 * b + 2, :], ps[:, 4 + b, :].rearrange("p (c s) -> p c s", c=2),
                               ACT.Copy).then_inc(qkT_sb, 1)

            def exps(hd):
                act.wait_ge(sm_rdy, hd + 1)
                for i in range(4):
                    last = act.activation(sm[:, hd % 2, i, :], sm[:, hd % 2, i, :], ACT.Exp, scale=DH ** -0.5,
                                          bias=nb[:, hd % 2, i:i + 1], accum_out=esum[:, hd % 2, i:i + 1])
                last.then_inc(ex_done, 1)

            exps(0)
            for hd in range(HEADS_A):
                if hd + 1 < HEADS_A:
                    exps(hd + 1)
                act.wait_ge(aT_ps, hd + 1)
                if hd >= 2:
                    act.wait_ge(av_ps, hd - 1)
                act.activation(aTt[:, hd % 2, :, :], ps[:, 4 + hd % 2, :].rearrange("p (k s) -> p k s", k=NT),
                               ACT.Copy).then_inc(aT_sb, 1)
            act.wait_ge(o_ss, 1)
            act.activation(osd[:, 0:8], oss[:, 0:8], ACT.Sqrt, scale=1.0 / P, bias=eps5[:, 0:1]).then_inc(o_sd, 1)
            for b in range(2):
                act.wait_ge(oT_ps, b + 1)
                act.activation(xs_hi[:, 2 * b:2 * b + 2, :], ps[:, 4 + b, :].rearrange("p (c s) -> p c s", c=2),
                               ACT.Copy, scale=gT[:, G_SUB:G_SUB + 1]).then_inc(mix_hi, 1)
            splits(P_MLP + 2)

            act.wait_ge(h_ready, H_AT[1])
            act.dma_start(p_tok[:, :, :], a["p"][0, 0].rearrange("(t p) d -> p t d", p=P)).then_inc(p_in, 16)
            norm_std(1)
            norm_hi(1)

            for s in range(HALF_FJ):
                splits(MLP_AT[0, s] + 2)
                act.wait_ge(piece_used, MLP_AT[0, s] + 1)
                act.activation(sil[:, s % 2, :], ps[:, 2 * (s % 2), :], ACT.Silu).then_inc(silu_sb, 1)
                splits(MLP_AT[1, s] + 2)
                act.wait_ge(gated_sb, s + 1)
                act.activation(g_hi[:, s % 2, :], gated[:, s % 2, :], ACT.Copy).then_inc(gated_hi, 1)
            splits(P_GATE_E + 2)

            def embed(i, pieces, used):
                norm_hi(2 + 3 * i)
                act.wait_ge(pT_ps, i + 1)
                act.activation(p_hi, ps[:, 4, :].rearrange("p (c s) -> p c s", c=2), ACT.Copy).then_inc(pT_hi, 1)
                for j in range(2):
                    pieces(2 * j + 1 + 2)
                    used(2 * j + 2)
                    for t in range(NT):
                        act.activation(sgm[:, t, j * 512:(j + 1) * 512], ps[:, 2 * j + t, :], ACT.Sigmoid).then_inc(sgm_sb, 1)

            act.wait_ge(h_ready, H_AT[2])
            norm_std(2)
            embed(0, lambda i: splits(P_GATE_E + i), lambda i: act.wait_ge(piece_used, P_GATE_E + i))
            splits(P_QKV_O + 2)

            act.wait_ge(h_ready, H_AT[3])
            norm_std(3)
            norm_hi(3)
            act.wait_ge(ba_neg, 1)
            act.activation(yexp[:, :, :], yneg[:, :, :], ACT.Exp)
            act.activation(ealog[:, :], alog[:, :], ACT.Exp).then_inc(ba_exp, 1)
            act.wait_ge(ba_exp, 1)
            act.activation(yln[:, :, :], yexp[:, :, 8:16], ACT.Ln, bias=1.0).then_inc(ba_ln, 1)
            act.wait_ge(pad_zero, 1)
            for n in range(6):
                for m in range(2):
                    i = P_QKV_O + 2 * n + m
                    splits(i + 2)
                    act.wait_ge(piece_used, i + 1)
                    if n >= 2 and m == 0:
                        act.wait_ge(cv_done, n - 1)
                    act.activation(upo[:, n % 2, 2 * m:2 * m + 2, DN_TAPS - 1:], ps[:, (2 * n + m) % 4, :].rearrange(
                        "p (c s) -> p c s", c=2), ACT.Copy).then_inc(q_pad, 1)
                if n >= 1:
                    act.wait_ge(cv_done, n)
                    act.activation(qkvT[:, 4 * (n - 1):4 * n, :], qkvT[:, 4 * (n - 1):4 * n, :], ACT.Silu).then_inc(cv_silu, 1)
            splits(P_Z + 2)
            act.wait_ge(cv_done, 6)
            act.activation(qkvT[:, 20:24, :], qkvT[:, 20:24, :], ACT.Silu).then_inc(cv_silu, 1)
            for j in range(2):
                splits(P_Z + 2 * j + 3)
                act.wait_ge(piece_used, P_Z + 2 * j + 2)
                for t in range(NT):
                    act.activation(zs[:, t, j * 512:(j + 1) * 512], ps[:, 4 + 2 * j + t, :], ACT.Silu).then_inc(z_sb, 1)
            splits(P_OUT_O + 2)
            act.wait_ge(cum_sb, 1)
            act.activation(dcy[:, :, :, :], dcy[:, :, :, :], ACT.Exp).then_inc(dcy_rdy, 1)
            act.wait_ge(cv_silu, 6)
            for g in range(9):
                if g < 8:
                    if g >= 2:
                        act.wait_ge(l2_ps, g - 1)
                    act.activation(bt[:, g % 2].rearrange("p a b -> p (a b)"),
                                   qkvT[:, 2 * g:2 * g + 2, :].rearrange("p a b -> p (a b)"), ACT.Square).then_inc(l2_sq, 1)
                if g >= 1:
                    act.wait_ge(l2_ps, g)
                    if g >= 3:
                        act.wait_ge(l2_done, g - 2)
                    act.activation(pm[:, (g - 1) % 2].rearrange("p a b -> p (a b)"), ps[:, (g - 1) % 4, :], ACT.Sqrt,
                                   bias=eps6[:, 0:1]).then_inc(l2_sd, 1)
            for t in range(NT):
                for b in range(2):
                    act.wait_ge(kv_ps, 4 * t + b + 1)
                    act.activation(ktok[:, t, 4 * b:4 * b + 4, :], ps[:, 4 * t + b, :].rearrange(
                        "p (c s) -> p c s", c=4), ACT.Copy).then_inc(k_sb, 1)
            four = dict(c=4)
            for t in range(NT):
                u = 2 * t
                for g in range(2):
                    act.wait_ge(dd_rdy, u + g + 1)
                    act.activation(AT[:, t, 4 * g:4 * g + 4, :], AT[:, t, 4 * g:4 * g + 4, :], ACT.Exp).then_inc(dec_exp, 1)
                for g in range(2):
                    act.wait_ge(x1_ps, u + g + 1)
                    act.activation(X[:, 4 * g:4 * g + 4, :], ps[:, g, :].rearrange("p (c s) -> p c s", **four),
                                   ACT.Copy).then_inc(x1_sb, 1)
                for l in range(1, LEVELS):
                    for g in range(2):
                        act.wait_ge(p_ps, (LEVELS - 1) * u + 2 * (l - 1) + g + 1)
                        act.activation(pm[:, g], ps[:, 2 + g, :].rearrange("p (c s) -> p c s", **four),
                                       ACT.Copy).then_inc(p_sb, 1)
                if t == 0:
                    for g in range(2):
                        act.wait_ge(u_ps, g + 1)
                        act.activation(un[:, 4 * g:4 * g + 4, :], ps[:, g, :].rearrange("p (c s) -> p c s", **four),
                                       ACT.Copy).then_inc(u_sb, 1)
                    for g in range(2):
                        act.wait_ge(s_ps, g + 1)
                        act.activation(S1[:, 4 * g:4 * g + 4, :], ps[:, 4 + g, :].rearrange("p (c s) -> p c s", **four),
                                       ACT.Copy).then_inc(s_sb, 1)
                else:
                    for g in range(2):
                        act.wait_ge(w_ps, g + 1)
                        act.activation(nwT[:, 4 * g:4 * g + 4, :], ps[:, g, :].rearrange("p (c s) -> p c s", **four),
                                       ACT.Copy, scale=-1.0).then_inc(w_sb, 1)
                    for g in range(2):
                        act.wait_ge(qg_ps, g + 1)
                        act.activation(qgT[:, 4 * g:4 * g + 4, :], ps[:, 6 + g, :].rearrange("p (c s) -> p c s", **four),
                                       ACT.Exp).then_inc(qg_exp, 1)
                    for g in range(2):
                        act.wait_ge(u_ps, 2 + g + 1)
                        act.activation(un[:, 4 * g:4 * g + 4, :], ps[:, 2 + g, :].rearrange("p (c s) -> p c s", **four),
                                       ACT.Copy).then_inc(u_sb, 1)
            act.wait_ge(od_sb, 4)
            for t in range(NT):
                last = act.activation(odq[:, t, :, :], AT[:, t, :, :], ACT.Square)
                last.then_inc(od_ss, 1)
            act.wait_ge(od_sd, 1)
            act.activation(osd[:, :], oss[:, :], ACT.Sqrt, scale=1.0 / P, bias=eps6[:, 0:1]).then_inc(od_sd, 1)
            for b in range(4):
                act.wait_ge(odT_ps, b + 1)
                act.activation(xs_hi[:, 2 * b:2 * b + 2, :], ps[:, b, :].rearrange("p (c s) -> p c s", c=2), ACT.Copy,
                               scale=gT[:, G_ON:G_ON + 1]).then_inc(odT_hi, 1)
            splits(P_MOE + 2)

            act.wait_ge(h_ready, H_AT[4])
            norm_std(4)
            act.dma_start(p_tok[:, :, :], a["p"][1, 0].rearrange("(t p) d -> p t d", p=P)).then_inc(p_in, 16)
            act.dma_start(gfin[:, :], a["ln_final"].unsqueeze(0).broadcast_to([P, D])).then_inc(gfin_in, 16)
            act.dma_start(gffn[:, :], a["ln_ffn"][1:2, :].broadcast_to([P, D])).then_inc(gffn_in, 16)
            norm_hi(4)
            act.wait_ge(lg_max, 1)
            for t in range(NT):
                last = act.activation(r_e[:, t, :], r_l[:, t, :], ACT.Exp, bias=r_nmx[:, t:t + 1])
            last.then_inc(lg_exp, 1)
            act.wait_ge(tab_rdy, 1)
            nblk = act.value_load(blk_i[0:1, 15:16], min_val=NE, max_val=NE + MAX_OVER)

            def tokens_hi(done):
                for q in range(2):
                    act.wait_ge(m_xg_ps, done + (q + 1))
                    act.activation(xg_hi[:, 4 * q:4 * q + 4, :], ps[:, 6 + q, :].rearrange("p (c s) -> p c s", c=4),
                                   ACT.Copy).then_inc(m_xhi, 1)

            tokens_hi(0)
            with act.Fori(0, nblk) as b:
                at = [SPLIT]

                def pieces(upto):
                    while at[0] <= upto:
                        i = at[0]
                        split(i, b * PER_BLOCK + (P_MOE + i - SPLIT + 1),
                              b * (16 * PER_BLOCK // RAW) + 16 * ((P_MOE + i) // RAW + 1))
                        at[0] += 1

                def silu_of(j):
                    i = MOE_AT[0, j, 1]
                    pieces(i + 2)
                    act.wait_ge(piece_used, b * PER_BLOCK + (P_MOE + i + 1))
                    act.activation(sil[:, j % 2, :], ps[:, 2 * (j % 2), :], ACT.Silu).then_inc(m_silu, 1)

                silu_of(0)
                pieces(MOE_AT[1, 0, 1] + 2)
                act.wait_ge(m_sT_ps, b + 1)
                act.activation(selgT[:, :], ps[:, 6, 0:SEQ], ACT.Copy).then_inc(m_sT, 1)
                for j in range(FJ):
                    if j + 1 < FJ:
                        silu_of(j + 1)
                    else:
                        pieces(MOE_AT[2, j - 1, 1] + 2)
                    act.wait_ge(m_gTps, b * FJ + (j + 1))
                    act.activation(g_hi[:, j % 2, :], ps[:, 2 * (j % 2), :], ACT.Copy).then_inc(m_ghi, 1)
                tokens_hi(b * 2 + 2)
                pieces(PER_BLOCK + 1)
                act.wait_ge(piece_used, b * PER_BLOCK + (P_MOE + PER_BLOCK))
                for half in range(2):
                    act.activation(ysb[:, half * 512:(half + 1) * 512], ps[:, 4 + half, :], ACT.Copy).then_inc(m_ysb, 1)
                pieces(PER_BLOCK + 2)

            act.wait_ge(m_add, nblk * 4 + 1)
            norm_std(5)
            tail = [SPLIT]

            def tail_pieces(upto):
                while tail[0] <= upto:
                    i = tail[0]
                    width = PIECE if i < 4 else D
                    act.wait_ge(raw_in[i % RAW], nblk * (16 * PER_BLOCK // RAW) + 16 * ((P_MOE + i) // RAW + 1))
                    act.wait_ge(piece_used, nblk * PER_BLOCK + (P_MOE + i - SPLIT + 1))
                    act.activation(w_hi[:, i % SPLIT, 0:width], raw[:, i % RAW, 0:width], ACT.Copy).then_inc(hi_rdy, 1)
                    tail[0] += 1

            embed(1, tail_pieces, lambda i: act.wait_ge(piece_used, nblk * PER_BLOCK + (P_MOE + i)))
            act.wait_ge(h_ready, H_AT[6])
            norm_std(6)

        @block.gpsimd
        def _(pool):
            for t in range(NT):
                u = 2 * t
                for l in range(LEVELS):
                    for g in range(2):
                        if l == 0:
                            pool.wait_ge(lt_sb, u + g + 1)
                            if t == 0:
                                pool.wait_ge(l2_ps, 8)
                            else:
                                pool.wait_ge(od_ps, 2)
                        elif l == 1:
                            pool.wait_ge(x1_rdy, u + g + 1)
                        else:
                            pool.wait_ge(p_ps, (LEVELS - 1) * u + 2 * (l - 2) + g + 1)
                        pool.tensor_tensor(bt[:, g], LT[:, 4 * g:4 * g + 4, :], over(level_mask(l), 4),
                                           ALU.mult).then_inc(bt_rdy, 1)

        @block.vector
        def _(dve):
            count = [0]

            def link(ins):
                count[0] += 1
                ins.then_inc(dve_link, 1)
                dve.wait_ge(dve_link, count[0])

            def split(n, hi_count, width=PIECE):
                dve.wait_ge(hi_rdy, hi_count)
                dve.tensor_tensor(w_lo[:, n % SPLIT, 0:width], raw[:, n % RAW, 0:width],
                                  w_hi[:, n % SPLIT, 0:width].bitcast(F32), ALU.subtract).then_inc(lo_rdy, 1)

            ahead = [0]

            def splits(upto):
                while ahead[0] <= upto:
                    n = ahead[0]
                    split(n, n + 1, D if n in (P_PROJ_E, P_PROJ_E + 1) else PIECE)
                    ahead[0] += 1

            dve.memset(eps5[:, :], SUBLN_EPS)
            dve.memset(upad[:, :, 0:SC_TAPS - 1], 0.0)
            dve.memset(eps6[:, :], RMS_EPS).then_inc(eps_set, 1)
            dve.wait_ge(setup_in, N_SETUP)
            dve.tensor_tensor(lamp[:, :, :], lamv.rearrange("p (a b) d -> p a b d", b=2)[:, :, 0, :],
                              lamv.rearrange("p (a b) d -> p a b d", b=2)[:, :, 1, :], ALU.mult).then_inc(dve_link, 1)
            count[0] += 1
            dve.wait_ge(dve_link, count[0])
            dve.tensor_reduce(lamd[:, :], lamp[:, :, :], AX, ALU.add).then_inc(lam_dot, 1)
            dve.wait_ge(st_ps, 1)
            link(dve.tensor_copy(gT[:, :], ps[:, 4, 0:62]))
            dve.tensor_copy(cwT[:, :], ps[:, 4, 128:224]).then_inc(st_sb, 1)
            dve.tensor_scalar(gT[:, G_SUB:G_SUB + 1], gT[:, G_SUB:G_SUB + 1], 1.0 - LAM0, None, ALU.mult).then_inc(st_sb, 1)

            def norm_hn(n):
                dve.wait_ge(n_std, n + 1)
                link(dve.reciprocal(rstd[:, n, :], std[:, n, :]))
                for t in range(NT):
                    dve.tensor_scalar(hn[:, t, :], h[:, t, :], rstd[:, n, t:t + 1], None, ALU.mult).then_inc(n_hn, 1)

            def norm_lo(n):
                for k in range(KC):
                    dve.wait_ge(n_hi, KC * n + 2 * (k // 2) + 2)
                    dve.scalar_tensor_tensor(xs_lo[:, k, :], ps[:, k // 2, (k % 2) * SEQ:(k % 2 + 1) * SEQ],
                                             gT[:, GAIN_AT[n] + k:GAIN_AT[n] + k + 1], xs_hi[:, k, :].bitcast(F32),
                                             ALU.mult, ALU.subtract).then_inc(n_lo, 1)

            norm_hn(0)
            dve.wait_ge(small_hi, 2)
            dve.tensor_tensor(wba_lo[:, :, :], wba[:, :, :], wba_hi[:, :, :].bitcast(F32), ALU.subtract).then_inc(small_lo, 1)
            dve.tensor_tensor(wrt_lo[:, :, :], wrt[:, :, :], wrt_hi[:, :, :].bitcast(F32), ALU.subtract).then_inc(small_lo, 1)
            dve.wait_ge(st_sb, 2)
            norm_lo(0)
            splits(2)

            dve.tensor_copy(posc[:, :], posi[:, 0:NT])
            link(dve.tensor_copy(posrow, posi[:, NT:NT + SEQ]))
            for t in range(NT):
                dve.tensor_scalar(maskb[:, t, :], posrow, posc[:, t:t + 1], NEG, ALU.is_gt, ALU.mult)
                last = dve.tensor_scalar(ang[:, t, :], con[:, C_FREQ:C_FREQ + HALF_ROT], posc[:, t:t + 1], None, ALU.mult)
            link(last)
            link(dve.tensor_scalar(turns, ang, 1.0 / (2 * math.pi), 12582912.0, ALU.mult, ALU.add))
            link(dve.tensor_scalar(turns, turns, 12582912.0, None, ALU.subtract))
            for part in TWO_PI:
                link(dve.scalar_tensor_tensor(ang, turns, -part, ang, ALU.mult, ALU.add))
            link(dve.tensor_scalar(cs[:, 1], ang, math.pi - 1e-6, -(math.pi - 1e-6), ALU.min, ALU.max))
            link(dve.scalar_tensor_tensor(ang, cs[:, 1], -1.0, cs[:, 1], ALU.mult, ALU.max))
            dve.tensor_scalar(cs[:, 0], ang, -1.0, math.pi / 2, ALU.mult, ALU.add).then_inc(ang_rdy, 1)
            dve.wait_ge(lam_exp, 1)
            link(dve.scalar_tensor_tensor(nlam[:, :], lame[:, 1:2], LAM0, lame[:, 0:1], ALU.subtract, ALU.subtract))

            splits(P_QKV_E + 5)
            dve.wait_ge(cs_rdy, 1)
            for t in range(NT):
                dve.wait_ge(qkv_sb, 3 + t)
                heads = qk[:, t, :].rearrange("p (h d) -> p h d", d=DH)
                x1, x2 = heads[:, :, 0:HALF_ROT], heads[:, :, HALF_ROT:ROT]
                cos, sin = over(cs[:, 0, t, :], 16), over(cs[:, 1, t, :], 16)
                dve.tensor_tensor(rt[:, 0], x1, cos, ALU.mult)
                dve.tensor_tensor(rt[:, 1], x2, sin, ALU.mult)
                dve.tensor_tensor(rt[:, 2], x2, cos, ALU.mult)
                link(dve.tensor_tensor(rt[:, 3], x1, sin, ALU.mult))
                dve.tensor_tensor(x1, rt[:, 0], rt[:, 1], ALU.subtract)
                link(dve.tensor_tensor(x2, rt[:, 2], rt[:, 3], ALU.add))
                dve.engine_nop().then_inc(rope_done, 1)
            for m in range(2):
                splits(P_CONV_E + 2 + m + 2)
                dve.wait_ge(c_sb, m + 1)
                dve.wait_ge(piece_used, P_CONV_E + 2 + m + 1)
                dve.tensor_tensor(upad[:, 2 * m:2 * m + 2, SC_TAPS - 1:], cT[:, 2 * m:2 * m + 2, :],
                                  ps[:, m, :].rearrange("p (c s) -> p c s", c=2), ALU.mult).then_inc(xb_used, 1)
            splits(P_OUT_E + 1)
            dve.wait_ge(xb_used, 2)
            for j in range(SC_TAPS):
                for m in range(4):
                    tap = gT[:, G_CW + 4 * j + m:G_CW + 4 * j + m + 1]
                    src = upad[:, m, j:j + SEQ]
                    if j == 0:
                        last = dve.tensor_scalar(mix_c[:, m, :], src, tap, None, ALU.mult)
                    else:
                        last = dve.scalar_tensor_tensor(mix_c[:, m, :], src, tap, mix_c[:, m, :], ALU.mult, ALU.add)
                link(last)
            dve.wait_ge(piece_used, P_CONV_E + 6)
            for m in range(4):
                dve.tensor_tensor(mix_c[:, m, :], mix_c[:, m, :],
                                  ps[:, 2 + m // 2, (m % 2) * SEQ:(m % 2 + 1) * SEQ], ALU.mult).then_inc(mix_conv, 1)
            for b in range(2, 4):
                dve.wait_ge(qkT_ps, b + 1)
                dve.tensor_copy(qkT[:, 2 * b:2 * b + 2, :], ps[:, 4 + b, :].rearrange("p (c s) -> p c s", c=2)).then_inc(qkT_sb, 1)
            dve.wait_ge(mix_hi, 1)
            dve.tensor_tensor(xs_lo[:, 4:8, :], mix_c, xs_hi[:, 4:8, :].bitcast(F32), ALU.subtract).then_inc(mix_lo, 1)
            splits(P_OUT_E + 2)

            def masked(hd):
                dve.wait_ge(sc_ps, hd + 1)
                for m in range(2):
                    dve.tensor_tensor(sm[:, hd % 2, 2 * m:2 * m + 2, :], ps[:, 2 * (hd % 2) + m, :].rearrange(
                        "p (t s) -> p t s", t=NT), maskb, ALU.add).then_inc(sm_read, 1)
                dve.wait_ge(sm_read, 2 * (hd + 1))
                link(dve.tensor_reduce(mx[:, hd % 2, :], sm[:, hd % 2], AX, ALU.max))
                dve.tensor_scalar(nb[:, hd % 2, :], mx[:, hd % 2, :], -(DH ** -0.5), None, ALU.mult).then_inc(sm_rdy, 1)

            masked(0)
            for hd in range(HEADS_A):
                if hd + 1 < HEADS_A:
                    masked(hd + 1)
                u = hd % 2
                dve.wait_ge(ex_done, hd + 1)
                link(dve.reciprocal(erc[:, u, :], esum[:, u, :]))
                link(dve.tensor_scalar(erc[:, u, 2:4], erc[:, u, 2:4], nlam[:, 0:1], None, ALU.mult))
                if hd >= 2:
                    dve.wait_ge(aT_ps, hd - 1)
                for t in range(NT):
                    last = dve.tensor_scalar(adf[:, u, t, :], sm[:, u, t, :], erc[:, u, t:t + 1], None, ALU.mult)
                link(last)
                for t in range(NT):
                    last = dve.scalar_tensor_tensor(adf[:, u, t, :], sm[:, u, 2 + t, :], erc[:, u, 2 + t:3 + t],
                                                    adf[:, u, t, :], ALU.mult, ALU.add)
                last.then_inc(a_done, 1)
                dve.wait_ge(a_done, hd + 1)
                if hd >= 1:
                    dve.wait_ge(av_ps, hd)
                    dve.tensor_copy(oat[:, :, hd - 1, :], ps[:, 6 + (hd - 1) % 2, 0:SEQ].rearrange(
                        "p (t v) -> p t v", t=NT)).then_inc(o_sb, 1)
            dve.wait_ge(av_ps, HEADS_A)
            dve.tensor_copy(oat[:, :, HEADS_A - 1, :], ps[:, 6 + (HEADS_A - 1) % 2, 0:SEQ].rearrange(
                "p (t v) -> p t v", t=NT)).then_inc(o_sb, 1)
            dve.wait_ge(o_sb, HEADS_A)
            o3 = oat.rearrange("p t h v -> p (t h) v")
            q3 = osq.rearrange("p t h v -> p (t h) v")
            link(dve.tensor_tensor(q3, o3, o3, ALU.mult))
            dve.tensor_reduce(oss[:, 0:8], q3, AX, ALU.add).then_inc(o_ss, 1)
            dve.wait_ge(o_sd, 1)
            link(dve.reciprocal(ors[:, 0:8], osd[:, 0:8]))
            dve.tensor_tensor(o3, o3, along(ors[:, 0:8], P), ALU.mult).then_inc(o_nrm, 1)

            def add_h(t, half, src):
                piece = h[:, t, half * 512:(half + 1) * 512]
                return dve.tensor_tensor(piece, piece, src, ALU.add)

            for b in range(2):
                dve.wait_ge(mix_hi, b + 2)
                dve.scalar_tensor_tensor(xs_lo[:, 2 * b:2 * b + 2, :], ps[:, 4 + b, :].rearrange("p (c s) -> p c s", c=2),
                                         gT[:, G_SUB:G_SUB + 1], xs_hi[:, 2 * b:2 * b + 2, :].bitcast(F32),
                                         ALU.mult, ALU.subtract).then_inc(mix_lo, 1)
            for j in range(2):
                splits(P_OUT_E + 2 * j + 3)
                dve.wait_ge(piece_used, P_OUT_E + 2 * j + 2)
                for t in range(NT):
                    add_h(t, j, ps[:, 2 * j + t, :]).then_inc(h_ready, 1)

            dve.wait_ge(h_ready, H_AT[1])
            norm_hn(1)
            splits(P_MLP + 2)
            norm_lo(1)
            for s in range(HALF_FJ):
                splits(MLP_AT[1, s] + 2)
                dve.wait_ge(piece_used, MLP_AT[1, s] + 1)
                dve.wait_ge(silu_sb, s + 1)
                dve.tensor_tensor(gated[:, s % 2, :], sil[:, s % 2, :], ps[:, 2 * (s % 2) + 1, :], ALU.mult).then_inc(gated_sb, 1)
                dve.wait_ge(gated_hi, s + 1)
                dve.tensor_tensor(g_lo[:, s % 2, :], gated[:, s % 2, :], g_hi[:, s % 2, :].bitcast(F32),
                                  ALU.subtract).then_inc(gated_lo, 1)
            splits(P_GATE_E + 1)
            dve.wait_ge(piece_used, P_GATE_E)
            for t in range(NT):
                for half in range(2):
                    add_h(t, half, ps[:, 4 + 2 * t + half, :]).then_inc(h_ready, 1)

            def embed(i, pieces, used):
                norm_lo(2 + 3 * i)
                dve.wait_ge(pT_hi, i + 1)
                dve.tensor_tensor(p_lo, ps[:, 4, :].rearrange("p (c s) -> p c s", c=2), p_hi.bitcast(F32),
                                  ALU.subtract).then_inc(pT_lo, 1)
                pieces(5)
                used(6)
                for j in range(2):
                    for t in range(NT):
                        dve.wait_ge(sgm_sb, 4 * i + 2 * j + t + 1)
                        link(dve.tensor_tensor(ptmp[:, t, :], sgm[:, t, j * 512:(j + 1) * 512],
                                               ps[:, 4 + 2 * j + t, :], ALU.mult))
                        add_h(t, j, ptmp[:, t, :]).then_inc(h_ready, 1)

            dve.wait_ge(h_ready, H_AT[2])
            norm_hn(2)
            splits(P_GATE_E + 2)
            embed(0, lambda i: splits(P_GATE_E + i), lambda i: dve.wait_ge(piece_used, P_GATE_E + i))

            dve.wait_ge(h_ready, H_AT[3])
            norm_hn(3)
            splits(P_QKV_O + 2)
            norm_lo(3)
            dve.memset(upo[:, :, :, 0:DN_TAPS - 1], 0.0).then_inc(pad_zero, 1)
            dve.wait_ge(ba_ps, 1)
            link(dve.tensor_copy(ba[:, :, :], ps[:, 7, 0:32].rearrange("p (t n) -> p t n", t=NT)))
            link(dve.tensor_tensor(ba[:, :, 8:16], ba[:, :, 8:16], over(dtb[:, :], NT), ALU.add))
            dve.tensor_scalar(yneg[:, :, 0:8], ba[:, :, 0:8], -1.0, None, ALU.mult)
            dve.scalar_tensor_tensor(yneg[:, :, 8:16], ba[:, :, 8:16], -1.0, ba[:, :, 8:16], ALU.mult, ALU.min).then_inc(ba_neg, 1)
            dve.wait_ge(ba_ln, 1)
            link(dve.tensor_scalar(yexp[:, :, 0:8], yexp[:, :, 0:8], 1.0, None, ALU.add))
            dve.reciprocal(beta[:, :, :], yexp[:, :, 0:8])
            link(dve.scalar_tensor_tensor(gdec[:, :, :], ba[:, :, 8:16], 0.0, yln[:, :, :], ALU.max, ALU.add))
            dve.scalar_tensor_tensor(gdec[:, :, :], gdec[:, :, :], -1.0, over(ealog[:, :], NT), ALU.mult, ALU.mult).then_inc(g_rdy, 1)

            def conv(n):
                splits(P_QKV_O + 2 * n + 3)
                for m in range(2):
                    dve.wait_ge(q_pad, 2 * n + m + 1)
                for j in range(DN_TAPS):
                    for m in range(4):
                        ch = 4 * n + m
                        tap = cwT[:, j * QKV_CHUNKS + ch:j * QKV_CHUNKS + ch + 1]
                        src = upo[:, n % 2, m, j:j + SEQ]
                        if j == 0:
                            last = dve.tensor_scalar(qkvT[:, ch, :], src, tap, None, ALU.mult)
                        else:
                            last = dve.scalar_tensor_tensor(qkvT[:, ch, :], src, tap, qkvT[:, ch, :], ALU.mult, ALU.add)
                    if j < DN_TAPS - 1:
                        link(last)
                last.then_inc(cv_done, 1)

            for n in range(6):
                conv(n)
            splits(P_Z + 2)
            dve.wait_ge(cum_ps, 1)
            link(dve.tensor_copy(cum[:, :, :, :], ps[:, 6, 0:32].rearrange("p (t k n) -> p t k n", t=NT, k=2)))
            dve.tensor_copy(dcy[:, :, 0, :], cum[:, :, 0, :])
            dve.tensor_tensor(dcy[:, :, 1, :], cum[:, :, 1, :], cum[:, :, 0, :], ALU.subtract).then_inc(cum_sb, 1)
            splits(P_OUT_O + 2)
            dve.wait_ge(cum_sb, 1)
            dve.wait_ge(dcy_rdy, 1)
            link(dve.tensor_tensor(bec[:, :, :], beta[:, :, :], dcy[:, :, 0, :], ALU.mult))
            for g in range(8):
                dve.wait_ge(l2_sd, g + 1)
                norms = pm[:, g % 2].rearrange("p a b -> p (a b)")
                link(dve.reciprocal(norms, norms))
                pair = qkvT[:, 2 * g:2 * g + 2, :].rearrange("p a b -> p (a b)")
                dve.scalar_tensor_tensor(pair, pair, P ** -0.5 if g < 4 else 1.0, norms, ALU.mult, ALU.mult).then_inc(l2_done, 1)
            for t in range(NT):
                for b in range(2):
                    dve.wait_ge(kv_ps, 4 * t + 2 + b + 1)
                    dve.tensor_tensor(vb[:, t, 4 * b:4 * b + 4, :], ps[:, 4 * t + 2 + b, :].rearrange(
                        "p (c s) -> p c s", c=4), along(beta[:, t, 4 * b:4 * b + 4], P), ALU.mult).then_inc(vb_sb, 1)
            dve.wait_ge(kv_ps, 8)
            for t in range(NT):
                tok = slice(t * P, (t + 1) * P)
                u = 2 * t
                for g in range(2):
                    dve.wait_ge(rc_ps, u + g + 1)
                    for c in range(4):
                        hd = 4 * g + c
                        last = dve.tensor_scalar(AT[:, t, hd, :], ps[:, g, c * P:(c + 1) * P],
                                                 cum[:, t, 0, hd:hd + 1], 0.0, ALU.subtract, ALU.min)
                    last.then_inc(dd_rdy, 1)
                    dve.wait_ge(br_ps, u + g + 1)
                    if t == 0:
                        dve.wait_ge(l2_done, 8)
                    else:
                        dve.wait_ge(x_ps, 12)
                    dve.tensor_tensor(pm[:, g], kT[:, 4 * g:4 * g + 4, tok], ps[:, 2 + g, :].rearrange(
                        "p (c s) -> p c s", c=4), ALU.mult).then_inc(kb_rdy, 1)
                for g in range(2):
                    heads = slice(4 * g, 4 * g + 4)
                    dve.wait_ge(dec_exp, u + g + 1)
                    link(dve.tensor_tensor(AT[:, t, heads, :], AT[:, t, heads, :], over(upper, 4), ALU.mult))
                    dve.wait_ge(lt_ps, u + g + 1)
                    dve.tensor_tensor(LT[:, heads, :], ps[:, 4 + g, :].rearrange("p (c s) -> p c s", c=4),
                                      AT[:, t, heads, :], ALU.mult).then_inc(lt_sb, 1)
                    dve.wait_ge(at_ps, u + g + 1)
                    dve.wait_ge(lt_sb, u + g + 1)
                    dve.tensor_tensor(AT[:, t, heads, :], ps[:, 6 + g, :].rearrange("p (c s) -> p c s", c=4),
                                      AT[:, t, heads, :], ALU.mult).then_inc(at_sb, 1)
                for g in range(2):
                    dve.wait_ge(bt_rdy, LEVELS * u + g + 1)
                    dve.tensor_tensor(XT[:, t, 4 * g:4 * g + 4, :], over(ident, 4), bt[:, g], ALU.subtract).then_inc(x1_rdy, 1)
                for l in range(1, LEVELS):
                    for g in range(2):
                        heads = slice(4 * g, 4 * g + 4)
                        v = (LEVELS - 1) * u + 2 * (l - 1) + g
                        dve.wait_ge(x_ps, v + 1)
                        if l == 1:
                            dve.wait_ge(x1_rdy, u + g + 1)
                        else:
                            dve.wait_ge(x_sb, v - 1)
                        if l < LEVELS - 1:
                            dve.wait_ge(x1_sb, u + g + 1)
                            dve.tensor_tensor(X[:, heads, :], X[:, heads, :], ps[:, 4 + g, :].rearrange(
                                "p (c s) -> p c s", c=4), ALU.subtract)
                        dve.tensor_tensor(XT[:, t, heads, :], XT[:, t, heads, :], ps[:, 6 + g, :].rearrange(
                            "p (c s) -> p c s", c=4), ALU.subtract).then_inc(x_sb, 1)
                dve.wait_ge(p_ps, (LEVELS - 1) * (u + 2))
                scale = dcy[:, 0, 1, :] if t == 0 else bec[:, 1, :]
                dve.wait_ge(k_sb, 4)
                dve.tensor_tensor(kbe, ktok[:, t], along(scale, P), ALU.mult).then_inc(ksc_rdy, 1)
                if t == 1:
                    for g in range(2):
                        dve.wait_ge(qg_exp, g + 1)
                        dve.tensor_tensor(qgT[:, 4 * g:4 * g + 4, :], qgT[:, 4 * g:4 * g + 4, :],
                                          qT[:, 4 * g:4 * g + 4, tok], ALU.mult).then_inc(qg_rdy, 1)
                for g in range(2):
                    dve.wait_ge(od_ps, u + g + 1)
                    dve.tensor_copy(AT[:, t, 4 * g:4 * g + 4, :], ps[:, (2 if t == 0 else 4) + g, :].rearrange(
                        "p (c s) -> p c s", c=4)).then_inc(od_sb, 1)
            for t in range(NT):
                dve.wait_ge(od_ss, t + 1)
                last = dve.tensor_reduce(oss[:, 8 * t:8 * t + 8], odq[:, t], AX, ALU.add)
            last.then_inc(od_sd, 1)
            dve.wait_ge(od_sd, 2)
            link(dve.reciprocal(ors[:, :], osd[:, :]))
            for t in range(NT):
                dve.tensor_tensor(AT[:, t], AT[:, t], along(ors[:, 8 * t:8 * t + 8], P), ALU.mult).then_inc(dve_link, 1)
                count[0] += 1
            dve.wait_ge(dve_link, count[0])
            for t in range(NT):
                dve.tensor_tensor(AT[:, t], AT[:, t], zs[:, t, :].rearrange("p (h d) -> p h d", d=P), ALU.mult).then_inc(od_nrm, 1)
            for b in range(4):
                dve.wait_ge(odT_hi, b + 1)
                dve.scalar_tensor_tensor(xs_lo[:, 2 * b:2 * b + 2, :], ps[:, b, :].rearrange("p (c s) -> p c s", c=2),
                                         gT[:, G_ON:G_ON + 1], xs_hi[:, 2 * b:2 * b + 2, :].bitcast(F32),
                                         ALU.mult, ALU.subtract).then_inc(odT_lo, 1)
            for j in range(2):
                splits(P_OUT_O + 2 * j + 3)
                dve.wait_ge(piece_used, P_OUT_O + 2 * j + 2)
                for t in range(NT):
                    add_h(t, j, ps[:, 4 + 2 * j + t, :]).then_inc(h_ready, 1)

            dve.wait_ge(h_ready, H_AT[4])
            norm_hn(4)
            splits(P_MOE + 2)
            norm_lo(4)
            dve.wait_ge(gffn_in, 16)
            for t in range(NT):
                dve.tensor_tensor(hn[:, t, :], hn[:, t, :], gffn, ALU.mult).then_inc(m_hn, 1)
            dve.wait_ge(lg_ps, 1)
            link(dve.tensor_copy(r_l, ps[:, 4, 0:NT * NE].rearrange("p (t e) -> p t e", t=NT)))
            link(dve.tensor_reduce(r_mx, r_l, AX, ALU.max))
            dve.tensor_scalar(r_nmx, r_mx, -1.0, None, ALU.mult).then_inc(lg_max, 1)
            for t in range(NT):
                other, own = over(r_l[:, t, :], NE), along(r_l[:, t, :], NE)
                dve.tensor_tensor(r_gt[:, t, :].rearrange("p (e f) -> p e f", e=NE), other, own, ALU.is_gt)
                last = dve.tensor_tensor(r_eq[:, t, :].rearrange("p (e f) -> p e f", e=NE), other, own, ALU.is_equal)
            link(last)
            link(dve.tensor_tensor(r_eq, r_eq, over(con[:, C_LOW:C_LOW + NE * NE], NT), ALU.mult))
            link(dve.tensor_tensor(r_gt, r_gt, r_eq, ALU.add))
            link(dve.tensor_reduce(r_rank, r_gt.rearrange("p t (e f) -> p t e f", e=NE), AX, ALU.add))
            dve.tensor_scalar(r_m, r_rank, 1.5, None, ALU.is_lt).then_inc(mk_rdy, 1)
            dve.wait_ge(mk_rdy, 1)
            dve.wait_ge(lg_exp, 1)
            link(dve.tensor_tensor(r_e, r_e, r_m, ALU.mult))
            link(dve.tensor_reduce(r_s, r_e, AX, ALU.add))
            link(dve.reciprocal(r_rs, r_s))
            dve.memset(posb[:, :, :], -1.0)
            dve.memset(gateb[:, :, :], 0.0)
            link(dve.memset(blk_f, 0.0))
            link(dve.tensor_tensor(gateb[:, :, 0:NE], r_e, along(r_rs, NE), ALU.mult))
            dve.wait_ge(rk_ps, 1)
            dve.tensor_scalar(r_ov, ps[:, 5, 2 * NE:3 * NE], float(P) + 0.5, None, ALU.is_gt)
            link(dve.tensor_tensor(r_im, ps[:, 5, 0:NT * NE].rearrange("p (t e) -> p t e", t=NT), r_m, ALU.mult))
            dve.tensor_scalar(posb[:, :, 0:NE], r_im, -1.0, None, ALU.add)
            w3 = r_w.rearrange("p (e f) -> p e f", e=NE)
            link(dve.tensor_tensor(w3, con[:, C_LOW:C_LOW + NE * NE].rearrange("p (e f) -> p e f", e=NE),
                                   over(r_ov, NE), ALU.mult))
            link(dve.tensor_reduce(r_ord, w3, AX, ALU.add))
            for i in range(MAX_OVER):
                last = dve.tensor_scalar(r_sl[:, i, :], r_ord, float(i), None, ALU.is_equal)
            link(last)
            link(dve.tensor_tensor(r_sl, r_sl, over(r_ov, MAX_OVER), ALU.mult))
            for t in range(NT):
                last = dve.tensor_tensor(r_t[:, t], r_sl, over(r_im[:, t, :], MAX_OVER), ALU.mult)
            link(last)
            link(dve.tensor_reduce(posb[:, :, NE:NE + MAX_OVER], r_t, AX, ALU.add))
            link(dve.tensor_scalar(posb[:, :, NE:NE + MAX_OVER], posb[:, :, NE:NE + MAX_OVER], -1.0 - P, None, ALU.add))
            for t in range(NT):
                last = dve.tensor_tensor(r_t[:, t], r_sl, over(gateb[:, t, 0:NE], MAX_OVER), ALU.mult)
            link(last)
            link(dve.tensor_reduce(gateb[:, :, NE:NE + MAX_OVER], r_t, AX, ALU.add))
            link(dve.tensor_tensor(r_sl, r_sl, over(con[:, C_EID:C_EID + NE], MAX_OVER), ALU.mult))
            dve.tensor_reduce(blk_f[:, NE:NE + MAX_OVER], r_sl, AX, ALU.add)
            dve.tensor_copy(blk_f[:, 0:NE], con[:, C_EID:C_EID + NE])
            link(dve.tensor_reduce(blk_f[:, 15:16], r_ov, AX, ALU.add))
            link(dve.tensor_scalar(blk_f[:, 15:16], blk_f[:, 15:16], float(NE), None, ALU.add))
            dve.tensor_copy(blk_i[:, :], blk_f).then_inc(tab_rdy, 1)
            dve.wait_ge(tab_rdy, 1)
            nblk = dve.value_load(blk_i[0:1, 15:16], min_val=NE, max_val=NE + MAX_OVER)

            def select(b):
                for t in range(NT):
                    dve.tensor_scalar(sel[:, t, :], iota, posb[:, t, bass.ds(b, 1)], None, ALU.is_equal)
                    last = dve.tensor_scalar(selg[:, t, :], iota, posb[:, t, bass.ds(b, 1)], gateb[:, t, bass.ds(b, 1)],
                                             ALU.is_equal, ALU.mult)
                last.then_inc(m_sel, 1)

            def tokens_lo(done):
                for q in range(2):
                    dve.wait_ge(m_xhi, done + (q + 1))
                    dve.tensor_tensor(xg_lo[:, 4 * q:4 * q + 4, :], ps[:, 6 + q, :].rearrange("p (c s) -> p c s", c=4),
                                      xg_hi[:, 4 * q:4 * q + 4, :].bitcast(F32), ALU.subtract).then_inc(m_xlo, 1)

            select(0)
            tokens_lo(0)
            dve.engine_nop().then_inc(m_add, 1)
            with dve.Fori(0, nblk) as b:
                at = [SPLIT]

                def pieces(upto):
                    while at[0] <= upto:
                        split(at[0], b * PER_BLOCK + (P_MOE + at[0] + 1))
                        at[0] += 1

                for j in range(FJ):
                    i = MOE_AT[1, j, 1]
                    pieces(i + 2)
                    dve.wait_ge(piece_used, b * PER_BLOCK + (P_MOE + i + 1))
                    dve.wait_ge(m_silu, b * FJ + (j + 1))
                    dve.tensor_tensor(gated[:, j % 2, :], sil[:, j % 2, :], ps[:, 2 * (j % 2) + 1, :],
                                      ALU.mult).then_inc(m_gated, 1)
                    if j == 0:
                        dve.wait_ge(m_sT_ps, b + 1)
                        select(b + 1)
                    if j + 1 < FJ:
                        pieces(MOE_AT[0, j + 1, 1] + 2)
                    else:
                        pieces(MOE_AT[2, j - 1, 1] + 2)
                    dve.wait_ge(m_ghi, b * FJ + (j + 1))
                    dve.tensor_tensor(g_lo[:, j % 2, :], ps[:, 2 * (j % 2), :], g_hi[:, j % 2, :].bitcast(F32),
                                      ALU.subtract).then_inc(m_glo, 1)
                tokens_lo(b * 2 + 2)
                pieces(PER_BLOCK + 2)
                for t in range(NT):
                    for half in range(2):
                        dve.wait_ge(m_sc, b * 4 + (2 * t + half + 1))
                        add_h(t, half, ps[:, 2 + 4 * t + half, :]).then_inc(m_add, 1)

            dve.wait_ge(m_add, nblk * 4 + 1)
            norm_hn(5)
            tail = [SPLIT]

            def tail_pieces(upto):
                while tail[0] <= upto:
                    split(tail[0], nblk * PER_BLOCK + (P_MOE + tail[0] + 1), PIECE if tail[0] < 4 else D)
                    tail[0] += 1

            embed(1, tail_pieces, lambda i: dve.wait_ge(piece_used, nblk * PER_BLOCK + (P_MOE + i)))

            dve.wait_ge(h_ready, H_AT[6])
            dve.wait_ge(n_std, 7)
            link(dve.reciprocal(rstd[:, 6, :], std[:, 6, :]))
            dve.wait_ge(gfin_in, 16)
            for t in range(NT):
                dve.scalar_tensor_tensor(hn[:, t, :], h[:, t, :], rstd[:, 6, t:t + 1], gfin, ALU.mult, ALU.mult).then_inc(f_out, 1)


_INS = ["x", "p", "positions", "ln_mix", "ln_ffn", "ln_ple", "ln_final", "w_in_even", "w_out_even",
        "lam_q1", "lam_k1", "lam_q2", "lam_k2", "subln_gain", "conv_w_short", "w_in_odd", "conv_w_qkv",
        "a_log", "dt_bias", "onorm_gain", "w_out_odd", "w1_dense", "w3_dense", "w2_dense",
        "w_router", "w1_moe", "w3_moe", "w2_moe", "w_ple_gate", "w_ple_proj"]


def kernel(**inputs):
    import concourse.bacc as bacc
    from concourse.bass_utils import run_bass_kernel_spmd

    nc = bacc.Bacc("TRN2", target_bir_lowering=False, num_devices=1)
    arrays, aps = {}, {}
    for name in _INS + ["con"]:
        v = shape_constants() if name == "con" else np.ascontiguousarray(inputs[name])
        arrays[f"in_{name}"] = v
        aps[name] = nc.dram_tensor(f"in_{name}", v.shape, mybir.dt.from_np(v.dtype), kind="ExternalInput").ap()
    out = nc.dram_tensor("out", (1, SEQ, D), F32, kind="ExternalOutput").ap()
    trunk(nc, aps, out)
    r = run_bass_kernel_spmd(nc, [arrays], core_ids=[0])
    return r.results[0]["out"]
```

```python
import math
from contextlib import ExitStack

import numpy as np

import concourse.bass as bass
from concourse import mybir

F32 = mybir.dt.float32
F32R = mybir.dt.float32r
I32 = mybir.dt.int32
ALU = mybir.AluOpType
ACT = mybir.ActivationFunctionType
AX = mybir.AxisListType.X

P = 128
SEQ = 256
D = 1024
NT = SEQ // P
KC = D // P
RMS_EPS = 1e-6
SUBLN_EPS = 1e-5
HEADS_A = 4
DH = 64
ROT = 16
HALF_ROT = ROT // 2
ROPE_THETA = 500000.0
LAM0 = 0.8 - 0.6 * math.exp(0.0)
SC_TAPS = 3
DN_TAPS = 4
HEADS_D = 8
QKV_CHUNKS = 3 * HEADS_D
FF = 3584
FJ = FF // 512
NE = 8
MAX_OVER = 3
HALF_FJ = 2 * FJ
PIECE = 2048
RAW = 6
SPLIT = 3
PER_BLOCK = 6 * FJ
PLE = 256
NEG = -1.0e30
TWO_PI = (6.28125, 0.0019350051879882812, 2 * math.pi - 6.28125 - 0.0019350051879882812)
ROWS_IN = 16 * 7
SMALL_IN = 16 * 11
LEVELS = 7

C_ID, C_UP, C_ONE, C_IOTA, C_LEV = 0, 128, 256, 384, 512
C_FREQ = C_LEV + LEVELS * 128
C_EID = C_FREQ + HALF_ROT
C_LOW = C_EID + NE
C_W = C_LOW + NE * NE

P_QKV_E = 0
P_CONV_E = P_QKV_E + 6
P_OUT_E = P_CONV_E + 6
P_MLP = P_OUT_E + 4
P_PROJ_E = P_MLP + 3 * HALF_FJ
P_GATE_E = P_PROJ_E + 2
P_QKV_O = P_GATE_E + 4
P_Z = P_QKV_O + 12
P_OUT_O = P_Z + 4
P_MOE = P_OUT_O + 4
for ring in (RAW, SPLIT):
    assert P_MOE % ring == 0 and PER_BLOCK % ring == 0


def shape_constants():
    c = np.zeros((P, C_W), np.float32)
    i = np.arange(P)
    c[:, C_ID:C_ID + P] = np.eye(P)
    c[:, C_UP:C_UP + P] = i[:, None] <= i[None, :]
    c[:, C_ONE:C_ONE + P] = 1.0
    c[:, C_IOTA:C_IOTA + P] = i[None, :]
    for level in range(LEVELS):
        s = 1 << level
        rows, cols = i[:, None] // s, i[None, :] // s
        c[:, C_LEV + level * P:C_LEV + (level + 1) * P] = (cols % 2 == 1) & (rows == cols - 1)
    c[:, C_FREQ:C_FREQ + HALF_ROT] = np.float32(ROPE_THETA) ** (
        -np.arange(0, ROT, 2, dtype=np.float32) / np.float32(ROT))
    e = np.arange(NE)
    c[:, C_EID:C_EID + NE] = e
    c[:, C_LOW:C_LOW + NE * NE] = (e[None, :] < e[:, None]).reshape(-1)
    return c


def up_down_order(steps):
    order = [(0, 0), (1, 0)]
    for j in range(1, steps):
        order += [(0, j), (1, j), (2, j - 1)]
    return order + [(2, steps - 1)]


MLP_ORDER = up_down_order(HALF_FJ)
MLP_AT = {key: P_MLP + i for i, key in enumerate(MLP_ORDER)}
MOE_ORDER = [(m, j, part) for m, j in up_down_order(FJ) for part in range(2)]
MOE_AT = {key: i for i, key in enumerate(MOE_ORDER)}


def trunk(nc, a, out):
    ctx = ExitStack()
    with ctx:
        def sb(name, shape, dt=F32):
            return ctx.enter_context(nc.sbuf_tensor(name, shape, dt))

        def sem(name):
            return ctx.enter_context(nc.semaphore(name))

        raw = sb("raw", [P, RAW, PIECE])
        w_hi = sb("w_hi", [P, SPLIT, PIECE], F32R)
        w_lo = sb("w_lo", [P, SPLIT, PIECE], F32R)
        with ExitStack() as place:
            x_hi, x_lo = (place.enter_context(nc.sbuf_tensor(x, [P, KC * SEQ], F32R)) for x in ("x_hi", "x_lo"))
        second_hi = sb("second_hi", [P, KC * SEQ])
        second_lo = sb("second_lo", [P, KC * SEQ])
        h = sb("h", [P, NT, D])
        hn = sb("hn", [P, NT, D])
        con = sb("con", [P, C_W])
        wba = sb("wba", [P, KC, 2 * HEADS_D])
        wrt = sb("wrt", [P, KC, NE])
        wba_hi = sb("wba_hi", [P, KC, 2 * HEADS_D], F32R)
        wba_lo = sb("wba_lo", [P, KC, 2 * HEADS_D], F32R)
        wrt_hi = sb("wrt_hi", [P, KC, NE], F32R)
        wrt_lo = sb("wrt_lo", [P, KC, NE], F32R)
        gT = sb("gT", [P, 62])
        cwT = sb("cwT", [P, DN_TAPS * QKV_CHUNKS])
        alog = sb("alog", [P, HEADS_D])
        dtb = sb("dtb", [P, HEADS_D])
        ssq = sb("ssq", [P, 7, NT])
        std = sb("std", [P, 7, NT])
        rstd = sb("rstd", [P, 7, NT])
        eps6 = sb("eps6", [P, 1])
        eps5 = sb("eps5", [P, 3])
        posi = sb("posi", [P, NT + SEQ], I32)
        posc = sb("posc", [P, NT])
        cs = sb("cs", [P, 2, NT, HALF_ROT])
        lamd = sb("lamd", [P, 2])
        lame = sb("lame", [P, 2])
        nlam = sb("nlam", [P, 1])
        mx = sb("mx", [P, 2, 4])
        nb = sb("nb", [P, 2, 4])
        esum = sb("esum", [P, 2, 4])
        erc = sb("erc", [P, 2, 4])
        oss = sb("oss", [P, NT * HEADS_D])
        osd = sb("osd", [P, NT * HEADS_D])
        ors = sb("ors", [P, NT * HEADS_D])
        ba = sb("ba", [P, NT, 2 * HEADS_D])
        yneg = sb("yneg", [P, NT, 2 * HEADS_D])
        yexp = sb("yexp", [P, NT, 2 * HEADS_D])
        yln = sb("yln", [P, NT, HEADS_D])
        beta = sb("beta", [P, NT, HEADS_D])
        gdec = sb("gdec", [P, NT, HEADS_D])
        cum = sb("cum", [P, NT, 2, HEADS_D])
        dcy = sb("dcy", [P, NT, 2, HEADS_D])
        bec = sb("bec", [P, NT, HEADS_D])
        ealog = sb("ealog", [P, HEADS_D])
        l2n = yneg[:, :, :].rearrange("p t (q n) -> p t q n", q=2).rearrange("p t q n -> p q t n")
        l2f = ba[:, :, :].rearrange("p t (q n) -> p t q n", q=2).rearrange("p t q n -> p q t n")
        zero = eps5[:, 2:3]
        table = eps5[:, 1:2]
        NBC = NE + MAX_OVER + 1
        posb = sb("posb", [P, NT, NBC])
        gateb = sb("gateb", [P, NT, NBC])
        blk_i = sb("blk_i", [P, 16], I32)
        ps = ctx.enter_context(nc.psum_tensor("ps", [P, 8, 512], F32))

        def by_chunk(x, n=SEQ):
            return x[:, 0:KC * n].rearrange("p (k s) -> p k s", k=KC)

        xs_hi, xs_lo = by_chunk(x_hi), by_chunk(x_lo)
        ident = con[:, C_ID:C_ID + P]
        upper = con[:, C_UP:C_UP + P]
        ones = con[:, C_ONE:C_ONE + P]
        iota = con[:, C_IOTA:C_IOTA + P]

        def over(ap, n):
            return ap.unsqueeze(1).broadcast_to([P, n, ap.shape[-1]])

        def along(ap, n):
            return ap.unsqueeze(2).broadcast_to([P, ap.shape[-1], n])

        def level_mask(l):
            return con[:, C_LEV + l * P:C_LEV + (l + 1) * P]

        class Area:

            def __init__(self, name):
                self.name, self.n, self.held = name, 0, ExitStack()

            def take(self, *dims, dt=F32):
                self.n += 1
                size = int(np.prod(dims))
                v = self.held.enter_context(nc.sbuf_tensor(f"{self.name}{self.n}", [P, size], dt))[:, :]
                if len(dims) == 1:
                    return v
                names = "abcd"[:len(dims)]
                return v.rearrange(f"p ({' '.join(names)}) -> p {' '.join(names)}",
                                   **dict(zip(names[1:], dims[1:])))

            def close(self):
                self.held.close()

        G_MIX, G_FFN, G_PLE, G_SUB, G_ON, G_CW = 0, 16, 32, 48, 49, 50
        GAIN_AT = [G_MIX, G_FFN, G_PLE, G_MIX + KC, G_FFN + KC, G_PLE + KC]

        ar = Area("even")
        qk = ar.take(NT, 1024)
        vt = ar.take(NT, 512)
        qkT = ar.take(KC, SEQ)
        mix_c = ar.take(4, SEQ)
        cT = ar.take(4, SEQ)
        PADS = SC_TAPS - 1 + SEQ
        upad = ar.take(4, PADS)
        rt = ar.take(4, 16, HALF_ROT)
        sm = ar.take(2, 4, SEQ)
        adf = ar.take(2, NT, SEQ)
        maskb = ar.take(NT, SEQ)
        rows1 = ar.take(P)
        rows2 = ar.take(P)
        posrow = ar.take(SEQ)
        lamv = ar.take(4, DH)
        lamp = ar.take(2, DH)
        ang = ar.take(NT, HALF_ROT)
        turns = ar.take(NT, HALF_ROT)
        oat = qk[:, 0, :].rearrange("p (t h v) -> p t h v", t=NT, h=HEADS_A)
        osq = qk[:, 1, :].rearrange("p (t h v) -> p t h v", t=NT, h=HEADS_A)
        aTt = cT.rearrange("p (u k) s -> p u k s", u=2)
        ar.close()

        ar = Area("ff")
        sil = ar.take(2, 512)
        gated = ar.take(2, 512)
        g_hi = ar.take(2, 512, dt=F32R)
        g_lo = ar.take(2, 512, dt=F32R)
        sgm = hn
        ptmp = ar.take(2, 512)
        p_tok = ar.take(NT, PLE)
        p_hi = ar.take(2, SEQ, dt=F32R)
        p_lo = ar.take(2, SEQ, dt=F32R)
        gfin = ar.take(D)
        gffn = ar.take(D)
        xg_hi, xg_lo = by_chunk(x_hi, P), by_chunk(x_lo, P)
        hn_hi = ar.take(NT, D, dt=F32R)
        hn_lo = ar.take(NT, D, dt=F32R)
        y_hi = ar.take(D, dt=F32R)
        y_lo = ar.take(D, dt=F32R)
        sel = ar.take(NT, P, dt=F32R)
        selT = ar.take(SEQ, dt=F32R)
        gsel = ar.take(NT)
        gslot = ar.take(1)
        r_l = ar.take(NT, NE)
        r_gt = ar.take(NT, NE * NE)
        r_eq = ar.take(NT, NE * NE)
        r_rank = ar.take(NT, NE)
        r_m = ar.take(NT, NE)
        r_mx = ar.take(NT)
        r_nmx = ar.take(NT)
        r_e = ar.take(NT, NE)
        r_s = ar.take(NT)
        r_rs = ar.take(NT)
        r_im = ar.take(NT, NE)
        r_ov = ar.take(NE)
        r_w = ar.take(NE * NE)
        r_ord = ar.take(NE)
        r_sl = ar.take(MAX_OVER, NE)
        r_t = ar.take(NT, MAX_OVER, NE)
        blk_f = ar.take(16)
        ar.close()

        ar = Area("odd")
        qkvT = ar.take(QKV_CHUNKS, SEQ)
        PADW = DN_TAPS - 1 + SEQ
        upo_flat = ar.take(2 * 4 * PADW)
        upo = upo_flat.rearrange("p (a b c) -> p a b c", a=2, b=4)
        def and_in(first, x, at, names, **dims):
            return first, x[:, at:at + HEADS_D * P].rearrange(names, **dims)

        LT = and_in(ar.take(HEADS_D, P), second_hi, 0, "p (h s) -> p h s", h=HEADS_D)
        X = and_in(ar.take(HEADS_D, P), second_hi, 1024, "p (h s) -> p h s", h=HEADS_D)
        XT = ar.take(NT, HEADS_D, P)
        bt = and_in(ar.take(2, 4, P), second_lo, 0, "p (g c s) -> p g c s", g=2, c=4)
        pm = and_in(ar.take(2, 4, P), second_lo, 1024, "p (g c s) -> p g c s", g=2, c=4)
        S1 = ar.take(HEADS_D, P)
        vb = ar.take(NT, HEADS_D, P)
        ar.close()
        qT, kT = qkvT[:, 0:8, :], qkvT[:, 8:16, :]
        by_tok = dict(t=NT, h=HEADS_D)
        ktok = upo_flat[:, 0:NT * D].rearrange("p (t h d) -> p t h d", **by_tok)
        AT = qkvT[:, 16:24, :].rearrange("p a b -> p (a b)").rearrange("p (t h d) -> p t h d", **by_tok)
        odq = ktok
        un = [b.rearrange("p a b c -> p (a b) c") for b in bt]
        qgT = pm[1].rearrange("p a b c -> p (a b) c")
        nwT, kbe, zs = LT[1], X, hn

        def at_level(l, t, g):
            return 4 * (l - 1) + 2 * t + g + 1

        raw_in = [sem(f"raw_in{i}") for i in range(RAW)]
        hi_rdy, lo_rdy = sem("hi_rdy"), sem("lo_rdy")
        piece_used = sem("piece_used")
        small_hi, small_lo = sem("small_hi"), sem("small_lo")
        mix_hi, mix_lo = sem("mix_hi"), sem("mix_lo")
        x_in = [sem(f"x_in{t}") for t in range(NT)]
        id_in, rows_in, out_done = sem("id_in"), sem("rows_in"), sem("out_done")
        small_in = sem("small_in")
        p_in, gfin_in = sem("p_in"), sem("gfin_in")
        dve_link, act_link = sem("dve_link"), sem("act_link")
        h_ready = sem("h_ready")
        n_std, n_hn, n_ps, n_hi, n_lo = (sem(x) for x in ("n_std", "n_hn", "n_ps", "n_hi", "n_lo"))
        eps_set, st_ps, st_sb = sem("eps_set"), sem("st_ps"), sem("st_sb")
        ang_rdy, cs_rdy, lam_dot, lam_exp = sem("ang_rdy"), sem("cs_rdy"), sem("lam_dot"), sem("lam_exp")
        qkv_sb, v_sb, c_sb, xb_used, rope_done, mix_conv = (sem(x) for x in (
            "qkv_sb", "v_sb", "c_sb", "xb_used", "rope_done", "mix_conv"))
        qkT_ps, qkT_sb = sem("qkT_ps"), sem("qkT_sb")
        sc_ps, sm_read, sm_rdy, ex_done, a_done = (sem(x) for x in (
            "sc_ps", "sm_read", "sm_rdy", "ex_done", "a_done"))
        aT_ps, aT_sb, av_ps, o_sb, o_ss, o_sd, o_nrm, oT_ps = (sem(x) for x in (
            "aT_ps", "aT_sb", "av_ps", "o_sb", "o_ss", "o_sd", "o_nrm", "oT_ps"))
        silu_sb, gated_sb, gated_hi, gated_lo = sem("silu_sb"), sem("gated_sb"), sem("gated_hi"), sem("gated_lo")
        pT_ps, pT_hi, pT_lo, sgm_sb = sem("pT_ps"), sem("pT_hi"), sem("pT_lo"), sem("sgm_sb")
        ba_ps, ba_neg, ba_exp, ba_ln, g_rdy, cum_ps, cum_sb, dcy_rdy = (sem(x) for x in (
            "ba_ps", "ba_neg", "ba_exp", "ba_ln", "g_rdy", "cum_ps", "cum_sb", "dcy_rdy"))
        q_pad, cv_done, cv_silu, z_sb, pad_zero = (sem(x) for x in (
            "q_pad", "cv_done", "cv_silu", "z_sb", "pad_zero"))
        l2_sq, l2_ps, l2_sd, l2_fac, l2_bc, l2_done = (sem(x) for x in (
            "l2_sq", "l2_ps", "l2_sd", "l2_fac", "l2_bc", "l2_done"))
        kv_ps, k_sb, vb_sb = sem("kv_ps"), sem("k_sb"), sem("vb_sb")
        rc_ps, dd_rdy, dec_exp, br_ps, kb_rdy, lt_ps, lt_sb, at_ps, at_sb = (sem(x) for x in (
            "rc_ps", "dd_rdy", "dec_exp", "br_ps", "kb_rdy", "lt_ps", "lt_sb", "at_ps", "at_sb"))
        bt_rdy, x1_rdy, x1_ps, x1_sb, p_ps, p_sb, x_ps, x_sb = (sem(x) for x in (
            "bt_rdy", "x1_rdy", "x1_ps", "x1_sb", "p_ps", "p_sb", "x_ps", "x_sb"))
        ksc_rdy, w_ps, w_sb, u_ps, u_sb, od_ps, od_sb, s_ps, s_sb, qg_ps, qg_exp, qg_rdy = (
            sem(x) for x in ("ksc_rdy", "w_ps", "w_sb", "u_ps", "u_sb", "od_ps", "od_sb", "s_ps",
                             "s_sb", "qg_ps", "qg_exp", "qg_rdy"))
        od_sum = sem("od_sum")
        od_ss, od_sd, od_nrm, odT_ps, odT_hi, odT_lo = (sem(x) for x in (
            "od_ss", "od_sd", "od_nrm", "odT_ps", "odT_hi", "odT_lo"))
        lg_ps, lg_max, lg_exp, mk_rdy, rk_ps, tab_rdy = (sem(x) for x in (
            "lg_ps", "lg_max", "lg_exp", "mk_rdy", "rk_ps", "tab_rdy"))
        m_sel, m_xg_ps, m_xhi, m_xlo, m_sT_ps, m_sT = (sem(x) for x in (
            "m_sel", "m_xg_ps", "m_xhi", "m_xlo", "m_sT_ps", "m_sT"))
        m_silu, m_gated, m_gTps, m_ghi, m_glo, m_ysb, m_sc, m_add = (sem(x) for x in (
            "m_silu", "m_gated", "m_gTps", "m_ghi", "m_glo", "m_ysb", "m_sc", "m_add"))
        gffn_in, m_hn, m_hhi, m_hlo, m_y0, m_yhi = (sem(x) for x in ("gffn_in", "m_hn", "m_hhi", "m_hlo", "m_y0", "m_yhi"))
        f_out = sem("f_out")

        H_AT = {1: (3, 4), 2: (6, 8), 3: (11, 12), 4: (15, 16), 6: (19, 20)}
        H_MOE = (3, 4)
        N_BANK = (0, 4, 4, 4, 0, 4)

        def part_k(w, j, half):
            return w.rearrange("(k p) n -> p k n", p=P)[:, 4 * half:4 * half + 4, j * 512:(j + 1) * 512]

        def part_n(w, j):
            return w.rearrange("(k p) n -> p k n", p=P)[:, :, j * SEQ:(j + 1) * SEQ]

        def part_rows(w, j):
            return w.rearrange("(k p) n -> p k n", p=P)[:, 2 * j:2 * j + 2, :]

        def split_of(n, width):
            return tuple(w[:, n % SPLIT, :].rearrange("p (k n) -> p k n", n=width) for w in (w_hi, w_lo))

        wie, woe, wio, woo = a["w_in_even"][0], a["w_out_even"][0], a["w_in_odd"][0], a["w_out_odd"][0]
        gate_w = [[part_k(a["w_ple_gate"][i], j, half) for j in range(2) for half in range(2)] for i in range(2)]
        proj_w = [[a["w_ple_proj"][i].rearrange("(k p) n -> p k n", p=P)[:, c:c + 1, :] for c in range(2)]
                  for i in range(2)]
        static = [part_k(wie, j, half) for j in range(3) for half in range(2)]
        static += [part_n(wie, 2 * j + half) for j in (4, 5, 3) for half in range(2)]
        static += [part_k(woe, j, half) for j in range(2) for half in range(2)]
        for m, j in MLP_ORDER:
            w = a[("w1_dense", "w3_dense", "w2_dense")[m]][0]
            static.append(part_n(w, j) if m < 2 else part_rows(w, j))
        static += proj_w[0] + gate_w[0]
        static += [part_n(wio, j) for j in range(12)]
        static += [part_k(wio, j, half) for j in (6, 7) for half in range(2)]
        static += [part_k(woo, j, half) for j in range(2) for half in range(2)]
        assert len(static) == P_MOE

        block = ctx.enter_context(nc.Block())

        @block.sync
        def _(sp):
            def put(n, src):
                dst = raw[:, n % RAW, 0:src.shape[1] * src.shape[2]].rearrange("p (k n) -> p k n", n=src.shape[2])
                sp.dma_start(dst, src).then_inc(raw_in[n % RAW], 16)

            small = [(lamv[:, i, :], a[w].broadcast_to([P, DH])) for i, w in enumerate(("lam_q1", "lam_k1", "lam_q2", "lam_k2"))]
            small += [
                (con[:, P:], a["con"][:, P:]),
                (posi[:, 0:NT], a["positions"].rearrange("o (t p) -> p (o t)", p=P)),
                (posi[:, NT:NT + SEQ], a["positions"].broadcast_to([P, SEQ])),
                (alog[:, :], a["a_log"].broadcast_to([P, HEADS_D])),
                (dtb[:, :], a["dt_bias"].broadcast_to([P, HEADS_D])),
                (wba[:, :, :], wio[:, 4 * 1024:4 * 1024 + 2 * HEADS_D].rearrange("(k p) n -> p k n", p=P)),
                (wrt[:, :, :], a["w_router"][0].rearrange("(k p) n -> p k n", p=P)),
            ]
            assert 16 * len(small) == SMALL_IN
            x_v = a["x"][0].rearrange("(t p) d -> p t d", p=P)
            rows = [
                (rows1[0:16, :], a["ln_mix"].rearrange("i (k p) -> (i k) p", p=P)),
                (rows1[16:32, :], a["ln_ffn"].rearrange("i (k p) -> (i k) p", p=P)),
                (rows1[32:48, :], a["ln_ple"].rearrange("i (k p) -> (i k) p", p=P)),
                (rows1[48:49, :], a["subln_gain"]),
                (rows1[49:50, :], a["onorm_gain"]),
                (rows1[50:62, :], a["conv_w_short"].rearrange("o j (m p) -> (o j m) p", p=P)),
                (rows2[0:96, :], a["conv_w_qkv"].rearrange("o j (m p) -> (o j m) p", p=P)),
            ]
            assert 16 * len(rows) == ROWS_IN
            sp.dma_start(h[:, 0, :], x_v[:, 0, :]).then_inc(x_in[0], 16)
            sp.dma_start(h[:, 1, :], x_v[:, 1, :]).then_inc(x_in[1], 16)
            sp.dma_start(con[:, 0:P], a["con"][:, 0:P]).then_inc(id_in, 16)
            for dst, src in rows:
                sp.dma_start(dst, src).then_inc(rows_in, 16)
            for n, src in enumerate(static):
                if n == 3:
                    for dst, at in small:
                        sp.dma_start(dst, at, allow_slow_non_contiguous=True).then_inc(small_in, 16)
                if n >= RAW:
                    sp.wait_ge(lo_rdy, n - RAW + 1)
                put(n, src)

            def expert_piece(e, i):
                m, j, part = MOE_ORDER[i]
                w = a[("w1_moe", "w3_moe", "w2_moe")[m]].rearrange("o e (k p) n -> p (o e) k n", p=P)
                w = w[:, bass.ds(e, 1)]
                if m < 2:
                    w = w[:, :, 4 * part:4 * part + 4, j * 512:(j + 1) * 512]
                else:
                    w = w[:, :, 4 * j + 2 * part:4 * j + 2 * part + 2, :]
                return w.rearrange("p o k n -> p (o k) n")

            for i in range(PER_BLOCK):
                sp.wait_ge(lo_rdy, P_MOE + i - RAW + 1)
                put(i, expert_piece(0, i))
            sp.wait_ge(tab_rdy, 1)
            nblk = sp.value_load(blk_i[0:1, 15:16], min_val=NE, max_val=NE + MAX_OVER)
            with sp.Fori(1, nblk) as b:
                e = sp.value_load(blk_i[0:1, bass.ds(b, 1)], min_val=0, max_val=NE - 1)
                for i in range(PER_BLOCK):
                    sp.wait_ge(lo_rdy, b * PER_BLOCK + (P_MOE + i - RAW + 1))
                    put(i, expert_piece(e, i))
            for i, src in enumerate(proj_w[1] + gate_w[1]):
                sp.wait_ge(lo_rdy, nblk * PER_BLOCK + (P_MOE + i - RAW + 1))
                put(i, src)
            out_v = out.rearrange("o (t p) d -> p (o t) d", p=P)
            for t in range(NT):
                sp.wait_ge(f_out, t + 1)
                sp.dma_start(out_v[:, t, :], hn[:, t, :]).then_inc(out_done, 16)
            sp.wait_ge(out_done, 16 * NT)

        @block.tensor
        def _(pe):
            def split_wait(n):
                pe.wait_ge(lo_rdy, n + 1)

            def product(acc, lhs, rhs, first, final):
                (lh, ll), (rh, rl) = lhs, rhs
                pe.matmul(acc, lh, rh, start=first, stop=False)
                pe.matmul(acc, lh, rl, start=False, stop=False)
                return pe.matmul(acc, ll, rh, start=False, stop=final)

            def first(norm, k):
                if norm is not None:
                    pe.wait_ge(n_lo, KC * norm + k + 1)

            def tokens_out(banks, x, n, half, tiles=NT, norm=None):
                wh, wl = split_of(n, 512)
                for t in range(tiles):
                    for k in range(4):
                        if t == 0:
                            first(norm, 4 * half + k)
                        xk = tuple(v[:, 4 * half + k, t * P:(t + 1) * P] for v in x)
                        last = product(ps[:, banks[t], :], xk, (wh[:, k, :], wl[:, k, :]),
                                       half == 0 and k == 0, half == 1 and k == 3)
                last.then_inc(piece_used, 1)

            def channels_out(bank, n, norm=None):
                wh, wl = split_of(n, SEQ)
                for c in range(2):
                    for k in range(KC):
                        if c == 0:
                            first(norm, k)
                        last = product(ps[:, bank, c * SEQ:(c + 1) * SEQ],
                                       (wh[:, k, c * P:(c + 1) * P], wl[:, k, c * P:(c + 1) * P]),
                                       (xs_hi[:, k, :], xs_lo[:, k, :]), k == 0, k == KC - 1)
                last.then_inc(piece_used, 1)

            def both_tokens_out(banks, n, norm=None):
                for half in range(2):
                    split_wait(n + half)
                    tokens_out(banks, (xs_hi, xs_lo), n + half, half, norm=norm)

            def turn(bank, src, done):
                for c in range(4):
                    last = pe.transpose(ps[:, bank, c * P:(c + 1) * P], src[:, c * P:(c + 1) * P], ident)
                last.then_inc(done, 1)

            def norm_x(n):
                for t in range(NT):
                    pe.wait_ge(n_hn, NT * n + t + 1)
                    for k in range(KC):
                        at = (k % 2) * SEQ + t * P
                        last = pe.transpose(ps[:, N_BANK[n] + k // 2, at:at + P], hn[:, t, k * P:(k + 1) * P], ident)
                        if t == NT - 1 and k % 2:
                            last.then_inc(n_ps, 1)

            pe.wait_ge(id_in, 16)
            pe.wait_ge(rows_in, ROWS_IN)
            pe.transpose(ps[:, 4, 0:62], rows1[0:62, :], ident[0:62, 0:62])
            pe.transpose(ps[:, 4, 128:224], rows2[0:96, :], ident[0:96, 0:96]).then_inc(st_ps, 1)

            norm_x(0)
            pe.wait_ge(st_sb, 2)
            both_tokens_out((4, 5), P_QKV_E, norm=0)
            both_tokens_out((6, 7), P_QKV_E + 2)
            both_tokens_out((0, 1), P_QKV_E + 4)
            for m in range(2):
                split_wait(P_CONV_E + m)
                channels_out(2 + m, P_CONV_E + m)
            pe.wait_ge(rope_done, NT)
            pe.wait_ge(qkv_sb, 4)
            for b in range(4):
                for c in (2 * b, 2 * b + 1):
                    for t in range(NT):
                        at = (c % 2) * SEQ + t * P
                        last = pe.transpose(ps[:, 4 + b, at:at + P], qk[:, t, c * P:(c + 1) * P], ident)
                last.then_inc(qkT_ps, 1)

            def scores(hd):
                for m in range(2):
                    for t in range(NT):
                        last = pe.matmul(ps[:, 2 * (hd % 2) + m, t * SEQ:(t + 1) * SEQ],
                                         qkT[DH * m:DH * (m + 1), hd, t * P:(t + 1) * P],
                                         qkT[DH * m:DH * (m + 1), 4 + hd, :], start=True, stop=True)
                last.then_inc(sc_ps, 1)

            def conv_piece(i):
                split_wait(P_CONV_E + i)
                if i >= 4:
                    pe.wait_ge(xb_used, i - 3)
                channels_out(6 + i % 2, P_CONV_E + i)

            pe.wait_ge(qkT_sb, 4)
            pe.wait_ge(v_sb, 2)
            scores(0)
            conv_piece(2)
            pe.wait_ge(c_sb, 2)
            scores(1)
            conv_piece(3)
            for hd in range(HEADS_A):
                pe.wait_ge(a_done, hd + 1)
                if hd >= 1:
                    pe.wait_ge(aT_sb, hd)
                for kt in range(NT):
                    for t in range(NT):
                        at = kt * SEQ + t * P
                        last = pe.transpose(ps[:, 4, at:at + P], adf[:, hd % 2, t, kt * P:(kt + 1) * P], ident)
                last.then_inc(aT_ps, 1)
                if hd + 2 < HEADS_A:
                    pe.wait_ge(sm_read, 2 * (hd + 1))
                    scores(hd + 2)
                    conv_piece(4 + hd)
                pe.wait_ge(aT_sb, hd + 1)
                if hd >= 1:
                    pe.wait_ge(o_sb, hd)
                for t in range(NT):
                    for kt in range(NT):
                        last = pe.matmul(ps[:, 5, t * P:(t + 1) * P],
                                         aTt[:, hd % 2, kt, t * P:(t + 1) * P],
                                         vt[:, kt, hd * P:(hd + 1) * P], start=(kt == 0), stop=(kt == NT - 1))
                last.then_inc(av_ps, 1)
            pe.wait_ge(o_nrm, 1)
            for b in range(2):
                for hd in (2 * b, 2 * b + 1):
                    for t in range(NT):
                        at = (hd % 2) * SEQ + t * P
                        last = pe.transpose(ps[:, 4 + b, at:at + P], oat[:, t, hd, :], ident)
                last.then_inc(oT_ps, 1)
            pe.wait_ge(mix_lo, 3)
            for j in range(2):
                both_tokens_out((2 * j, 2 * j + 1), P_OUT_E + 2 * j)

            norm_x(1)

            def turn_p(i):
                pe.wait_ge(p_in, 16 * (i + 1))
                for c in range(2):
                    for t in range(NT):
                        last = pe.transpose(ps[:, 1, c * SEQ + t * P:c * SEQ + (t + 1) * P],
                                            p_tok[:, t, c * P:(c + 1) * P], ident)
                last.then_inc(pT_ps, 1)

            def hidden(m, s, norm=None):
                split_wait(MLP_AT[m, s])
                channels_out(2 * (s % 2) + m, MLP_AT[m, s], norm=norm)

            hidden(0, 0, norm=1)
            hidden(1, 0)
            for s in range(HALF_FJ):
                if s + 1 < HALF_FJ:
                    hidden(0, s + 1)
                    hidden(1, s + 1)
                n = MLP_AT[2, s]
                split_wait(n)
                pe.wait_ge(gated_lo, s + 1)
                if s == HALF_FJ - 1:
                    turn_p(0)
                wh, wl = split_of(n, D)
                for c in range(2):
                    for t in range(NT):
                        at = c * SEQ + t * P
                        for half in range(2):
                            cut = slice(half * 512, (half + 1) * 512)
                            last = product(ps[:, 4 + 2 * t + half, :],
                                           (g_hi[:, s % 2, at:at + P], g_lo[:, s % 2, at:at + P]),
                                           (wh[:, c, cut], wl[:, c, cut]),
                                           s == 0 and c == 0, s == HALF_FJ - 1 and c == 1)
                last.then_inc(piece_used, 1)

            def embed(i, wait_piece, wait_h=None):
                pe.wait_ge(pT_lo, i + 1)
                for c in range(2):
                    wait_piece(c)
                    wh, wl = (w[:, (P_PROJ_E * (1 - i) + c) % SPLIT, 0:D] for w in (w_hi, w_lo))
                    for j in range(2):
                        if c == 0 and j == 1 and wait_h is not None:
                            wait_h()
                        cut = slice(j * 512, (j + 1) * 512)
                        for t in range(NT):
                            tok = slice(t * P, (t + 1) * P)
                            last = product(ps[:, 2 * j + t, :], (p_hi[:, c, tok], p_lo[:, c, tok]),
                                           (wh[:, cut], wl[:, cut]), c == 0, c == 1)
                    last.then_inc(piece_used, 1)
                norm_x(2 + 3 * i)
                pe.wait_ge(n_lo, KC * (2 + 3 * i) + 2)
                for j in range(2):
                    for half in range(2):
                        wait_piece(2 + 2 * j + half)
                        tokens_out((4 + 2 * j, 5 + 2 * j), (xs_hi, xs_lo), P_GATE_E * (1 - i) + 2 * i + 2 * j + half,
                                   half, norm=2 + 3 * i if j == 0 else None)

            embed(0, lambda i: split_wait(P_PROJ_E + i))

            norm_x(3)
            pe.wait_ge(small_lo, 2)

            def small_product(norm, bank, width, wh, wl, done):
                for t in range(NT):
                    for k in range(KC):
                        if t == 0:
                            first(norm, k)
                        tok = slice(t * P, (t + 1) * P)
                        last = product(ps[:, bank, t * width:(t + 1) * width], (xs_hi[:, k, tok], xs_lo[:, k, tok]),
                                       (wh[:, k, :], wl[:, k, :]), k == 0, k == KC - 1)
                last.then_inc(done, 1)

            small_product(3, 3, 2 * HEADS_D, wba_hi, wba_lo, ba_ps)

            def l2_sum(g):
                pe.wait_ge(l2_sq, g + 1)
                squares = bt[0][:, g % 2].rearrange("p a b -> p (a b)")
                for c in range(2):
                    for t in range(NT):
                        at = t * 8 + (2 * g + c) % 8
                        last = pe.matmul(ps[:, 4 + g // 4, at:at + 1], squares[:, c * SEQ + t * P:c * SEQ + (t + 1) * P],
                                         ones[:, 0:1], start=True, stop=True)
                last.then_inc(l2_ps, 1)

            def l2_spread(i):
                pe.wait_ge(l2_fac, i + 1)
                for g in range(4 * i, 4 * i + 4):
                    if g >= 4:
                        pe.wait_ge(l2_done, g - 3)
                    for c in range(2):
                        for t in range(NT):
                            hd = (2 * g + c) % 8
                            last = pe.matmul(ps[:, g % 4, c * SEQ + t * P:c * SEQ + (t + 1) * P],
                                             l2f[:, i, t, hd:hd + 1].broadcast_to([P, P]), ident, start=True, stop=True)
                    last.then_inc(l2_bc, 1)

            for n in range(12):
                split_wait(P_QKV_O + n)
                if n == 3:
                    pe.wait_ge(ba_neg, 1)
                if n >= 4:
                    pe.wait_ge(q_pad, n - 3)
                channels_out(n % 4, P_QKV_O + n)
                if n == 5:
                    pe.wait_ge(g_rdy, 1)
                    for t in range(NT):
                        pe.matmul(ps[:, 7, t * 16:t * 16 + 8], upper, gdec[:, t, :], start=True, stop=True)
                        last = pe.matmul(ps[:, 7, t * 16 + 8:t * 16 + 16], ones, gdec[:, t, :], start=True, stop=True)
                    last.then_inc(cum_ps, 1)
                if 6 <= n < 10:
                    l2_sum(n - 6)
                if n >= 10:
                    l2_sum(2 * n - 16)
                    l2_sum(2 * n - 15)
            pe.wait_ge(q_pad, 12)
            l2_spread(0)
            pe.wait_ge(l2_sd, 2)
            both_tokens_out((4, 5), P_Z)
            l2_spread(1)
            pe.wait_ge(cum_sb, 1)
            both_tokens_out((6, 7), P_Z + 2)
            pe.wait_ge(cv_silu, 6)
            pe.wait_ge(l2_done, 8)
            for t in range(NT):
                if t == 1:
                    pe.wait_ge(z_sb, 4)
                for b in (2, 3, 0, 1):
                    for c in range(4):
                        hd = 4 * b + c
                        last = pe.transpose(ps[:, 4 * t + b, c * P:(c + 1) * P],
                                            qkvT[:, 8 + hd, t * P:(t + 1) * P], ident)
                    last.then_inc(kv_ps, 1)

            def head_cols(bank, c):
                return ps[:, bank, c * P:(c + 1) * P]

            for t in range(NT):
                tok = slice(t * P, (t + 1) * P)
                u = 2 * t
                if t == 0:
                    pe.wait_ge(k_sb, 4)
                    pe.wait_ge(vb_sb, 4)
                for g in range(2):
                    if t == 1:
                        pe.wait_ge(dd_rdy, g + 1)
                    for c in range(4):
                        last = pe.matmul(head_cols(g, c), gdec[:, t, 4 * g + c:4 * g + c + 1].broadcast_to([P, P]),
                                         upper, start=True, stop=True)
                    last.then_inc(rc_ps, 1)
                    if t == 1:
                        pe.wait_ge(kb_rdy, g + 1)
                    for c in range(4):
                        last = pe.matmul(head_cols(2 + g, c), beta[:, t, 4 * g + c:4 * g + c + 1].broadcast_to([P, P]),
                                         ident, start=True, stop=True)
                    last.then_inc(br_ps, 1)
                for g in range(2):
                    if t == 1:
                        pe.wait_ge(at_sb, g + 1)
                    for c in range(4):
                        last = pe.matmul(head_cols(6 + g, c), kT[:, 4 * g + c, tok], qT[:, 4 * g + c, tok],
                                         start=True, stop=True)
                    last.then_inc(at_ps, 1)
                for g in range(2):
                    if t == 1:
                        pe.wait_ge(lt_sb, g + 1)
                    pe.wait_ge(kb_rdy, u + g + 1)
                    for c in range(4):
                        last = pe.matmul(head_cols(4 + g, c), kT[:, 4 * g + c, tok], pm[t][:, g, c, :],
                                         start=True, stop=True)
                    last.then_inc(lt_ps, 1)
            for t in range(NT):
                for g in range(2):
                    pe.wait_ge(x1_rdy, 2 * t + g + 1)
                    pe.wait_ge(dd_rdy if t == 0 else kb_rdy, 2 + g + 1)
                    for c in range(4):
                        last = pe.transpose(head_cols(2 * t + g, c), XT[:, t, 4 * g + c, :], ident)
                    last.then_inc(x1_ps, 1)
            for l in range(1, LEVELS):
                for t in range(NT):
                    for g in range(2):
                        pe.wait_ge(bt_rdy, at_level(l + 1, t, g))
                        if l == 1:
                            pe.wait_ge(x1_sb, 2 * t + g + 1)
                        else:
                            pe.wait_ge(x_sb, at_level(l - 1, t, g))
                        for c in range(4):
                            last = pe.matmul(head_cols(2 * t + g, c), bt[t][:, g, c, :], X[t][:, 4 * g + c, :],
                                             start=True, stop=True)
                        last.then_inc(p_ps, 1)
                for t in range(NT):
                    for g in range(2):
                        if l == 1 and t == 0:
                            pe.wait_ge(at_sb, 2 + g + 1)
                            pe.wait_ge(lt_sb, 2 + g + 1)
                        else:
                            pe.wait_ge(x_sb, at_level(l, t, g) - 2)
                        pe.wait_ge(p_sb, at_level(l, t, g))
                        for c in range(4):
                            last = pe.matmul(head_cols(6 + g, c), pm[t][:, g, c, :], XT[:, t, 4 * g + c, :],
                                             start=True, stop=True)
                        if l < LEVELS - 1:
                            for c in range(4):
                                last = pe.matmul(head_cols(4 + g, c), XT[:, t, 4 * g + c, :], pm[t][:, g, c, :],
                                                 start=True, stop=True)
                        last.then_inc(x_ps, 1)
            for g in range(2):
                pe.wait_ge(x_sb, at_level(LEVELS - 1, 0, g))
                for c in range(4):
                    last = pe.matmul(head_cols(g, c), XT[:, 0, 4 * g + c, :], vb[:, 0, 4 * g + c, :],
                                     start=True, stop=True)
                last.then_inc(u_ps, 1)
            pe.wait_ge(ksc_rdy, 2)
            for g in range(2):
                pe.wait_ge(x_sb, at_level(LEVELS - 1, 1, g))
                for c in range(4):
                    last = pe.matmul(head_cols(6 + g, c), kbe[1][:, 4 * g + c, :], XT[:, 1, 4 * g + c, :],
                                     start=True, stop=True)
                last.then_inc(w_ps, 1)
            for g in range(2):
                pe.wait_ge(u_sb, g + 1)
                for c in range(4):
                    last = pe.matmul(head_cols(4 + g, c), kbe[0][:, 4 * g + c, :], un[0][:, 4 * g + c, :],
                                     start=True, stop=True)
                last.then_inc(s_ps, 1)
            for g in range(2):
                for c in range(4):
                    last = pe.matmul(head_cols(2 + g, c), AT[:, 0, 4 * g + c, :], un[0][:, 4 * g + c, :],
                                     start=True, stop=True)
                last.then_inc(od_ps, 1)
            for g in range(2):
                for c in range(4):
                    last = pe.matmul(head_cols(g, c), gdec[:, 1, 4 * g + c:4 * g + c + 1].broadcast_to([P, P]),
                                     upper, start=True, stop=True)
                last.then_inc(qg_ps, 1)
            for g in range(2):
                pe.wait_ge(w_sb, g + 1)
                pe.wait_ge(s_sb, g + 1)
                for c in range(4):
                    hd = 4 * g + c
                    pe.matmul(head_cols(6 + g, c), XT[:, 1, hd, :], vb[:, 1, hd, :], start=True, stop=False)
                    last = pe.matmul(head_cols(6 + g, c), nwT[:, hd, :], S1[:, hd, :], start=False, stop=True)
                last.then_inc(u_ps, 1)
            for g in range(2):
                pe.wait_ge(u_sb, 2 + g + 1)
                pe.wait_ge(qg_rdy, g + 1)
                for c in range(4):
                    hd = 4 * g + c
                    pe.matmul(head_cols(4 + g, c), qgT[:, hd, :], S1[:, hd, :], start=True, stop=False)
                    last = pe.matmul(head_cols(4 + g, c), AT[:, 1, hd, :], un[1][:, hd, :], start=False, stop=True)
                last.then_inc(od_ps, 1)
            for t in range(NT):
                pe.wait_ge(od_nrm, t + 1)
                for hd in range(HEADS_D):
                    at = (hd % 2) * SEQ + t * P
                    last = pe.transpose(ps[:, hd // 2, at:at + P], AT[:, t, hd, :], ident)
                    if t == NT - 1 and hd % 2:
                        last.then_inc(odT_ps, 1)
            pe.wait_ge(odT_lo, 4)
            for j in range(2):
                both_tokens_out((4 + 2 * j, 5 + 2 * j), P_OUT_O + 2 * j)

            norm_x(4)
            small_product(4, 4, NE, wrt_hi, wrt_lo, lg_ps)
            pe.wait_ge(mk_rdy, 1)
            pe.matmul(ps[:, 5, 0:NE], upper, r_m[:, 0, :], start=True, stop=True)
            pe.matmul(ps[:, 5, NE:2 * NE], ones, r_m[:, 0, :], start=True, stop=False)
            pe.matmul(ps[:, 5, NE:2 * NE], upper, r_m[:, 1, :], start=False, stop=True)
            pe.matmul(ps[:, 5, 2 * NE:3 * NE], ones, r_m[:, 0, :], start=True, stop=False)
            pe.matmul(ps[:, 5, 2 * NE:3 * NE], ones, r_m[:, 1, :], start=False, stop=True).then_inc(rk_ps, 1)

            def gather():
                for q in range(2):
                    for c in range(4):
                        for t in range(NT):
                            tok = slice((4 * q + c) * P, (4 * q + c + 1) * P)
                            pe.matmul(ps[:, 6 + q, c * P:(c + 1) * P], hn_hi[:, t, tok], sel[:, t, :],
                                      start=(t == 0), stop=False)
                            last = pe.matmul(ps[:, 6 + q, c * P:(c + 1) * P], hn_lo[:, t, tok], sel[:, t, :],
                                             start=False, stop=(t == NT - 1))
                    last.then_inc(m_xg_ps, 1)

            def scatter(b):
                for half in range(2):
                    pe.wait_ge(m_ysb, b * 2 + (half + 1))
                    cut = slice(half * 512, (half + 1) * 512)
                    for t in range(NT):
                        tok = slice(t * P, (t + 1) * P)
                        pe.matmul(ps[:, 2 + 4 * t + half, :], selT[:, tok], y_hi[:, cut], start=True, stop=False)
                        pe.matmul(ps[:, 2 + 4 * t + half, :], selT[:, tok], y_lo[:, cut],
                                  start=False, stop=True).then_inc(m_sc, 1)

            pe.wait_ge(m_hlo, NT)
            pe.wait_ge(m_sel, 1)
            gather()
            pe.wait_ge(tab_rdy, 1)
            nblk = pe.value_load(blk_i[0:1, 15:16], min_val=NE, max_val=NE + MAX_OVER)
            with pe.Fori(0, nblk) as b:
                def ready(i):
                    pe.wait_ge(lo_rdy, b * PER_BLOCK + (P_MOE + i + 1))

                def up(m, j):
                    for half in range(2):
                        i = MOE_AT[m, j, half]
                        ready(i)
                        tokens_out((2 * (j % 2) + m,), (xg_hi, xg_lo), i, half, 1)

                pe.wait_ge(m_xlo, b * 2 + 2)
                up(0, 0)
                scatter(b)
                up(1, 0)
                pe.wait_ge(m_add, b * 4 + 4)
                for t in range(NT):
                    pe.transpose(ps[:, 6, t * P:(t + 1) * P], sel[:, t, :].bitcast(F32), ident)
                for t in range(NT):
                    last = pe.matmul(ps[:, 6, SEQ:SEQ + 1], sel[:, t, :].bitcast(F32), gsel[:, t:t + 1],
                                     start=(t == 0), stop=(t == NT - 1))
                last.then_inc(m_sT_ps, 1)
                for j in range(FJ):
                    if j + 1 < FJ:
                        up(0, j + 1)
                    pe.wait_ge(m_gated, b * FJ + (j + 1))
                    turn(2 * (j % 2), gated[:, j % 2, :], m_gTps)
                    if j + 1 < FJ:
                        up(1, j + 1)
                    else:
                        pe.wait_ge(m_sel, b + 2)
                        pe.wait_ge(m_sT, b + 1)
                        gather()
                    pe.wait_ge(m_glo, b * FJ + (j + 1))
                    for part in range(2):
                        i = MOE_AT[2, j, part]
                        ready(i)
                        wh, wl = split_of(i, D)
                        for half in range(2):
                            for c in range(2):
                                at = (2 * part + c) * P
                                cut = slice(half * 512, (half + 1) * 512)
                                last = product(ps[:, 4 + half, :],
                                               (g_hi[:, j % 2, at:at + P], g_lo[:, j % 2, at:at + P]),
                                               (wh[:, c, cut], wl[:, c, cut]),
                                               j == 0 and part == 0 and c == 0, j == FJ - 1 and part == 1 and c == 1)
                            if j == FJ - 1 and part == 1 and half == 0:
                                last.then_inc(m_y0, 1)
                        last.then_inc(piece_used, 1)

            pe.wait_ge(m_xlo, nblk * 2 + 2)
            turn_p(1)
            scatter(nblk)
            embed(1, lambda i: pe.wait_ge(lo_rdy, nblk * PER_BLOCK + (P_MOE + i + 1)),
                  lambda: pe.wait_ge(m_add, nblk * 4 + H_MOE[1]))

        @block.scalar
        def _(act):
            count = [0]

            def link(ins):
                count[0] += 1
                ins.then_inc(act_link, 1)
                act.wait_ge(act_link, count[0])

            def split(n, used, landed):
                act.wait_ge(raw_in[n % RAW], landed)
                if used is not None:
                    act.wait_ge(piece_used, used)
                act.activation(w_hi[:, n % SPLIT, :], raw[:, n % RAW, :], ACT.Copy).then_inc(hi_rdy, 1)

            ahead = [0]

            def splits(upto):
                while ahead[0] <= upto:
                    n = ahead[0]
                    if n in (P_PROJ_E, P_PROJ_E + 1):
                        act.wait_ge(raw_in[n % RAW], 16 * (n // RAW + 1))
                        act.wait_ge(piece_used, n - SPLIT + 1)
                        act.activation(w_hi[:, n % SPLIT, 0:D], raw[:, n % RAW, 0:D], ACT.Copy).then_inc(hi_rdy, 1)
                    else:
                        split(n, n - SPLIT + 1 if n >= SPLIT else None, 16 * (n // RAW + 1))
                    ahead[0] += 1

            def load_table(f):
                link(act.activation(table, eps6[:, 0:1], f))

            def norm_std(n, h_wait):
                load_table(ACT.Sqrt)
                for t in range(NT):
                    h_wait(t)
                    link(act.activation(hn[:, t, :], h[:, t, :], ACT.Square, accum_out=ssq[:, n, t:t + 1]))
                    act.activation(std[:, n, t:t + 1], ssq[:, n, t:t + 1], ACT.Sqrt, scale=1.0 / D,
                                   bias=eps6[:, 0:1]).then_inc(n_std, 1)

            def h_is(n):
                return lambda t: act.wait_ge(h_ready, H_AT[n][t])

            def norm_hi(n):
                for k in range(KC):
                    act.wait_ge(n_ps, 4 * n + k // 2 + 1)
                    act.activation(xs_hi[:, k, :], ps[:, N_BANK[n] + k // 2, (k % 2) * SEQ:(k % 2 + 1) * SEQ], ACT.Copy,
                                   scale=gT[:, GAIN_AT[n] + k:GAIN_AT[n] + k + 1]).then_inc(n_hi, 1)

            act.wait_ge(eps_set, 1)
            norm_std(0, lambda t: act.wait_ge(x_in[t], 16))
            splits(0)
            act.wait_ge(st_sb, 2)
            norm_hi(0)
            splits(2)
            act.wait_ge(ang_rdy, 1)
            act.activation(cs[:, :, :, :], cs[:, :, :, :], ACT.Sin).then_inc(cs_rdy, 1)
            act.wait_ge(lam_dot, 1)
            act.activation(lame[:, :], lamd[:, :], ACT.Exp).then_inc(lam_exp, 1)

            for n in range(2):
                splits(P_QKV_E + 2 * n + 3)
                act.wait_ge(piece_used, P_QKV_E + 2 * n + 2)
                for t in range(NT):
                    act.activation(qk[:, t, n * 512:(n + 1) * 512], ps[:, 4 + 2 * n + t, :], ACT.Copy).then_inc(qkv_sb, 1)
            splits(P_QKV_E + 7)
            act.wait_ge(piece_used, P_QKV_E + 6)
            for t in range(NT):
                act.activation(vt[:, t, :], ps[:, t, :], ACT.Copy).then_inc(v_sb, 1)
            act.wait_ge(small_in, SMALL_IN)
            act.activation(wba_hi[:, :, :], wba[:, :, :], ACT.Copy).then_inc(small_hi, 1)
            act.activation(wrt_hi[:, :, :], wrt[:, :, :], ACT.Copy).then_inc(small_hi, 1)
            for m in range(2):
                splits(P_CONV_E + m + 2)
                act.wait_ge(piece_used, P_CONV_E + m + 1)
                act.activation(cT[:, 2 * m:2 * m + 2, :], ps[:, 2 + m, :].rearrange("p (c s) -> p c s", c=2),
                               ACT.Copy).then_inc(c_sb, 1)
            for b in range(2):
                act.wait_ge(qkT_ps, b + 1)
                act.activation(qkT[:, 2 * b:2 * b + 2, :], ps[:, 4 + b, :].rearrange("p (c s) -> p c s", c=2),
                               ACT.Copy).then_inc(qkT_sb, 1)

            def exps(hd):
                act.wait_ge(sm_rdy, hd + 1)
                for i in range(4):
                    last = act.activation(sm[:, hd % 2, i, :], sm[:, hd % 2, i, :], ACT.Exp, scale=DH ** -0.5,
                                          bias=nb[:, hd % 2, i:i + 1], accum_out=esum[:, hd % 2, i:i + 1])
                last.then_inc(ex_done, 1)

            splits(P_CONV_E + 4)
            exps(0)
            splits(P_CONV_E + 5)
            for hd in range(HEADS_A):
                if hd + 1 < HEADS_A:
                    exps(hd + 1)
                act.wait_ge(aT_ps, hd + 1)
                if hd >= 2:
                    act.wait_ge(av_ps, hd - 1)
                act.activation(aTt[:, hd % 2, :, :], ps[:, 4, :].rearrange("p (k s) -> p k s", k=NT),
                               ACT.Copy).then_inc(aT_sb, 1)
                if hd == 1:
                    splits(P_OUT_E)
            load_table(ACT.Sqrt)
            act.wait_ge(o_ss, 1)
            act.activation(osd[:, 0:8], oss[:, 0:8], ACT.Sqrt, scale=1.0 / P, bias=eps5[:, 0:1]).then_inc(o_sd, 1)
            splits(P_OUT_E + 1)
            act.wait_ge(mix_conv, 4)
            act.activation(xs_hi[:, 4:8, :], mix_c, ACT.Copy).then_inc(mix_hi, 1)
            for b in range(2):
                act.wait_ge(oT_ps, b + 1)
                act.activation(xs_hi[:, 2 * b:2 * b + 2, :], ps[:, 4 + b, :].rearrange("p (c s) -> p c s", c=2),
                               ACT.Copy, scale=gT[:, G_SUB:G_SUB + 1]).then_inc(mix_hi, 1)
            splits(P_OUT_E + 5)

            act.wait_ge(h_ready, H_AT[1][0])
            act.dma_start(p_tok[:, :, :], a["p"][0, 0].rearrange("(t p) d -> p t d", p=P)).then_inc(p_in, 16)
            norm_std(1, h_is(1))
            splits(P_MLP + 2)
            norm_hi(1)

            for s in range(HALF_FJ):
                splits(MLP_AT[0, s] + 2)
                act.wait_ge(piece_used, MLP_AT[0, s] + 1)
                act.activation(sil[:, s % 2, :], ps[:, 2 * (s % 2), :], ACT.Silu).then_inc(silu_sb, 1)
                splits(MLP_AT[1, s] + 2)
                act.wait_ge(gated_sb, s + 1)
                act.activation(g_hi[:, s % 2, :], gated[:, s % 2, :], ACT.Copy).then_inc(gated_hi, 1)
            def p_first(i):
                act.wait_ge(pT_ps, i + 1)
                act.activation(p_hi, ps[:, 1, :].rearrange("p (c s) -> p c s", c=2), ACT.Copy).then_inc(pT_hi, 1)

            def embed(i, pieces, used):
                norm_hi(2 + 3 * i)
                for j in range(2):
                    pieces(5 + 2 * j)
                    load_table(ACT.Sigmoid)
                    used(2 * j + 4)
                    for t in range(NT):
                        act.activation(sgm[:, t, j * 512:(j + 1) * 512], ps[:, 4 + 2 * j + t, :], ACT.Sigmoid).then_inc(sgm_sb, 1)

            p_first(0)
            splits(P_PROJ_E + 1)
            norm_std(2, h_is(2))
            splits(P_PROJ_E + 2)
            embed(0, lambda i: splits(P_PROJ_E + i), lambda i: act.wait_ge(piece_used, P_PROJ_E + i))
            norm_std(3, h_is(3))
            splits(P_QKV_O + 2)
            norm_hi(3)
            act.wait_ge(ba_neg, 1)
            act.activation(yexp[:, :, :], yneg[:, :, :], ACT.Exp)
            act.activation(ealog[:, :], alog[:, :], ACT.Exp).then_inc(ba_exp, 1)
            act.wait_ge(ba_exp, 1)
            act.activation(yln[:, :, :], yexp[:, :, 8:16], ACT.Ln, bias=1.0).then_inc(ba_ln, 1)
            act.wait_ge(pad_zero, 1)

            def square(g):
                if g >= 2:
                    act.wait_ge(l2_ps, g - 1)
                act.activation(bt[0][:, g % 2].rearrange("p a b -> p (a b)"),
                               qkvT[:, 2 * g:2 * g + 2, :].rearrange("p a b -> p (a b)"), ACT.Square).then_inc(l2_sq, 1)

            def roots(i):
                act.wait_ge(l2_ps, 4 * i + 4)
                act.activation(l2n[:, i], ps[:, 4 + i, 0:NT * 8].rearrange("p (t n) -> p t n", t=NT), ACT.Sqrt,
                               bias=eps6[:, 0:1]).then_inc(l2_sd, 1)

            def silu_conv(n):
                act.wait_ge(cv_done, n + 1)
                act.activation(qkvT[:, 4 * n:4 * n + 4, :], qkvT[:, 4 * n:4 * n + 4, :], ACT.Silu).then_inc(cv_silu, 1)

            def silu_z(j):
                splits(P_Z + 2 * j + 3)
                act.wait_ge(piece_used, P_Z + 2 * j + 2)
                for t in range(NT):
                    act.activation(zs[:, t, j * 512:(j + 1) * 512], ps[:, 4 + 2 * j + t, :], ACT.Silu).then_inc(z_sb, 1)

            for n in range(6):
                if n in (3, 5):
                    act.wait_ge(cv_silu, n - 1)
                    square(2 * n - 6)
                    square(2 * n - 5)
                for m in range(2):
                    i = P_QKV_O + 2 * n + m
                    splits(i + 2)
                    act.wait_ge(piece_used, i + 1)
                    if n >= 2 and m == 0:
                        act.wait_ge(cv_done, n - 1)
                    pair = ps[:, (2 * n + m) % 4, :].rearrange("p (c s) -> p c s", c=2)
                    act.activation(upo[:, n % 2, 2 * m:2 * m + 2, DN_TAPS - 1:], pair, ACT.Copy).then_inc(q_pad, 1)
                if n in (3, 5):
                    square(2 * n - 4)
                    square(2 * n - 3)
                if n == 4:
                    roots(0)
                    act.wait_ge(cum_sb, 1)
                    act.activation(dcy[:, :, :, :], dcy[:, :, :, :], ACT.Exp).then_inc(dcy_rdy, 1)
                if n == 5:
                    roots(1)
                if n >= 1:
                    silu_conv(n - 1)
            splits(P_Z + 1)
            silu_conv(5)
            silu_z(0)
            splits(P_Z + 3)
            silu_z(1)
            splits(P_OUT_O + 2)
            for t in range(NT):
                for b in range(2):
                    act.wait_ge(kv_ps, 4 * t + 2 + b + 1)
                    act.activation(ktok[:, t, 4 * b:4 * b + 4, :], ps[:, 4 * t + b, :].rearrange(
                        "p (c s) -> p c s", c=4), ACT.Copy).then_inc(k_sb, 1)

            def head_squares(t):
                act.wait_ge(od_sb, 2 * t + 2)
                act.activation(odq[:, t, :, :], AT[:, t, :, :], ACT.Square).then_inc(od_ss, 1)

            def head_roots(t):
                act.wait_ge(od_sum, t + 1)
                act.activation(osd[:, 8 * t:8 * t + 8], oss[:, 8 * t:8 * t + 8], ACT.Sqrt, scale=1.0 / P,
                               bias=eps6[:, 0:1]).then_inc(od_sd, 1)

            for t in range(NT):
                for g in range(2):
                    act.wait_ge(dd_rdy, 2 * t + g + 1)
                    act.activation(AT[:, t, 4 * g:4 * g + 4, :], AT[:, t, 4 * g:4 * g + 4, :], ACT.Exp).then_inc(dec_exp, 1)

            def out_of(bank):
                return ps[:, bank, :].rearrange("p (c s) -> p c s", c=4)

            for t in range(NT):
                for g in range(2):
                    act.wait_ge(x1_ps, 2 * t + g + 1)
                    act.activation(X[t][:, 4 * g:4 * g + 4, :], out_of(2 * t + g), ACT.Copy).then_inc(x1_sb, 1)
            for l in range(1, LEVELS):
                for t in range(NT):
                    for g in range(2):
                        act.wait_ge(p_ps, at_level(l, t, g))
                        act.activation(pm[t][:, g], out_of(2 * t + g), ACT.Copy).then_inc(p_sb, 1)
            for g in range(2):
                act.wait_ge(u_ps, g + 1)
                act.activation(un[0][:, 4 * g:4 * g + 4, :], out_of(g), ACT.Copy).then_inc(u_sb, 1)
            for g in range(2):
                act.wait_ge(w_ps, g + 1)
                act.activation(nwT[:, 4 * g:4 * g + 4, :], out_of(6 + g), ACT.Copy, scale=-1.0).then_inc(w_sb, 1)
            for g in range(2):
                act.wait_ge(s_ps, g + 1)
                act.activation(S1[:, 4 * g:4 * g + 4, :], out_of(4 + g), ACT.Copy).then_inc(s_sb, 1)
            for g in range(2):
                act.wait_ge(qg_ps, g + 1)
                act.activation(qgT[:, 4 * g:4 * g + 4, :], out_of(g), ACT.Exp).then_inc(qg_exp, 1)
            load_table(ACT.Sqrt)
            head_squares(0)
            for g in range(2):
                act.wait_ge(u_ps, 2 + g + 1)
                act.activation(un[1][:, 4 * g:4 * g + 4, :], out_of(6 + g), ACT.Copy).then_inc(u_sb, 1)
                if g == 0:
                    head_roots(0)
            head_squares(1)
            head_roots(1)
            for b in range(4):
                act.wait_ge(odT_ps, b + 1)
                act.activation(xs_hi[:, 2 * b:2 * b + 2, :], ps[:, b, :].rearrange("p (c s) -> p c s", c=2), ACT.Copy,
                               scale=gT[:, G_ON:G_ON + 1]).then_inc(odT_hi, 1)
            splits(P_OUT_O + 5)

            norm_std(4, h_is(4))
            splits(P_MOE + 2)
            act.dma_start(p_tok[:, :, :], a["p"][1, 0].rearrange("(t p) d -> p t d", p=P)).then_inc(p_in, 16)
            act.dma_start(gfin[:, :], a["ln_final"].unsqueeze(0).broadcast_to([P, D])).then_inc(gfin_in, 16)
            act.dma_start(gffn[:, :], a["ln_ffn"][1:2, :].broadcast_to([P, D])).then_inc(gffn_in, 16)
            norm_hi(4)
            for t in range(NT):
                act.wait_ge(m_hn, t + 1)
                act.activation(hn_hi[:, t, :], hn[:, t, :], ACT.Copy).then_inc(m_hhi, 1)
            act.wait_ge(lg_max, 1)
            for t in range(NT):
                last = act.activation(r_e[:, t, :], r_l[:, t, :], ACT.Exp, bias=r_nmx[:, t:t + 1])
            last.then_inc(lg_exp, 1)
            def tokens_hi(done):
                for q in range(2):
                    act.wait_ge(m_xg_ps, done + (q + 1))
                    act.activation(xg_hi[:, 4 * q:4 * q + 4, :], ps[:, 6 + q, :].rearrange("p (c s) -> p c s", c=4),
                                   ACT.Copy).then_inc(m_xhi, 1)

            tokens_hi(0)
            act.wait_ge(tab_rdy, 1)
            nblk = act.value_load(blk_i[0:1, 15:16], min_val=NE, max_val=NE + MAX_OVER)

            with act.Fori(0, nblk) as b:
                at = [SPLIT]

                def pieces(upto):
                    while at[0] <= upto:
                        i = at[0]
                        split(i, b * PER_BLOCK + (P_MOE + i - SPLIT + 1),
                              b * (16 * PER_BLOCK // RAW) + 16 * ((P_MOE + i) // RAW + 1))
                        at[0] += 1

                def silu_of(j):
                    i = MOE_AT[0, j, 1]
                    pieces(i + 2)
                    act.wait_ge(piece_used, b * PER_BLOCK + (P_MOE + i + 1))
                    act.activation(sil[:, j % 2, :], ps[:, 2 * (j % 2), :], ACT.Silu).then_inc(m_silu, 1)

                silu_of(0)
                pieces(MOE_AT[1, 0, 1] + 2)
                act.wait_ge(m_sT_ps, b + 1)
                act.activation(gslot, ps[:, 6, SEQ:SEQ + 1], ACT.Copy)
                act.activation(selT, ps[:, 6, 0:SEQ], ACT.Copy).then_inc(m_sT, 1)
                for j in range(FJ):
                    if j + 1 < FJ:
                        silu_of(j + 1)
                    else:
                        pieces(MOE_AT[2, j - 1, 1] + 2)
                    act.wait_ge(m_gTps, b * FJ + (j + 1))
                    act.activation(g_hi[:, j % 2, :], ps[:, 2 * (j % 2), :], ACT.Copy).then_inc(m_ghi, 1)
                tokens_hi(b * 2 + 2)
                pieces(PER_BLOCK + 1)
                act.wait_ge(m_sT, b + 1)
                for half in range(2):
                    if half == 0:
                        act.wait_ge(m_y0, b + 1)
                    else:
                        act.wait_ge(piece_used, b * PER_BLOCK + (P_MOE + PER_BLOCK))
                    act.activation(y_hi[:, half * 512:(half + 1) * 512], ps[:, 4 + half, :], ACT.Copy,
                                   scale=gslot[:, 0:1]).then_inc(m_yhi, 1)
                pieces(PER_BLOCK + 2)

            p_first(1)
            norm_std(5, lambda t: act.wait_ge(m_add, nblk * 4 + H_MOE[t]))
            tail = [SPLIT]

            def tail_pieces(upto):
                while tail[0] <= min(upto, 5):
                    i = tail[0]
                    width = D if i < 2 else PIECE
                    act.wait_ge(raw_in[i % RAW], nblk * (16 * PER_BLOCK // RAW) + 16 * ((P_MOE + i) // RAW + 1))
                    act.wait_ge(piece_used, nblk * PER_BLOCK + (P_MOE + i - SPLIT + 1))
                    act.activation(w_hi[:, i % SPLIT, 0:width], raw[:, i % RAW, 0:width], ACT.Copy).then_inc(hi_rdy, 1)
                    tail[0] += 1

            embed(1, tail_pieces, lambda i: act.wait_ge(piece_used, nblk * PER_BLOCK + (P_MOE + i)))
            norm_std(6, h_is(6))

        @block.gpsimd
        def _(pool):
            for l in range(LEVELS):
                for t in range(NT):
                    for g in range(2):
                        if l == 0:
                            pool.wait_ge(lt_sb, 2 * t + g + 1)
                            if t == 0:
                                pool.wait_ge(l2_ps, 8)
                        elif l == 1:
                            pool.wait_ge(x1_rdy, 2 * t + g + 1)
                        else:
                            pool.wait_ge(p_ps, at_level(l - 1, t, g))
                        pool.tensor_tensor(bt[t][:, g], LT[t][:, 4 * g:4 * g + 4, :], over(level_mask(l), 4),
                                           ALU.mult).then_inc(bt_rdy, 1)

        @block.vector
        def _(dve):
            count = [0]

            def link(ins):
                count[0] += 1
                ins.then_inc(dve_link, 1)
                dve.wait_ge(dve_link, count[0])

            def split(n, hi_count, width=PIECE):
                dve.wait_ge(hi_rdy, hi_count)
                dve.tensor_tensor(w_lo[:, n % SPLIT, 0:width], raw[:, n % RAW, 0:width],
                                  w_hi[:, n % SPLIT, 0:width].bitcast(F32), ALU.subtract).then_inc(lo_rdy, 1)

            ahead = [0]

            def splits(upto):
                while ahead[0] <= upto:
                    n = ahead[0]
                    split(n, n + 1, D if n in (P_PROJ_E, P_PROJ_E + 1) else PIECE)
                    ahead[0] += 1

            dve.memset(eps5[:, :], SUBLN_EPS)
            dve.memset(upad[:, :, 0:SC_TAPS - 1], 0.0)
            dve.memset(eps6[:, :], RMS_EPS).then_inc(eps_set, 1)

            def norm_hn(n):
                for t in range(NT):
                    dve.wait_ge(n_std, NT * n + t + 1)
                    link(dve.reciprocal(rstd[:, n, t:t + 1], std[:, n, t:t + 1]))
                    dve.tensor_scalar(hn[:, t, :], h[:, t, :], rstd[:, n, t:t + 1], None, ALU.mult).then_inc(n_hn, 1)

            def norm_lo(n):
                for k in range(KC):
                    dve.wait_ge(n_hi, KC * n + 2 * (k // 2) + 2)
                    dve.scalar_tensor_tensor(xs_lo[:, k, :], ps[:, N_BANK[n] + k // 2, (k % 2) * SEQ:(k % 2 + 1) * SEQ],
                                             gT[:, GAIN_AT[n] + k:GAIN_AT[n] + k + 1], xs_hi[:, k, :].bitcast(F32),
                                             ALU.mult, ALU.subtract).then_inc(n_lo, 1)

            norm_hn(0)
            dve.wait_ge(st_ps, 1)
            link(dve.tensor_copy(gT[:, :], ps[:, 4, 0:62]))
            dve.tensor_copy(cwT[:, :], ps[:, 4, 128:224]).then_inc(st_sb, 1)
            dve.tensor_scalar(gT[:, G_SUB:G_SUB + 1], gT[:, G_SUB:G_SUB + 1], 1.0 - LAM0, None, ALU.mult).then_inc(st_sb, 1)
            dve.wait_ge(st_sb, 2)
            splits(0)
            norm_lo(0)
            splits(2)

            dve.wait_ge(small_in, SMALL_IN)
            dve.tensor_copy(posc[:, :], posi[:, 0:NT])
            link(dve.tensor_copy(posrow, posi[:, NT:NT + SEQ]))
            for t in range(NT):
                dve.tensor_scalar(maskb[:, t, :], posrow, posc[:, t:t + 1], NEG, ALU.is_gt, ALU.mult)
                last = dve.tensor_scalar(ang[:, t, :], con[:, C_FREQ:C_FREQ + HALF_ROT], posc[:, t:t + 1], None, ALU.mult)
            link(last)
            link(dve.tensor_scalar(turns, ang, 1.0 / (2 * math.pi), 12582912.0, ALU.mult, ALU.add))
            link(dve.tensor_scalar(turns, turns, 12582912.0, None, ALU.subtract))
            for part in TWO_PI:
                link(dve.scalar_tensor_tensor(ang, turns, -part, ang, ALU.mult, ALU.add))
            link(dve.tensor_scalar(cs[:, 1], ang, math.pi - 1e-6, -(math.pi - 1e-6), ALU.min, ALU.max))
            link(dve.scalar_tensor_tensor(ang, cs[:, 1], -1.0, cs[:, 1], ALU.mult, ALU.max))
            dve.tensor_scalar(cs[:, 0], ang, -1.0, math.pi / 2, ALU.mult, ALU.add).then_inc(ang_rdy, 1)
            dve.wait_ge(small_in, SMALL_IN)
            dve.tensor_tensor(lamp[:, :, :], lamv.rearrange("p (a b) d -> p a b d", b=2)[:, :, 0, :],
                              lamv.rearrange("p (a b) d -> p a b d", b=2)[:, :, 1, :], ALU.mult).then_inc(dve_link, 1)
            count[0] += 1
            dve.wait_ge(dve_link, count[0])
            dve.tensor_reduce(lamd[:, :], lamp[:, :, :], AX, ALU.add).then_inc(lam_dot, 1)
            dve.wait_ge(lam_exp, 1)
            link(dve.scalar_tensor_tensor(nlam[:, :], lame[:, 1:2], LAM0, lame[:, 0:1], ALU.subtract, ALU.subtract))

            splits(P_QKV_E + 5)
            dve.wait_ge(cs_rdy, 1)
            for t in range(NT):
                dve.wait_ge(qkv_sb, 3 + t)
                heads = qk[:, t, :].rearrange("p (h d) -> p h d", d=DH)
                x1, x2 = heads[:, :, 0:HALF_ROT], heads[:, :, HALF_ROT:ROT]
                cos, sin = over(cs[:, 0, t, :], 16), over(cs[:, 1, t, :], 16)
                dve.tensor_tensor(rt[:, 0], x1, cos, ALU.mult)
                dve.tensor_tensor(rt[:, 1], x2, sin, ALU.mult)
                dve.tensor_tensor(rt[:, 2], x2, cos, ALU.mult)
                link(dve.tensor_tensor(rt[:, 3], x1, sin, ALU.mult))
                dve.tensor_tensor(x1, rt[:, 0], rt[:, 1], ALU.subtract)
                link(dve.tensor_tensor(x2, rt[:, 2], rt[:, 3], ALU.add))
                dve.engine_nop().then_inc(rope_done, 1)
                splits(P_QKV_E + 6 + t)
            dve.wait_ge(small_hi, 2)
            dve.tensor_tensor(wba_lo[:, :, :], wba[:, :, :], wba_hi[:, :, :].bitcast(F32), ALU.subtract).then_inc(small_lo, 1)
            dve.tensor_tensor(wrt_lo[:, :, :], wrt[:, :, :], wrt_hi[:, :, :].bitcast(F32), ALU.subtract).then_inc(small_lo, 1)
            splits(P_CONV_E + 3)
            for b in range(2, 4):
                dve.wait_ge(qkT_ps, b + 1)
                dve.tensor_copy(qkT[:, 2 * b:2 * b + 2, :], ps[:, 4 + b, :].rearrange("p (c s) -> p c s", c=2)).then_inc(qkT_sb, 1)

            def gate_in(m):
                dve.wait_ge(c_sb, m + 1)
                dve.wait_ge(piece_used, P_CONV_E + 2 + m + 1)
                dve.tensor_tensor(upad[:, 2 * m:2 * m + 2, SC_TAPS - 1:], cT[:, 2 * m:2 * m + 2, :],
                                  ps[:, 6 + m, :].rearrange("p (c s) -> p c s", c=2), ALU.mult).then_inc(xb_used, 1)

            def taps():
                dve.wait_ge(xb_used, 2)
                for j in range(SC_TAPS):
                    for m in range(4):
                        tap = gT[:, G_CW + 4 * j + m:G_CW + 4 * j + m + 1]
                        src = upad[:, m, j:j + SEQ]
                        if j == 0:
                            last = dve.tensor_scalar(mix_c[:, m, :], src, tap, None, ALU.mult)
                        else:
                            last = dve.scalar_tensor_tensor(mix_c[:, m, :], src, tap, mix_c[:, m, :], ALU.mult, ALU.add)
                    link(last)

            def gate_out():
                dve.wait_ge(piece_used, P_CONV_E + 6)
                for m in range(4):
                    dve.tensor_tensor(mix_c[:, m, :], mix_c[:, m, :],
                                      ps[:, 6 + m // 2, (m % 2) * SEQ:(m % 2 + 1) * SEQ], ALU.mult).then_inc(mix_conv, 1)

            def masked(hd):
                dve.wait_ge(sc_ps, hd + 1)
                for m in range(2):
                    dve.tensor_tensor(sm[:, hd % 2, 2 * m:2 * m + 2, :], ps[:, 2 * (hd % 2) + m, :].rearrange(
                        "p (t s) -> p t s", t=NT), maskb, ALU.add).then_inc(sm_read, 1)
                dve.wait_ge(sm_read, 2 * (hd + 1))
                link(dve.tensor_reduce(mx[:, hd % 2, :], sm[:, hd % 2], AX, ALU.max))
                dve.tensor_scalar(nb[:, hd % 2, :], mx[:, hd % 2, :], -(DH ** -0.5), None, ALU.mult).then_inc(sm_rdy, 1)

            masked(0)
            splits(P_CONV_E + 4)
            for hd in range(HEADS_A):
                if hd + 1 < HEADS_A:
                    masked(hd + 1)
                if hd < 2:
                    gate_in(hd)
                u = hd % 2
                dve.wait_ge(ex_done, hd + 1)
                link(dve.reciprocal(erc[:, u, :], esum[:, u, :]))
                link(dve.tensor_scalar(erc[:, u, 2:4], erc[:, u, 2:4], nlam[:, 0:1], None, ALU.mult))
                if hd >= 2:
                    dve.wait_ge(aT_ps, hd - 1)
                for t in range(NT):
                    last = dve.tensor_scalar(adf[:, u, t, :], sm[:, u, t, :], erc[:, u, t:t + 1], None, ALU.mult)
                link(last)
                for t in range(NT):
                    last = dve.scalar_tensor_tensor(adf[:, u, t, :], sm[:, u, 2 + t, :], erc[:, u, 2 + t:3 + t],
                                                    adf[:, u, t, :], ALU.mult, ALU.add)
                last.then_inc(a_done, 1)
                dve.wait_ge(a_done, hd + 1)
                if hd >= 1:
                    dve.wait_ge(av_ps, hd)
                    dve.tensor_copy(oat[:, :, hd - 1, :], ps[:, 5, 0:SEQ].rearrange(
                        "p (t v) -> p t v", t=NT)).then_inc(o_sb, 1)
                if hd == 0:
                    splits(P_CONV_E + 5)
                if hd == 1:
                    splits(P_OUT_E)
                if hd == 3:
                    taps()
            dve.wait_ge(av_ps, HEADS_A)
            dve.tensor_copy(oat[:, :, HEADS_A - 1, :], ps[:, 5, 0:SEQ].rearrange(
                "p (t v) -> p t v", t=NT)).then_inc(o_sb, 1)
            dve.wait_ge(o_sb, HEADS_A)
            o3 = oat.rearrange("p t h v -> p (t h) v")
            q3 = osq.rearrange("p t h v -> p (t h) v")
            link(dve.tensor_tensor(q3, o3, o3, ALU.mult))
            dve.tensor_reduce(oss[:, 0:8], q3, AX, ALU.add).then_inc(o_ss, 1)
            gate_out()
            dve.wait_ge(o_sd, 1)
            link(dve.reciprocal(ors[:, 0:8], osd[:, 0:8]))
            dve.tensor_tensor(o3, o3, along(ors[:, 0:8], P), ALU.mult).then_inc(o_nrm, 1)
            splits(P_OUT_E + 1)
            dve.wait_ge(mix_hi, 1)
            dve.tensor_tensor(xs_lo[:, 4:8, :], mix_c, xs_hi[:, 4:8, :].bitcast(F32), ALU.subtract).then_inc(mix_lo, 1)

            def add_h(t, half, src):
                piece = h[:, t, half * 512:(half + 1) * 512]
                return dve.tensor_tensor(piece, piece, src, ALU.add)

            for b in range(2):
                dve.wait_ge(mix_hi, b + 2)
                dve.scalar_tensor_tensor(xs_lo[:, 2 * b:2 * b + 2, :], ps[:, 4 + b, :].rearrange("p (c s) -> p c s", c=2),
                                         gT[:, G_SUB:G_SUB + 1], xs_hi[:, 2 * b:2 * b + 2, :].bitcast(F32),
                                         ALU.mult, ALU.subtract).then_inc(mix_lo, 1)
            for j in range(2):
                splits(P_OUT_E + 2 * j + 3)
                dve.wait_ge(piece_used, P_OUT_E + 2 * j + 2)
                for t in range(NT):
                    add_h(t, j, ps[:, 2 * j + t, :]).then_inc(h_ready, 1)

            dve.wait_ge(h_ready, H_AT[1][1])
            norm_hn(1)
            splits(P_MLP + 2)
            norm_lo(1)
            for s in range(HALF_FJ):
                splits(MLP_AT[1, s] + 2)
                dve.wait_ge(piece_used, MLP_AT[1, s] + 1)
                dve.wait_ge(silu_sb, s + 1)
                dve.tensor_tensor(gated[:, s % 2, :], sil[:, s % 2, :], ps[:, 2 * (s % 2) + 1, :], ALU.mult).then_inc(gated_sb, 1)
                dve.wait_ge(gated_hi, s + 1)
                dve.tensor_tensor(g_lo[:, s % 2, :], gated[:, s % 2, :], g_hi[:, s % 2, :].bitcast(F32),
                                  ALU.subtract).then_inc(gated_lo, 1)

            def p_second(i):
                dve.wait_ge(pT_hi, i + 1)
                dve.tensor_tensor(p_lo, ps[:, 1, :].rearrange("p (c s) -> p c s", c=2), p_hi.bitcast(F32),
                                  ALU.subtract).then_inc(pT_lo, 1)

            p_second(0)
            splits(P_PROJ_E + 1)
            dve.wait_ge(piece_used, P_PROJ_E)
            for t in range(NT):
                for half in range(2):
                    add_h(t, half, ps[:, 4 + 2 * t + half, :]).then_inc(h_ready, 1)

            def embed(i, pieces, used):
                norm_lo(2 + 3 * i)
                pieces(5)
                for j in range(2):
                    for t in range(NT):
                        dve.wait_ge(sgm_sb, 4 * i + 2 * j + t + 1)
                        link(dve.tensor_tensor(ptmp[:, t, :], sgm[:, t, j * 512:(j + 1) * 512],
                                               ps[:, 2 * j + t, :], ALU.mult))
                        add_h(t, j, ptmp[:, t, :]).then_inc(h_ready, 1)
                    if j == 0:
                        pieces(7)

            dve.wait_ge(h_ready, H_AT[2][1])
            norm_hn(2)
            splits(P_PROJ_E + 2)
            embed(0, lambda i: splits(P_PROJ_E + i), lambda i: dve.wait_ge(piece_used, P_PROJ_E + i))

            dve.wait_ge(h_ready, H_AT[3][1])
            norm_hn(3)
            splits(P_QKV_O + 2)
            norm_lo(3)
            dve.memset(upo[:, :, :, 0:DN_TAPS - 1], 0.0).then_inc(pad_zero, 1)
            dve.wait_ge(ba_ps, 1)
            link(dve.tensor_copy(ba[:, :, :], ps[:, 3, 0:32].rearrange("p (t n) -> p t n", t=NT)))
            link(dve.tensor_tensor(ba[:, :, 8:16], ba[:, :, 8:16], over(dtb[:, :], NT), ALU.add))
            dve.tensor_scalar(yneg[:, :, 0:8], ba[:, :, 0:8], -1.0, None, ALU.mult)
            dve.scalar_tensor_tensor(yneg[:, :, 8:16], ba[:, :, 8:16], -1.0, ba[:, :, 8:16], ALU.mult, ALU.min).then_inc(ba_neg, 1)
            dve.wait_ge(ba_ln, 1)
            link(dve.tensor_scalar(yexp[:, :, 0:8], yexp[:, :, 0:8], 1.0, None, ALU.add))
            dve.reciprocal(beta[:, :, :], yexp[:, :, 0:8])
            link(dve.scalar_tensor_tensor(gdec[:, :, :], ba[:, :, 8:16], 0.0, yln[:, :, :], ALU.max, ALU.add))
            dve.scalar_tensor_tensor(gdec[:, :, :], gdec[:, :, :], -1.0, over(ealog[:, :], NT), ALU.mult, ALU.mult).then_inc(g_rdy, 1)

            def conv(n):
                splits(P_QKV_O + 2 * n + 3)
                for m in range(2):
                    dve.wait_ge(q_pad, 2 * n + m + 1)
                for j in range(DN_TAPS):
                    for m in range(4):
                        ch = 4 * n + m
                        tap = cwT[:, j * QKV_CHUNKS + ch:j * QKV_CHUNKS + ch + 1]
                        src = upo[:, n % 2, m, j:j + SEQ]
                        if j == 0:
                            last = dve.tensor_scalar(qkvT[:, ch, :], src, tap, None, ALU.mult)
                        else:
                            last = dve.scalar_tensor_tensor(qkvT[:, ch, :], src, tap, qkvT[:, ch, :], ALU.mult, ALU.add)
                    if j < DN_TAPS - 1:
                        link(last)
                last.then_inc(cv_done, 1)

            def factors(i):
                dve.wait_ge(l2_sd, i + 1)
                dve.reciprocal(l2f[:, i], l2n[:, i]).then_inc(l2_fac, 1)

            def normalise(g):
                dve.wait_ge(l2_bc, g + 1)
                pair = qkvT[:, 2 * g:2 * g + 2, :].rearrange("p a b -> p (a b)")
                dve.scalar_tensor_tensor(pair, pair, P ** -0.5 if g < 4 else 1.0, ps[:, g % 4, :],
                                         ALU.mult, ALU.mult).then_inc(l2_done, 1)

            for n in range(6):
                if n == 3:
                    dve.wait_ge(cum_ps, 1)
                    link(dve.tensor_copy(cum[:, :, :, :], ps[:, 7, 0:32].rearrange("p (t k n) -> p t k n", t=NT, k=2)))
                    dve.tensor_copy(dcy[:, :, 0, :], cum[:, :, 0, :])
                    dve.tensor_tensor(dcy[:, :, 1, :], cum[:, :, 1, :], cum[:, :, 0, :], ALU.subtract).then_inc(cum_sb, 1)
                if n == 5:
                    splits(P_QKV_O + 2 * n + 3)
                    factors(0)
                conv(n)
            splits(P_Z + 2)
            for g in range(4):
                normalise(g)
            factors(1)
            dve.wait_ge(dcy_rdy, 1)
            link(dve.tensor_tensor(bec[:, :, :], beta[:, :, :], dcy[:, :, 0, :], ALU.mult))
            splits(P_Z + 3)
            for g in range(4, 8):
                normalise(g)
            for t in range(NT):
                for b in range(2):
                    dve.wait_ge(kv_ps, 4 * t + b + 1)
                    dve.tensor_tensor(vb[:, t, 4 * b:4 * b + 4, :], ps[:, 4 * t + 2 + b, :].rearrange(
                        "p (c s) -> p c s", c=4), along(beta[:, t, 4 * b:4 * b + 4], P), ALU.mult).then_inc(vb_sb, 1)
            dve.wait_ge(kv_ps, 8)
            def head_scale(t):
                dve.wait_ge(od_ss, t + 1)
                dve.tensor_reduce(oss[:, 8 * t:8 * t + 8], odq[:, t], AX, ALU.add).then_inc(od_sum, 1)
                dve.wait_ge(od_sd, t + 1)
                link(dve.reciprocal(ors[:, 8 * t:8 * t + 8], osd[:, 8 * t:8 * t + 8]))
                for hd in range(HEADS_D):
                    last = dve.scalar_tensor_tensor(AT[:, t, hd, :], AT[:, t, hd, :], ors[:, 8 * t + hd:8 * t + hd + 1],
                                                    zs[:, t, hd * P:(hd + 1) * P], ALU.mult, ALU.mult)
                last.then_inc(od_nrm, 1)

            def out_of(bank):
                return ps[:, bank, :].rearrange("p (c s) -> p c s", c=4)

            for t in range(NT):
                for g in range(2):
                    dve.wait_ge(rc_ps, 2 * t + g + 1)
                    for c in range(4):
                        hd = 4 * g + c
                        last = dve.tensor_scalar(AT[:, t, hd, :], ps[:, g, c * P:(c + 1) * P],
                                                 cum[:, t, 0, hd:hd + 1], 0.0, ALU.subtract, ALU.min)
                    last.then_inc(dd_rdy, 1)
                    dve.wait_ge(br_ps, 2 * t + g + 1)
                    dve.tensor_tensor(pm[t][:, g], kT[:, 4 * g:4 * g + 4, t * P:(t + 1) * P], out_of(2 + g),
                                      ALU.mult).then_inc(kb_rdy, 1)
            for t in range(NT):
                u = 2 * t
                for g in range(2):
                    heads = slice(4 * g, 4 * g + 4)
                    dve.wait_ge(dec_exp, u + g + 1)
                    link(dve.tensor_tensor(AT[:, t, heads, :], AT[:, t, heads, :], over(upper, 4), ALU.mult))
                    dve.wait_ge(lt_ps, u + g + 1)
                    dve.tensor_tensor(LT[t][:, heads, :], out_of(4 + g), AT[:, t, heads, :], ALU.mult).then_inc(lt_sb, 1)
                    dve.wait_ge(at_ps, u + g + 1)
                    dve.wait_ge(lt_sb, u + g + 1)
                    dve.tensor_tensor(AT[:, t, heads, :], out_of(6 + g), AT[:, t, heads, :], ALU.mult).then_inc(at_sb, 1)
                for g in range(2):
                    dve.wait_ge(bt_rdy, u + g + 1)
                    dve.tensor_tensor(XT[:, t, 4 * g:4 * g + 4, :], over(ident, 4), bt[t][:, g], ALU.subtract).then_inc(x1_rdy, 1)
            dve.wait_ge(k_sb, 4)
            for l in range(1, LEVELS):
                for t in range(NT):
                    if l == LEVELS - 1:
                        dve.wait_ge(p_ps, at_level(l, t, 1))
                        scale = dcy[:, 0, 1, :] if t == 0 else bec[:, 1, :]
                        dve.tensor_tensor(kbe[t], ktok[:, t], along(scale, P), ALU.mult).then_inc(ksc_rdy, 1)
                    for g in range(2):
                        heads = slice(4 * g, 4 * g + 4)
                        dve.wait_ge(x_ps, at_level(l, t, g))
                        if l == 1:
                            dve.wait_ge(x1_rdy, 2 * t + g + 1)
                        else:
                            dve.wait_ge(x_sb, at_level(l - 1, t, g))
                        if l < LEVELS - 1:
                            dve.wait_ge(x1_sb, 2 * t + g + 1)
                            dve.tensor_tensor(X[t][:, heads, :], X[t][:, heads, :], out_of(4 + g), ALU.subtract)
                        dve.tensor_tensor(XT[:, t, heads, :], XT[:, t, heads, :], out_of(6 + g),
                                          ALU.subtract).then_inc(x_sb, 1)
                if 2 <= l < 5:
                    splits(P_OUT_O + l - 2)
            for g in range(2):
                dve.wait_ge(od_ps, g + 1)
                dve.tensor_copy(AT[:, 0, 4 * g:4 * g + 4, :], out_of(2 + g)).then_inc(od_sb, 1)
            for g in range(2):
                dve.wait_ge(qg_exp, g + 1)
                dve.tensor_tensor(qgT[:, 4 * g:4 * g + 4, :], qgT[:, 4 * g:4 * g + 4, :],
                                  qT[:, 4 * g:4 * g + 4, P:2 * P], ALU.mult).then_inc(qg_rdy, 1)
            head_scale(0)
            for g in range(2):
                dve.wait_ge(od_ps, 2 + g + 1)
                dve.tensor_copy(AT[:, 1, 4 * g:4 * g + 4, :], out_of(4 + g)).then_inc(od_sb, 1)
            head_scale(1)
            for b in range(4):
                dve.wait_ge(odT_hi, b + 1)
                dve.scalar_tensor_tensor(xs_lo[:, 2 * b:2 * b + 2, :], ps[:, b, :].rearrange("p (c s) -> p c s", c=2),
                                         gT[:, G_ON:G_ON + 1], xs_hi[:, 2 * b:2 * b + 2, :].bitcast(F32),
                                         ALU.mult, ALU.subtract).then_inc(odT_lo, 1)
            link(dve.memset(zero, 0.0))
            dve.tensor_copy(y_hi, zero.broadcast_to([P, D]))
            dve.tensor_copy(selT, zero.broadcast_to([P, SEQ]))
            dve.tensor_copy(y_lo, zero.broadcast_to([P, D])).then_inc(m_ysb, 2)
            for j in range(2):
                splits(P_OUT_O + 2 * j + 3)
                dve.wait_ge(piece_used, P_OUT_O + 2 * j + 2)
                for t in range(NT):
                    add_h(t, j, ps[:, 4 + 2 * j + t, :]).then_inc(h_ready, 1)

            def select(b):
                for t in range(NT):
                    dve.tensor_scalar(sel[:, t, :], iota, posb[:, t, bass.ds(b, 1)], None, ALU.is_equal)
                    last = dve.tensor_copy(gsel[:, t:t + 1], gateb[:, t, bass.ds(b, 1)])
                last.then_inc(m_sel, 1)

            def tokens_lo(done):
                for q in range(2):
                    dve.wait_ge(m_xhi, done + (q + 1))
                    dve.tensor_tensor(xg_lo[:, 4 * q:4 * q + 4, :], ps[:, 6 + q, :].rearrange("p (c s) -> p c s", c=4),
                                      xg_hi[:, 4 * q:4 * q + 4, :].bitcast(F32), ALU.subtract).then_inc(m_xlo, 1)

            dve.wait_ge(h_ready, H_AT[4][1])
            norm_hn(4)
            splits(P_MOE + 2)
            norm_lo(4)
            dve.wait_ge(gffn_in, 16)
            for t in range(NT):
                dve.tensor_tensor(hn[:, t, :], hn[:, t, :], gffn, ALU.mult).then_inc(m_hn, 1)
            for t in range(NT):
                dve.wait_ge(m_hhi, t + 1)
                dve.tensor_tensor(hn_lo[:, t, :], hn[:, t, :], hn_hi[:, t, :].bitcast(F32), ALU.subtract).then_inc(m_hlo, 1)
            dve.wait_ge(lg_ps, 1)
            link(dve.tensor_copy(r_l, ps[:, 4, 0:NT * NE].rearrange("p (t e) -> p t e", t=NT)))
            link(dve.tensor_reduce(r_mx, r_l, AX, ALU.max))
            dve.tensor_scalar(r_nmx, r_mx, -1.0, None, ALU.mult).then_inc(lg_max, 1)
            for t in range(NT):
                other, own = over(r_l[:, t, :], NE), along(r_l[:, t, :], NE)
                dve.tensor_tensor(r_gt[:, t, :].rearrange("p (e f) -> p e f", e=NE), other, own, ALU.is_gt)
                last = dve.tensor_tensor(r_eq[:, t, :].rearrange("p (e f) -> p e f", e=NE), other, own, ALU.is_equal)
            link(last)
            link(dve.tensor_tensor(r_eq, r_eq, over(con[:, C_LOW:C_LOW + NE * NE], NT), ALU.mult))
            link(dve.tensor_tensor(r_gt, r_gt, r_eq, ALU.add))
            link(dve.tensor_reduce(r_rank, r_gt.rearrange("p t (e f) -> p t e f", e=NE), AX, ALU.add))
            dve.tensor_scalar(r_m, r_rank, 1.5, None, ALU.is_lt).then_inc(mk_rdy, 1)
            dve.wait_ge(mk_rdy, 1)
            dve.wait_ge(lg_exp, 1)
            link(dve.tensor_tensor(r_e, r_e, r_m, ALU.mult))
            link(dve.tensor_reduce(r_s, r_e, AX, ALU.add))
            link(dve.reciprocal(r_rs, r_s))
            dve.memset(posb[:, :, :], -1.0)
            dve.memset(gateb[:, :, :], 0.0)
            link(dve.memset(blk_f, 0.0))
            link(dve.tensor_tensor(gateb[:, :, 0:NE], r_e, along(r_rs, NE), ALU.mult))
            dve.wait_ge(rk_ps, 1)
            dve.tensor_scalar(r_ov, ps[:, 5, 2 * NE:3 * NE], float(P) + 0.5, None, ALU.is_gt)
            link(dve.tensor_tensor(r_im, ps[:, 5, 0:NT * NE].rearrange("p (t e) -> p t e", t=NT), r_m, ALU.mult))
            link(dve.tensor_scalar(posb[:, :, 0:NE], r_im, -1.0, None, ALU.add))
            select(0)
            w3 = r_w.rearrange("p (e f) -> p e f", e=NE)
            link(dve.tensor_tensor(w3, con[:, C_LOW:C_LOW + NE * NE].rearrange("p (e f) -> p e f", e=NE),
                                   over(r_ov, NE), ALU.mult))
            link(dve.tensor_reduce(r_ord, w3, AX, ALU.add))
            for i in range(MAX_OVER):
                last = dve.tensor_scalar(r_sl[:, i, :], r_ord, float(i), None, ALU.is_equal)
            link(last)
            link(dve.tensor_tensor(r_sl, r_sl, over(r_ov, MAX_OVER), ALU.mult))
            for t in range(NT):
                last = dve.tensor_tensor(r_t[:, t], r_sl, over(r_im[:, t, :], MAX_OVER), ALU.mult)
            link(last)
            link(dve.tensor_reduce(posb[:, :, NE:NE + MAX_OVER], r_t, AX, ALU.add))
            link(dve.tensor_scalar(posb[:, :, NE:NE + MAX_OVER], posb[:, :, NE:NE + MAX_OVER], -1.0 - P, None, ALU.add))
            for t in range(NT):
                last = dve.tensor_tensor(r_t[:, t], r_sl, over(gateb[:, t, 0:NE], MAX_OVER), ALU.mult)
            link(last)
            link(dve.tensor_reduce(gateb[:, :, NE:NE + MAX_OVER], r_t, AX, ALU.add))
            tokens_lo(0)
            link(dve.tensor_tensor(r_sl, r_sl, over(con[:, C_EID:C_EID + NE], MAX_OVER), ALU.mult))
            dve.tensor_reduce(blk_f[:, NE:NE + MAX_OVER], r_sl, AX, ALU.add)
            dve.tensor_copy(blk_f[:, 0:NE], con[:, C_EID:C_EID + NE])
            link(dve.tensor_reduce(blk_f[:, 15:16], r_ov, AX, ALU.add))
            link(dve.tensor_scalar(blk_f[:, 15:16], blk_f[:, 15:16], float(NE), None, ALU.add))
            dve.tensor_copy(blk_i[:, :], blk_f).then_inc(tab_rdy, 1)
            dve.wait_ge(tab_rdy, 1)
            nblk = dve.value_load(blk_i[0:1, 15:16], min_val=NE, max_val=NE + MAX_OVER)

            def adds(b):
                for half in range(2):
                    for t in range(NT):
                        dve.wait_ge(m_sc, b * 4 + (2 * half + t + 1))
                        add_h(t, half, ps[:, 2 + 4 * t + half, :]).then_inc(m_add, 1)

            with dve.Fori(0, nblk) as b:
                at = [SPLIT]

                def pieces(upto):
                    while at[0] <= upto:
                        split(at[0], b * PER_BLOCK + (P_MOE + at[0] + 1))
                        at[0] += 1

                pieces(3)
                adds(b)
                for j in range(FJ):
                    i = MOE_AT[1, j, 1]
                    pieces(i + 2)
                    dve.wait_ge(piece_used, b * PER_BLOCK + (P_MOE + i + 1))
                    dve.wait_ge(m_silu, b * FJ + (j + 1))
                    dve.tensor_tensor(gated[:, j % 2, :], sil[:, j % 2, :], ps[:, 2 * (j % 2) + 1, :],
                                      ALU.mult).then_inc(m_gated, 1)
                    if j == 0:
                        dve.wait_ge(m_sT_ps, b + 1)
                        select(b + 1)
                    if j + 1 < FJ:
                        pieces(MOE_AT[0, j + 1, 1] + 2)
                    else:
                        pieces(MOE_AT[2, j - 1, 1] + 2)
                    dve.wait_ge(m_ghi, b * FJ + (j + 1))
                    dve.tensor_tensor(g_lo[:, j % 2, :], ps[:, 2 * (j % 2), :], g_hi[:, j % 2, :].bitcast(F32),
                                      ALU.subtract).then_inc(m_glo, 1)
                tokens_lo(b * 2 + 2)
                pieces(PER_BLOCK + 1)
                for half in range(2):
                    cut = slice(half * 512, (half + 1) * 512)
                    dve.wait_ge(m_yhi, b * 2 + (half + 1))
                    dve.scalar_tensor_tensor(y_lo[:, cut], ps[:, 4 + half, :], gslot[:, 0:1], y_hi[:, cut].bitcast(F32),
                                             ALU.mult, ALU.subtract).then_inc(m_ysb, 1)
                pieces(PER_BLOCK + 2)

            p_second(1)
            adds(nblk)
            dve.wait_ge(m_add, nblk * 4 + H_MOE[1])
            norm_hn(5)
            tail = [SPLIT]

            def tail_pieces(upto):
                while tail[0] <= min(upto, 5):
                    split(tail[0], nblk * PER_BLOCK + (P_MOE + tail[0] + 1), D if tail[0] < 2 else PIECE)
                    tail[0] += 1

            embed(1, tail_pieces, lambda i: dve.wait_ge(piece_used, nblk * PER_BLOCK + (P_MOE + i)))

            dve.wait_ge(gfin_in, 16)
            for t in range(NT):
                dve.wait_ge(n_std, 6 * NT + t + 1)
                link(dve.reciprocal(rstd[:, 6, t:t + 1], std[:, 6, t:t + 1]))
                dve.scalar_tensor_tensor(hn[:, t, :], h[:, t, :], rstd[:, 6, t:t + 1], gfin, ALU.mult, ALU.mult).then_inc(f_out, 1)


_INS = ["x", "p", "positions", "ln_mix", "ln_ffn", "ln_ple", "ln_final", "w_in_even", "w_out_even",
        "lam_q1", "lam_k1", "lam_q2", "lam_k2", "subln_gain", "conv_w_short", "w_in_odd", "conv_w_qkv",
        "a_log", "dt_bias", "onorm_gain", "w_out_odd", "w1_dense", "w3_dense", "w2_dense",
        "w_router", "w1_moe", "w3_moe", "w2_moe", "w_ple_gate", "w_ple_proj"]


def kernel(**inputs):
    import concourse.bacc as bacc
    from concourse.bass_utils import run_bass_kernel_spmd

    nc = bacc.Bacc("TRN2", target_bir_lowering=False, num_devices=1)
    arrays, aps = {}, {}
    for name in _INS + ["con"]:
        v = shape_constants() if name == "con" else np.ascontiguousarray(inputs[name])
        arrays[f"in_{name}"] = v
        aps[name] = nc.dram_tensor(f"in_{name}", v.shape, mybir.dt.from_np(v.dtype), kind="ExternalInput").ap()
    out = nc.dram_tensor("out", (1, SEQ, D), F32, kind="ExternalOutput").ap()
    trunk(nc, aps, out)
    r = run_bass_kernel_spmd(nc, [arrays], core_ids=[0])
    return r.results[0]["out"]
```
